# Optimizing a Trainium2 kernel written in Bass

```python
import math
import jax, jax.numpy as jnp
from jax import lax
import numpy as np

D_MODEL = 1024
BATCH = 1
SEQ = 512
DEPTH = 1

MEM_LEN = 256
HEAD_DIM = 64
EPS = 1e-6
A_HEADS = 6
A_PATTERNS = ((128, 1), (512, 4), (2048, 16))
N_BUCKETS = 32
REL_MAX_DIST = 2048
B_HEADS = 4
B_KEY_DIM = 64
B_VAL_DIM = 96
B_CHUNK = 64
C_HEADS = 4
N_EXPERTS = 64
TOP_K = 8
N_GROUPS = 8
TOPK_GROUPS = 4
EXPERT_HIDDEN = 256
SHARED_HIDDEN = 256
ROUTED_SCALE = 2.5
MOE_BLOCK = 128

A_WIDTH = A_HEADS * HEAD_DIM
B_QK_WIDTH = B_HEADS * B_KEY_DIM
B_WIDTH = B_HEADS * B_VAL_DIM
C_WIDTH = C_HEADS * HEAD_DIM
N_BRANCHES = 3
IN_SPLITS = (A_WIDTH, A_WIDTH, A_WIDTH, B_QK_WIDTH, B_QK_WIDTH, B_WIDTH, B_WIDTH, C_WIDTH, N_BRANCHES * D_MODEL)
IN_WIDTH = sum(IN_SPLITS)

kernel_name = 'hybrid_dilated_hgrn2_memxattn_moe_block'

def split_cols(t, sizes):
    out, start = [], 0
    for s in sizes:
        out.append(t[..., start:start + s])
        start += s
    return out

def rmsnorm(t, g):
    tf = t.astype(jnp.float32)
    tf = tf * lax.rsqrt(jnp.mean(tf * tf, axis=-1, keepdims=True) + EPS)
    return (tf * g.astype(jnp.float32)).astype(t.dtype)

def t5_bucket(dist):
    d = dist.astype(jnp.int32)
    max_exact = N_BUCKETS // 2
    large = max_exact + (jnp.log(jnp.maximum(d, 1).astype(jnp.float32) / max_exact)
                         / math.log(REL_MAX_DIST / max_exact) * (N_BUCKETS - max_exact)).astype(jnp.int32)
    return jnp.where(d < max_exact, d, jnp.minimum(large, N_BUCKETS - 1))

def dilated_window_attention(q, k, v, rel_bias, window, dilation):
    B, S, H, E = q.shape
    w = window // dilation
    L = S // dilation
    nb = -(-L // w)
    Lp = nb * w

    def to_residue(t):
        t = t.reshape(B, L, dilation, H, E).transpose(0, 2, 3, 1, 4)
        return jnp.pad(t, ((0, 0), (0, 0), (0, 0), (0, Lp - L), (0, 0)))

    qs, ks, vs = to_residue(q), to_residue(k), to_residue(v)
    qb = qs.reshape(B, dilation, H, nb, w, E)

    def with_prev(t):
        tp = jnp.pad(t, ((0, 0), (0, 0), (0, 0), (w, 0), (0, 0)))
        return jnp.concatenate([tp[:, :, :, :Lp].reshape(B, dilation, H, nb, w, E),
                                t.reshape(B, dilation, H, nb, w, E)], axis=4)

    kb, vb = with_prev(ks), with_prev(vs)
    i = jnp.arange(w)[:, None]
    c = jnp.arange(2 * w)[None, :]
    steps = w + i - c
    in_band = (steps >= 0) & (steps <= w)
    blk = jnp.arange(nb)[:, None, None]
    valid = in_band[None] & ((blk > 0) | (c[None] >= w))
    bias = rel_bias.astype(jnp.float32)[t5_bucket(jnp.clip(steps, 0, w) * dilation)]
    bias = bias.transpose(2, 0, 1)
    logits = jnp.einsum('brhnie,brhnce->brhnic', qb, kb) + bias[None, None, :, None]
    logits = jnp.where(valid[None, None, None], logits, -jnp.inf)
    m = jnp.max(logits, axis=-1, keepdims=True)
    p = jnp.exp(logits - m)
    den = jnp.sum(p, axis=-1, keepdims=True)
    o = jnp.einsum('brhnic,brhnce->brhnie', p, vb) / den
    lse = (m + jnp.log(den))[..., 0]
    o = o.reshape(B, dilation, H, Lp, E)[:, :, :, :L].transpose(0, 3, 1, 2, 4).reshape(B, S, H, E)
    lse = lse.reshape(B, dilation, H, Lp)[:, :, :, :L].transpose(0, 3, 1, 2).reshape(B, S, H)
    return o, lse

def dilated_attention_branch(qa, ka, va, q_norm, k_norm, rel_bias):
    B, S, _ = qa.shape
    q = rmsnorm(qa.reshape(B, S, A_HEADS, HEAD_DIM), q_norm).astype(jnp.float32) * HEAD_DIM ** -0.5
    k = rmsnorm(ka.reshape(B, S, A_HEADS, HEAD_DIM), k_norm).astype(jnp.float32)
    v = va.reshape(B, S, A_HEADS, HEAD_DIM).astype(jnp.float32)
    outs, lses = [], []
    for window, dilation in A_PATTERNS:
        o, lse = dilated_window_attention(q, k, v, rel_bias, window, dilation)
        outs.append(o)
        lses.append(lse)
    wts = jax.nn.softmax(jnp.stack(lses, axis=0), axis=0)
    o = jnp.sum(jnp.stack(outs, axis=0) * wts[..., None], axis=0)
    return o.reshape(B, S, A_WIDTH).astype(qa.dtype)

def chunked_gated_recurrence(q, k, log_f, v):
    B, S, H, DK = q.shape
    DV = v.shape[-1]
    nc = S // B_CHUNK

    def chunks(t):
        return t.reshape(B, nc, B_CHUNK, H, t.shape[-1]).transpose(1, 0, 3, 2, 4)

    causal = jnp.tril(jnp.ones((B_CHUNK, B_CHUNK), bool))[:, :, None]

    def step(state, inp):
        qt, kt, gt, vt = inp
        b = jnp.cumsum(gt, axis=2)
        diff = jnp.where(causal, b[:, :, :, None, :] - b[:, :, None, :, :], -jnp.inf)
        scores = jnp.einsum('bhtk,bhsk,bhtsk->bhts', qt, kt, jnp.exp(diff))
        o = (jnp.einsum('bhts,bhsv->bhtv', scores, vt)
             + jnp.einsum('bhtk,bhkv->bhtv', qt * jnp.exp(b), state))
        b_last = b[:, :, -1:, :]
        state = (jnp.exp(b_last[:, :, 0, :])[..., None] * state
                 + jnp.einsum('bhsk,bhsv->bhkv', kt * jnp.exp(b_last - b), vt))
        return state, o

    state0 = jnp.zeros((B, H, DK, DV), jnp.float32)
    _, o = lax.scan(step, state0, (chunks(q), chunks(k), chunks(log_f), chunks(v)))
    return o.transpose(1, 0, 3, 2, 4).reshape(B, S, H, DV)

def hgrn2_branch(qb, fb, ib, og, lower_bound, out_norm):
    B, S, _ = qb.shape
    q = jax.nn.silu(qb.astype(jnp.float32)).reshape(B, S, B_HEADS, B_KEY_DIM) * B_KEY_DIM ** -0.5
    f = lower_bound + (1.0 - lower_bound) * jax.nn.sigmoid(fb.astype(jnp.float32))
    f = f.reshape(B, S, B_HEADS, B_KEY_DIM)
    k = 1.0 - f
    v = ib.astype(jnp.float32).reshape(B, S, B_HEADS, B_VAL_DIM)
    o = chunked_gated_recurrence(q, k, jnp.log(f), v)
    o = rmsnorm(o, out_norm.reshape(B_HEADS, B_VAL_DIM))
    o = o * jax.nn.silu(og.astype(jnp.float32)).reshape(B, S, B_HEADS, B_VAL_DIM)
    return o.reshape(B, S, B_WIDTH).astype(qb.dtype)

def memory_branch(qc, mem_n, w_mem_kv, q_norm, k_norm):
    B, S, _ = qc.shape
    M = mem_n.shape[1]
    km, vm = split_cols(mem_n @ w_mem_kv, (C_WIDTH, C_WIDTH))
    k = rmsnorm(km.reshape(B, M, C_HEADS, HEAD_DIM), k_norm).astype(jnp.float32)
    v = vm.reshape(B, M, C_HEADS, HEAD_DIM).astype(jnp.float32)
    q = rmsnorm(qc.reshape(B, S, C_HEADS, HEAD_DIM), q_norm).astype(jnp.float32) * HEAD_DIM ** -0.5
    p = jax.nn.softmax(jnp.einsum('bshe,bmhe->bhsm', q, k), axis=-1)
    o = jnp.einsum('bhsm,bmhe->bshe', p, v)
    return o.reshape(B, S, C_WIDTH).astype(qc.dtype)

def swiglu(t, w_up, w_down):
    gate, up = split_cols(t @ w_up, (w_down.shape[0], w_down.shape[0]))
    return (jax.nn.silu(gate) * up) @ w_down

def routed_experts(u, idx, wts, w_exp_up, w_exp_down):
    T, D = u.shape
    TK = T * TOP_K
    flat_e = idx.reshape(-1).astype(jnp.int32)
    order = jnp.argsort(flat_e).astype(jnp.int32)
    e_sorted = flat_e[order]
    counts = jnp.bincount(flat_e, length=N_EXPERTS).astype(jnp.int32)
    padded = (counts + MOE_BLOCK - 1) // MOE_BLOCK * MOE_BLOCK
    start = jnp.cumsum(counts) - counts
    pend = jnp.cumsum(padded)
    pstart = pend - padded
    dest = pstart[e_sorted] + jnp.arange(TK, dtype=jnp.int32) - start[e_sorted]
    n_blocks = -(-TK // MOE_BLOCK) + N_EXPERTS
    slot_of_row = jnp.full((n_blocks * MOE_BLOCK,), TK, jnp.int32).at[dest].set(order)
    block_expert = jnp.minimum(jnp.searchsorted(pend, jnp.arange(n_blocks, dtype=jnp.int32) * MOE_BLOCK,
                                                side='right'), N_EXPERTS - 1)
    tok_of_slot = jnp.concatenate([jnp.arange(TK, dtype=jnp.int32) // TOP_K, jnp.full((1,), T, jnp.int32)])
    w_of_slot = jnp.concatenate([wts.reshape(-1).astype(jnp.float32), jnp.zeros((1,), jnp.float32)])
    u_pad = jnp.concatenate([u, jnp.zeros((1, D), u.dtype)], axis=0)

    def step(acc, blk):
        slots = lax.dynamic_slice_in_dim(slot_of_row, blk * MOE_BLOCK, MOE_BLOCK)
        tok = tok_of_slot[slots]
        e = block_expert[blk]
        y = swiglu(u_pad[tok], w_exp_up[e], w_exp_down[e])
        return acc.at[tok].add(y.astype(jnp.float32) * w_of_slot[slots][:, None]), None

    acc, _ = lax.scan(step, jnp.zeros((T + 1, D), jnp.float32), jnp.arange(n_blocks, dtype=jnp.int32))
    return acc[:T]

def moe_ffn(u, w_router, router_bias, w_exp_up, w_exp_down, w_shared_up, w_shared_down):
    T = u.shape[0]
    per_group = N_EXPERTS // N_GROUPS
    s = jax.nn.sigmoid(u.astype(jnp.float32) @ w_router.astype(jnp.float32))
    choice = s + router_bias.astype(jnp.float32)
    group_score = jnp.sum(lax.top_k(choice.reshape(T, N_GROUPS, per_group), 2)[0], axis=-1)
    _, top_groups = lax.top_k(group_score, TOPK_GROUPS)
    group_mask = jnp.sum(jax.nn.one_hot(top_groups, N_GROUPS, dtype=jnp.float32), axis=1) > 0
    expert_mask = jnp.repeat(group_mask, per_group, axis=1)
    _, idx = lax.top_k(jnp.where(expert_mask, choice, -jnp.inf), TOP_K)
    w = jnp.take_along_axis(s, idx, axis=1)
    w = ROUTED_SCALE * w / jnp.sum(w, axis=-1, keepdims=True)
    routed = routed_experts(u, idx, w, w_exp_up, w_exp_down)
    shared = swiglu(u, w_shared_up, w_shared_down).astype(jnp.float32)
    return (routed + shared).astype(u.dtype)

def setup_inputs(seed: int = 0) -> dict:
    key = jax.random.key(seed)
    ks = jax.random.split(key, 24)
    f32 = jnp.float32

    def nrm(k, shape, scale):
        return jax.random.normal(k, shape, f32) * scale

    def gain(k, shape):
        return 1.0 + 0.02 * jax.random.normal(k, shape, f32)

    L = DEPTH
    return {
        'x': nrm(ks[0], (BATCH, SEQ, D_MODEL), 1.0),
        'mem': nrm(ks[1], (BATCH, MEM_LEN, D_MODEL), 1.0),
        'attn_norm_g': gain(ks[2], (L, D_MODEL)),
        'w_in': nrm(ks[3], (L, D_MODEL, IN_WIDTH), D_MODEL ** -0.5),
        'q_norm_a': gain(ks[4], (L, HEAD_DIM)),
        'k_norm_a': gain(ks[5], (L, HEAD_DIM)),
        'rel_bias': nrm(ks[6], (N_BUCKETS, A_HEADS), 0.1),
        'lb_logits': nrm(ks[7], (DEPTH + 1, B_QK_WIDTH), 0.5),
        'out_norm_b': gain(ks[8], (L, B_WIDTH)),
        'mem_norm_g': gain(ks[9], (L, D_MODEL)),
        'w_mem_kv': nrm(ks[10], (L, D_MODEL, 2 * C_WIDTH), D_MODEL ** -0.5),
        'q_norm_c': gain(ks[11], (L, HEAD_DIM)),
        'k_norm_c': gain(ks[12], (L, HEAD_DIM)),
        'w_branch_a': nrm(ks[13], (L, A_WIDTH, D_MODEL), A_WIDTH ** -0.5),
        'w_branch_b': nrm(ks[14], (L, B_WIDTH, D_MODEL), B_WIDTH ** -0.5),
        'w_branch_c': nrm(ks[15], (L, C_WIDTH, D_MODEL), C_WIDTH ** -0.5),
        'w_out': nrm(ks[16], (L, D_MODEL, D_MODEL), D_MODEL ** -0.5),
        'ffn_norm_g': gain(ks[17], (L, D_MODEL)),
        'w_router': nrm(ks[18], (L, D_MODEL, N_EXPERTS), D_MODEL ** -0.5),
        'router_bias': nrm(ks[19], (L, N_EXPERTS), 0.01),
        'w_exp_up': nrm(ks[20], (L, N_EXPERTS, D_MODEL, 2 * EXPERT_HIDDEN), D_MODEL ** -0.5),
        'w_exp_down': nrm(ks[21], (L, N_EXPERTS, EXPERT_HIDDEN, D_MODEL), EXPERT_HIDDEN ** -0.5),
        'w_shared_up': nrm(ks[22], (L, D_MODEL, 2 * SHARED_HIDDEN), D_MODEL ** -0.5),
        'w_shared_down': nrm(ks[23], (L, SHARED_HIDDEN, D_MODEL), SHARED_HIDDEN ** -0.5),
    }

def reference(x, mem, attn_norm_g, w_in, q_norm_a, k_norm_a, rel_bias, lb_logits, out_norm_b,
              mem_norm_g, w_mem_kv, q_norm_c, k_norm_c, w_branch_a, w_branch_b, w_branch_c, w_out,
              ffn_norm_g, w_router, router_bias, w_exp_up, w_exp_down, w_shared_up, w_shared_down):
    B, S, D = x.shape
    lower_bounds = jnp.cumsum(jax.nn.softmax(lb_logits.astype(jnp.float32), axis=0), axis=0)
    for layer in range(DEPTH):
        h = rmsnorm(x, attn_norm_g[layer])
        qa, ka, va, qb, fb, ib, og, qc, gate_pre = split_cols(h @ w_in[layer], IN_SPLITS)
        ya = dilated_attention_branch(qa, ka, va, q_norm_a[layer], k_norm_a[layer], rel_bias)
        yb = hgrn2_branch(qb, fb, ib, og, lower_bounds[layer], out_norm_b[layer])
        yc = memory_branch(qc, rmsnorm(mem, mem_norm_g[layer]), w_mem_kv[layer], q_norm_c[layer], k_norm_c[layer])
        g_a, g_b, g_c = split_cols(jax.nn.sigmoid(gate_pre), (D, D, D))
        mixed = (g_a * (ya @ w_branch_a[layer]) + g_b * (yb @ w_branch_b[layer])
                 + g_c * (yc @ w_branch_c[layer]))
        x = x + mixed @ w_out[layer]
        u = rmsnorm(x, ffn_norm_g[layer]).reshape(B * S, D)
        y = moe_ffn(u, w_router[layer], router_bias[layer], w_exp_up[layer], w_exp_down[layer],
                    w_shared_up[layer], w_shared_down[layer])
        x = x + y.reshape(B, S, D)
    return x


_drawn_inputs = setup_inputs


def setup_inputs(seed=0):
    import zlib

    import numpy as np

    out = dict(_drawn_inputs(seed))
    spreads = {}
    factors = {'q_norm_a': 3.409, 'mem_norm_g': 2.954, 'q_norm_c': 3.559}
    for name, (base, spread) in spreads.items():
        noise = np.random.default_rng([zlib.crc32(name.encode()), seed]).standard_normal(out[name].shape)
        drawn = base * np.exp(spread * noise) if base else spread * noise
        out[name] = __import__('jax').numpy.asarray(drawn.astype(out[name].dtype))
    for name, factor in factors.items():
        out[name] = (out[name] * factor).astype(out[name].dtype)
    return out
```

```python
from contextlib import ExitStack

import numpy as np

import concourse.bass as bass
from concourse import mybir

F32 = mybir.dt.float32
I32 = mybir.dt.int32
U32 = mybir.dt.uint32
ALU = mybir.AluOpType
ACT = mybir.ActivationFunctionType
AX = mybir.AxisListType

P = 128
D, T, M = 1024, 512, 256
KD, NT, NM = D // P, T // P, M // P
HD = 64
AW, BK, BV, CW = 6 * HD, 4 * HD, 4 * 96, 4 * HD
VD = 96
EPS = 1e-6
LEVELS = 7
E, FH = 64, 256
GROUPS, TOP_GROUPS, TOP_K = 8, 4, 8
ROUTED_SCALE = 2.5
MASKED = -1e30
SPAN = T + P
QA, KA, VA, QB, IB, OG, QC, GATES = 0, 384, 768, 1152, 1664, 2048, 2432, 2688
A_PAIRS, C_PAIRS = 3, 2
UNITS = 2 * NT
SLOTS = 4
PASSES = T // P
NO_TOKEN = 4096.0


def shape_constants():
    i = np.arange(P)
    r, c = i[:, None], i[None, :]
    level = np.where(c >= r, np.bitwise_xor(r, c), 1000)
    square = np.stack([r == c, r + c == P - 1, np.broadcast_to(c, (P, P)), r < c, np.ones((P, P)), level], 1)
    d = T - 1 - np.arange(SPAN)
    times = ((d >= 0) & (d <= 128)).astype(int) + ((d >= 0) & (d % 4 == 0)) + ((d >= 0) & (d % 16 == 0))
    far = 16 + (np.log(np.maximum(d, 1).astype(np.float32) / np.float32(16)) / np.float32(np.log(128.0))
                * np.float32(16)).astype(np.int32)
    bucket = np.where(d < 16, d, np.minimum(far, 31))
    hot = (bucket[None, :] == np.arange(32)[:, None]) & (times > 0)[None, :]
    last = np.where(times > 0, np.log(np.maximum(times, 1)), MASKED)
    tokens = np.stack([i + P * t - NO_TOKEN for t in range(NT)], 1)
    return {
        "square": np.ascontiguousarray(square, dtype=np.float32),
        "bucket": np.concatenate([hot, last[None, :]], 0).astype(np.float32),
        "tokens": np.ascontiguousarray(tokens, dtype=np.float32),
    }


def view(a, *shape):
    names = "abcd"[:len(shape)]
    return a if len(shape) == 1 else a.rearrange(
        f"p ({' '.join(names)}) -> p {' '.join(names)}", **dict(zip(names[1:], shape[1:])))


def bcast(a, *shape):
    return a.broadcast_to(list(shape))


def build(nc, io, out, const, u_dram, table_dram, debug=None):
    ctx = ExitStack()
    with ctx:
        def sem(name):
            return ctx.enter_context(nc.semaphore(name))

        words = 53200
        arena = ctx.enter_context(nc.sbuf_tensor("arena", [P, words], F32))
        top = [0]

        def at(offset, *shape):
            return view(arena[:, offset:offset + int(np.prod(shape))], *shape)

        def take(*shape):
            offset = top[0]
            top[0] += int(np.prod(shape))
            assert top[0] <= words, top[0]
            return offset

        square = at(take(6, P), 6, P)
        ident, flip, counting, before, ones, level = (square[:, n, :] for n in range(6))
        gains = at(take(32), 32)
        lb = at(take(8), 8)
        small = at(take(320), 320)
        x_tok = at(take(NT, D), NT, D)
        hT_at = take(KD, T)
        hT = at(hT_at, KD, T)
        bias_at = take(6, T)
        bias = at(bias_at, 6, T)
        ring_at = take(3, KD, T)
        ring = at(ring_at, 3, KD, T)
        gates_at = take(3 * KD, T)
        gates = at(gates_at, 3 * KD, T)
        qa_at, ka_at, va_at = take(NT, AW), take(NT, AW), take(NT, AW)
        qa, ka, va = (at(o, NT, AW) for o in (qa_at, ka_at, va_at))
        kv = at(take(NM, 2 * CW), NM, 2 * CW)
        ib_at, og_at = take(NT, BV), take(NT, BV)
        ib, og = at(ib_at, NT, BV), at(og_at, NT, BV)
        qc = at(take(NT, CW), NT, CW)
        staging_at = take(2, NT, P)
        staging = at(staging_at, 2, NT, P)
        qkT_at = take(2, T)
        qkT = at(qkT_at, 2, T)
        logits_at = take(2, T)
        logits, probs, probsT = at(logits_at, 2, T), at(take(2, T), 2, T), at(take(2, T), 2, T)
        w_router = at(take(KD, E), KD, E)
        out_norm = at(take(BV), BV)

        xn = at(qa_at, NT, D)
        squares = at(ib_at, 2, NT, AW)
        hankel = at(logits_at, 6, T)
        bucket = at(staging_at, SPAN)
        table = at(qkT_at, SPAN)
        scores = at(logits_at, 16, P)
        kdT = at(logits_at + 2048, 2, 3 * P)
        mask = at(staging_at, 2, P)
        state = at(staging_at + 256, NT - 1, 2, 2 * VD)
        mem = at(gates_at, NM, D)
        memT = at(gates_at + 2048, KD, M)
        rec = gates_at + 4096
        fT, qT, kT, bT = (at(rec + n * 1024, 2, T) for n in range(4))
        expo = [at(rec + (4 + n) * 1024, 2, T) for n in range(2)]
        kq = [at(rec + (6 + n) * 1024, 2, T) for n in range(2)]
        o_tok = at(rec, NT, BV)
        o_sq = at(rec + 2048, NT, BV)
        o_gate = at(rec + 4096, NT, BV)
        c_sq = at(rec + 6144, 2048)
        w_a = at(ring_at + 2 * KD * T, 3, D)
        w_b, w_c = at(hT_at, 3, D), at(hT_at + 3 * D, 2, D)
        ffn_gain = at(hT_at + 5 * D, D)
        w_out = at(ring_at, KD, D)
        yT = at(ka_at, KD, T)
        uT = at(hT_at, KD, T)
        u_tok = at(gates_at + 4096, NT, D)
        w_sup = at(gates_at + 8192, KD, 2 * FH)
        w_sdn = at(ka_at, 2, D)
        s_hid = at(ka_at + 2048, 2, FH)
        s_hidT = at(ka_at + 2560, 2, 2, P)
        s_tanh = at(ka_at + 3072, 2, FH)
        ro = [at(ib_at + n * 256, NT, E) for n in range(16)]
        (score, choice, masked, masked2, picked, weight, place) = ro[0:7]
        route_in = at(ib_at + 7 * 256, NT, E, 2)
        router_bias = at(ib_at + 9 * 256, E)
        rs = at(ib_at + 10 * 256, 1024)
        w_up = [at(ring_at + s * 6144, KD, 2 * FH) for s in range(SLOTS)]
        w_dn = [at(ring_at + s * 6144 + 4096, 2, D) for s in range(SLOTS)]
        gathered = at(staging_at, 2, D)
        y_out = at(logits_at, 2, D)
        select = at(logits_at + 2048, 2, NT, P)
        gatheredT = at(bias_at, 2, KD, P)
        hid = at(bias_at + 2048, 2, FH)
        hidT = at(bias_at + 2560, 2, 2, P)
        e_tanh = at(qa_at, 2, FH)
        e_act = at(qa_at + 512, 2, FH)
        index = small[:, 300:304].bitcast(U32)
        slot_w = small[:, 304:308]
        most = small[:, 308:309]
        most_i = small[:, 309:310].bitcast(I32)

        rel = small[:, 312:318]
        ps = [ctx.enter_context(nc.psum_tensor(f"bank{n}", [P, 512], F32)) for n in range(8)]

        c_in = [sem(f"const_in{n}") for n in range(12)]
        x_in = [sem(f"x_in{t}") for t in range(NT)]
        mem_in = sem("mem_in")
        ring_in = [sem(f"ring_in{s}") for s in range(3)]
        table_out, hankel_in = sem("table_out"), sem("hankel_in")
        w_used = sem("w_used")
        x_squared, x_rooted, x_normed, mem_normed = map(sem, ("x_squared", "x_rooted", "x_normed", "mem_normed"))
        unit_done, unit_out = sem("unit_done"), sem("unit_out")
        v_step, a_step = sem("v_step"), sem("a_step")
        lb_in_exp, lb_exp = sem("lb_in_exp"), sem("lb_exp")
        f_exp, f_ready, q_tanh, log_ready = map(sem, ("f_exp", "f_ready", "q_tanh", "log_ready"))
        diff_ready, expo_ready, kq_ready = map(sem, ("diff_ready", "expo_ready", "kq_ready"))
        level_done, level_taken = sem("level_done"), sem("level_taken")
        inc_done, state_ready = sem("inc_done"), sem("state_ready")
        qk_squared, qk_summed, qk_rooted = sem("qk_squared"), sem("qk_summed"), sem("qk_rooted")
        o_summed, o_rooted, og_tanh, c_summed, c_rooted = map(sem, ("o_summed", "o_rooted", "og_tanh", "c_summed", "c_rooted"))
        staged, pair_done, pair_out = map(sem, ("staged", "pair_done", "pair_out"))
        qk_done, max_ready, exp_done, pT_done, pT_out, pv_done, y_done = map(
            sem, ("qk_done", "max_ready", "exp_done", "pT_done", "pT_out", "pv_done", "y_done"))
        gate_done, gate_tanh, gate_out = map(sem, ("gate_done", "gate_tanh", "gate_out"))
        branch_in = [sem(f"branch_in{n}") for n in range(4)]
        yT_done, yT_out, mix_done, mix_taken, mixed = map(sem, ("yT_done", "yT_out", "mix_done", "mix_taken", "mixed"))
        x1_done, x1_ready, x1_squared, x1_rooted, u_ready = map(sem, ("x1_done", "x1_ready", "x1_squared", "x1_rooted", "u_ready"))
        u_stored, uT_done, uT_out = map(sem, ("u_stored", "uT_done", "uT_out"))
        shared_in = [sem("shared_up_in"), sem("shared_down_in")]
        r_done, r_tanh, picked_ready, place_done, routed = map(sem, ("r_done", "r_tanh", "picked_ready", "place_done", "routed"))
        s_up, s_tanhed, s_hidden, s_hidT_done, s_hidT_out, s_down, out_ready, out_stored = map(
            sem, ("s_up", "s_tanhed", "s_hidden", "s_hidT_done", "s_hidT_out", "s_down", "out_ready", "out_stored"))
        up_in = [sem(f"up_in{s}") for s in range(SLOTS)]
        dn_in = [sem(f"dn_in{s}") for s in range(SLOTS)]
        sel_ready, route_done, index_ready = map(sem, ("sel_ready", "route_done", "index_ready"))
        gather_in = [sem(f"gather_in{n}") for n in range(2)]
        gT_done, gT_out_a, gT_out_v = map(sem, ("gT_done", "gT_out_a", "gT_out_v"))
        up_done, tanh_done, hid_ready, hidT_done, hidT_out = map(sem, ("up_done", "tanh_done", "hid_ready", "hidT_done", "hidT_out"))
        down_done, y_out_a, y_out_v, added, cleared = map(sem, ("down_done", "y_out_a", "y_out_v", "added", "cleared"))

        groups = [(QB, 512), (QA, 384), (KA, 384), (VA, 384), (IB, 384), (OG, 384), (None, 512), (QC, 256)]
        plan = [("hT", k) for k in range(KD)] + [("table", 0), ("table", 1)]
        plan += [("qf", b) for b in (2, 3, 0, 1)]
        plan += [("qa", t) for t in range(NT)] + [("ka", t) for t in range(NT)] + [("bias", h) for h in range(6)]
        plan += [("level", 0)] + [("va", t) for t in range(NT)] + [("level", 1)] + [("ib", t) for t in range(NT)]
        plan += [("level", 2)] + [("og", t) for t in range(NT)] + [("level", 3)] + [("memT", k) for k in range(KD)]
        plan += [("level", 4), ("kv", 0), ("level", 5), ("kv", 1), ("level", 6)]
        plan += [("qc", t) for t in range(NT)] + [("level", 7), ("kdT", 0), ("kdT", 1), ("increments", 0)]
        plan += [("o", c) for c in range(NT)]
        units = [u for u in plan if u[0] not in ("level", "increments")]
        number = {u: n for n, u in enumerate(units)}
        group_of = {"qf": 0, "qa": 1, "ka": 2, "va": 3, "ib": 4, "og": 5, "kv": 6, "qc": 7}
        token_major = {"qa": (qa, AW), "ka": (ka, AW), "va": (va, AW), "ib": (ib, BV), "og": (og, BV), "qc": (qc, CW)}

        def score_at(c, h):
            return (c // 2 * 2 + h % 2) * 4 + c % 2 * 2 + h // 2

        def ring_value(g):
            return 16 * (g // 3 + 1)

        block = ctx.enter_context(nc.Block())

        @block.sync
        def _(sp):
            sp.dma_start(square[:, :, :], const["square"]).then_inc(c_in[0], 16)
            for t in range(NT):
                sp.dma_start(x_tok[:, t, :], io["x"][0, t * P:(t + 1) * P, :]).then_inc(x_in[t], 16)
            w_in = io["w_in"][0].rearrange("(k p) n -> p k n", p=P)

            def load_group(g):
                column, width = groups[g]
                if g >= 3:
                    sp.wait_ge(w_used, g - 2)
                src = (io["w_mem_kv"][0].rearrange("(k p) n -> p k n", p=P) if column is None
                       else w_in[:, :, column:column + width])
                sp.dma_start(ring[:, g % 3, :, 0:width], src).then_inc(ring_in[g % 3], 16)

            load_group(0)
            load_group(1)
            sp.dma_start(mem[:, :, :], io["mem"][0].rearrange("(t p) d -> p t d", p=P)).then_inc(mem_in, 16)
            load_group(2)
            sp.wait_ge(unit_out, number["table", 1] + 1)
            sp.dma_start(table_dram, table[0:6, :]).then_inc(table_out, 16)
            sp.wait_ge(table_out, 16)
            for h in range(6):
                src = bass.AP(table_dram.tensor, h * SPAN, [[1, P], [1, T]])
                sp.dma_start(hankel[:, h, :], src).then_inc(hankel_in, 16)
            for g in range(3, len(groups)):
                load_group(g)
            sp.wait_ge(w_used, 6)
            sp.dma_start(w_a[:, :, :], io["w_branch_a"][0].rearrange("(k p) n -> p k n", p=P)).then_inc(branch_in[0], 16)
            sp.dma_start(w_router[:, :, :], io["w_router"][0].rearrange("(k p) n -> p k n", p=P)).then_inc(c_in[10], 16)
            sp.wait_ge(w_used, 7)
            sp.dma_start(ring[:, 0, :, :], w_in[:, :, GATES:GATES + 512]).then_inc(ring_in[0], 16)
            sp.wait_ge(w_used, 8)
            sp.dma_start(ring[:, 1, :, :], w_in[:, :, GATES + 512:GATES + 1024]).then_inc(ring_in[1], 16)
            with sp.Fori(0, A_PAIRS - 1) as i:
                for s in range(2):
                    sp.wait_ge(gate_done, i * UNITS + (s + 1) * NT)
                    src = w_in[:, :, bass.ds(i * 1024 + (GATES + 1024 + s * 512), 512)]
                    sp.dma_start(ring[:, s, :, :], src).then_inc(ring_in[s], 16)
            sp.wait_ge(gate_done, A_PAIRS * UNITS)
            sp.wait_ge(max_ready, A_PAIRS * UNITS)
            sp.dma_start(w_b[:, :, :], io["w_branch_b"][0].rearrange("(k p) n -> p k n", p=P)).then_inc(branch_in[1], 16)
            sp.dma_start(w_c[:, :, :], io["w_branch_c"][0].rearrange("(k p) n -> p k n", p=P)).then_inc(branch_in[2], 16)
            sp.dma_start(w_out[:, :, :], io["w_out"][0].rearrange("(k p) n -> p k n", p=P)).then_inc(branch_in[3], 16)
            sp.dma_start(ffn_gain, bcast(io["ffn_norm_g"], P, D)).then_inc(c_in[11], 16)
            sp.wait_ge(yT_done, KD)
            sp.dma_start(router_bias, bcast(io["router_bias"], P, E)).then_inc(c_in[9], 16)
            sp.dma_start(rs[:, 616:620], const["tokens"]).then_inc(c_in[9], 16)
            sp.wait_ge(mixed, KD)
            sp.dma_start(w_sup[:, :, :], io["w_shared_up"][0].rearrange("(k p) n -> p k n", p=P)).then_inc(shared_in[0], 16)
            sp.wait_ge(mix_done, 3 * KD)
            sp.dma_start(w_sdn[:, :, :], io["w_shared_down"][0].rearrange("(k p) n -> p k n", p=P)).then_inc(shared_in[1], 16)
            for t in range(NT):
                sp.wait_ge(u_ready, t + 1)
                sp.dma_start(u_dram[t * P:(t + 1) * P, :], u_tok[:, t, :]).then_inc(u_stored, 16)

            up_src = io["w_exp_up"][0].rearrange("e (k p) n -> p e k n", p=P)
            dn_src = io["w_exp_down"][0].rearrange("e (k p) n -> p e k n", p=P)

            def load_expert(e, s, n):
                if not isinstance(n, int) or n >= SLOTS:
                    sp.wait_ge(up_done, n - (SLOTS - 1))
                sp.dma_start(w_up[s][:, :, :], up_src[:, e]).then_inc(up_in[s], 16)
                if not isinstance(n, int) or n >= SLOTS:
                    sp.wait_ge(down_done, n - (SLOTS - 1))
                sp.dma_start(w_dn[s][:, :, :], dn_src[:, e]).then_inc(dn_in[s], 16)

            sp.wait_ge(x1_done, 2 * NT)
            load_expert(0, 0, 0)
            load_expert(1, 1, 1)
            sp.wait_ge(u_stored, 16 * NT)
            sp.wait_ge(uT_done, NT)
            load_expert(2, 2, 2)
            sp.wait_ge(s_up, NT)
            load_expert(3, 3, 3)
            for t in range(NT):
                sp.wait_ge(out_ready, t + 1)
                sp.dma_start(out[0, t * P:(t + 1) * P, :], x_tok[:, t, :]).then_inc(out_stored, 16)
            with sp.Fori(1, E // SLOTS) as g:
                for s in range(SLOTS):
                    load_expert(g * SLOTS + s, s, g * SLOTS + s)
            sp.wait_ge(routed, 1)
            fullest = sp.value_load(most_i[0:1, 0:1], min_val=0, max_val=T)
            with sp.If(fullest > P):
                with sp.Fori(0, PASSES - 1) as r:
                    with sp.Fori(0, E // SLOTS) as g:
                        for s in range(SLOTS):
                            load_expert(g * SLOTS + s, s, r * E + (g * SLOTS + (E + s)))

        @block.gpsimd
        def _(pool):
            pool.dma_start(gains[:, 0:8], io["attn_norm_g"][0].rearrange("(k p) -> p k", p=P),
                           allow_slow_non_contiguous=True).then_inc(c_in[1], 16)
            pool.dma_start(gains[:, 8:16], io["mem_norm_g"][0].rearrange("(k p) -> p k", p=P),
                           allow_slow_non_contiguous=True).then_inc(c_in[2], 16)
            for n, name in enumerate(("q_norm_a", "k_norm_a", "q_norm_c", "k_norm_c")):
                for half in range(2):
                    pool.dma_start(gains[half * HD:(half + 1) * HD, 16 + n:17 + n], io[name].rearrange("a p -> p a"),
                                   allow_slow_non_contiguous=True).then_inc(c_in[3], 16)
            pool.dma_start(lb[:, 0:4], io["lb_logits"].rearrange("r (b p) -> p (r b)", p=P),
                           allow_slow_non_contiguous=True).then_inc(c_in[4], 16)
            pool.dma_start(rel[0:32, :], io["rel_bias"]).then_inc(c_in[5], 16)
            pool.dma_start(bucket[0:33, :], const["bucket"]).then_inc(c_in[6], 16)
            pool.dma_start(out_norm, bcast(io["out_norm_b"], P, BV)).then_inc(c_in[7], 16)
            pool.memset(gains[:, 20:21], EPS).then_inc(c_in[8], 1)
            pool.wait_ge(c_in[8], 1)
            pool.memset(rel[32:33, :], 1.0).then_inc(c_in[8], 1)

            pool.wait_ge(y_done, (A_PAIRS + C_PAIRS) * UNITS)
            pool.wait_ge(x1_done, 1)
            pool.memset(gathered[:, :, :], 0.0).then_inc(cleared, 1)
            bound = pool.to_reg(T - 1)
            count = pool.alloc_register("experts_done")
            target = pool.alloc_register("wait_value")
            out_rows = out.rearrange("a t d -> (a t) d")

            def wait_count(semaphore, scale, plus):
                pool.reg_mul(target, count, scale) if scale != 1 else pool.reg_mov(target, count)
                pool.reg_add(target, target, plus)
                pool.wait_ge(cleared, 1)
                pool.wait_ge(semaphore, target)

            def gather(n, ahead):
                wait_count(index_ready, 1, ahead + 1)
                if ahead >= 2:
                    wait_count(gT_done, 1, ahead - 1)
                pool.indirect_dma_start(gathered[:, n % 2, :], None, u_dram,
                                        bass.IndirectOffsetOnAxis(ap=index[:, n % 4:n % 4 + 1], axis=0),
                                        bounds_check=bound, oob_is_err=False).then_inc(gather_in[n % 2], 16)

            def scatter(n):
                wait_count(y_out_a, 1, 1)
                wait_count(y_out_v, 1, 1)
                if n > 0 or not first_pass[0]:
                    wait_count(added, 16, 0)
                pool.indirect_dma_start(out_rows, bass.IndirectOffsetOnAxis(ap=index[:, n % 4:n % 4 + 1], axis=0),
                                        y_out[:, n % 2, :], None, bounds_check=bound, oob_is_err=False,
                                        compute_op=ALU.add).then_inc(added, 16)
                pool.reg_add(count, count, 1)

            def expert_pass():
                gather(0, 0)
                gather(1, 1)
                for n in range(SLOTS):
                    gather(n + 2, 2)
                    scatter(n)
                first_pass[0] = False
                with pool.Fori(1, E // SLOTS - 1):
                    for n in range(SLOTS):
                        gather(n + 2, 2)
                        scatter(n)
                for n in range(SLOTS):
                    if n + 2 < SLOTS:
                        gather(n + 2, 2)
                    scatter(n)

            first_pass = [True]
            pool.reg_mov(count, 0)
            pool.wait_ge(cleared, 1)
            pool.wait_ge(u_stored, 16 * NT)
            pool.wait_ge(out_stored, 16 * NT)
            expert_pass()
            fullest = pool.value_load(most_i[0:1, 0:1], min_val=0, max_val=T)
            pool.wait_ge(added, 16 * E)
            with pool.If(fullest > P):
                with pool.Fori(0, PASSES - 1):
                    expert_pass()
                pool.wait_ge(added, 16 * E * PASSES)

        @block.scalar
        def _(act):
            def copy(o, i, **kw):
                return nc.scalar.activation(o, i, ACT.Copy, **kw)

            act.wait_ge(c_in[8], 2)
            for t in range(NT):
                act.wait_ge(x_in[t], 16)
                nc.scalar.activation(xn[:, t, :], x_tok[:, t, :], ACT.Square,
                                     accum_out=small[:, t:t + 1]).then_inc(x_squared, 1)
            act.wait_ge(x_squared, NT)
            nc.scalar.activation(small[:, 6:10], small[:, 0:4], ACT.Sqrt, bias=gains[:, 20:21],
                                 scale=1.0 / D).then_inc(x_rooted, 1)
            act.wait_ge(mem_in, 16)
            for t in range(NM):
                nc.scalar.activation(memT[:, 0:4, :].rearrange("p a b -> p (a b)") if t == 0 else
                                     memT[:, 4:8, :].rearrange("p a b -> p (a b)"), mem[:, t, :], ACT.Square,
                                     accum_out=small[:, 4 + t:5 + t]).then_inc(x_squared, 1)
            act.wait_ge(x_squared, NT + NM)
            nc.scalar.activation(small[:, 10:12], small[:, 4:6], ACT.Sqrt, bias=gains[:, 20:21],
                                 scale=1.0 / D).then_inc(x_rooted, 1)
            act.wait_ge(lb_in_exp, 1)
            nc.scalar.activation(lb[:, 0:4], lb[:, 0:4], ACT.Exp).then_inc(lb_exp, 1)

            def exponents(j):
                if j <= LEVELS:
                    act.wait_ge(diff_ready, j + 1)
                e = expo[j % 2]
                if j < LEVELS:
                    m = 1 << (LEVELS - 1 - j)
                    v = e.rearrange("p b (n m) -> p (b n) m", m=2 * m)
                    nc.scalar.activation(v[:, :, 0:m], v[:, :, 0:m], ACT.Exp, scale=-1.0).then_inc(expo_ready, 1)
                    nc.scalar.activation(v[:, :, m:2 * m], v[:, :, m:2 * m], ACT.Exp).then_inc(expo_ready, 1)
                elif j == LEVELS:
                    nc.scalar.activation(e, e, ACT.Exp, scale=-1.0).then_inc(expo_ready, 2)
                else:
                    act.wait_ge(kq_ready, j - 1)
                    nc.scalar.activation(e, bT[:, :, :], ACT.Exp).then_inc(expo_ready, 2)

            def forget_gate():
                act.wait_ge(unit_out, number["qf", 3] + 1)
                nc.scalar.activation(expo[0][:, :, :], fT[:, :, :], ACT.Exp, scale=-1.0).then_inc(f_exp, 1)
                act.wait_ge(unit_out, number["qf", 1] + 1)
                nc.scalar.activation(expo[1][:, :, :], qT[:, :, :], ACT.Tanh, scale=0.5).then_inc(q_tanh, 1)
                act.wait_ge(f_ready, 1)
                nc.scalar.activation(fT[:, :, :], fT[:, :, :], ACT.Ln).then_inc(log_ready, 1)

            def roots_a():
                act.wait_ge(qk_summed, 2)
                nc.scalar.activation(small[:, 68:116], small[:, 20:68], ACT.Sqrt, bias=gains[:, 20:21],
                                     scale=1.0 / HD).then_inc(qk_rooted, 1)

            between = {("qa", 0): [forget_gate], ("va", 1): [roots_a]}
            for j, unit in enumerate((("ka", 2), ("bias", 3), ("va", 3), ("ib", 3), ("og", 3), ("memT", 6), ("kv", 0),
                                      ("qc", 1), ("qc", 3))):
                between[unit] = [lambda j=j: exponents(j)]
            act.wait_ge(c_in[1], 16)
            act.wait_ge(c_in[2], 16)
            for n, (kind, k) in enumerate(units):
                for extra in between.get((kind, k), ()):
                    extra()
                bank = ps[n % 4]
                if kind == "ib" and k == 0:
                    act.wait_ge(qk_summed, 2)
                act.wait_ge(unit_done, n + 1)
                if kind == "hT":
                    ins = copy(hT[:, k, :], bank[:, :], scale=gains[:, k:k + 1])
                elif kind == "memT":
                    ins = copy(memT[:, k, :], bank[:, 0:M], scale=gains[:, 8 + k:9 + k])
                elif kind == "table":
                    ins = copy(table[0:6, k * T:min(SPAN, (k + 1) * T)], bank[0:6, 0:min(T, SPAN - k * T)])
                elif kind == "qf":
                    ins = copy((qT, fT)[k // 2][:, k % 2, :], bank[:, :])
                elif kind == "bias":
                    ins = copy(bias[:, k, :], bank[:, :])
                elif kind == "kv":
                    ins = copy(kv[:, k, :], bank[:, :])
                elif kind == "kdT":
                    ins = copy(kdT[:, k, :], bank[:, 0:3 * P])
                elif kind == "o":
                    ins = copy(o_tok[:, k, :], bank[:, 0:BV])
                else:
                    dst, width = token_major[kind]
                    ins = copy(dst[:, k, :], bank[:, 0:width])
                ins.then_inc(unit_out, 1)

            act.wait_ge(state_ready, 6)
            act.wait_ge(unit_out, len(units))
            nc.scalar.activation(o_gate[:, :, :], og[:, :, :], ACT.Tanh, scale=0.5).then_inc(og_tanh, 1)
            act.wait_ge(o_summed, 1)
            nc.scalar.activation(small[:, 180:196], small[:, 164:180], ACT.Sqrt, bias=gains[:, 20:21],
                                 scale=1.0 / VD).then_inc(o_rooted, 1)
            act.wait_ge(c_summed, 2)
            nc.scalar.activation(small[:, 236:260], small[:, 212:236], ACT.Sqrt, bias=gains[:, 20:21],
                                 scale=1.0 / HD).then_inc(c_rooted, 1)

            def attention(i, dilated):
                pairs = 0 if dilated else A_PAIRS
                n0 = i * UNITS + pairs * UNITS
                act.wait_ge(pair_done, i + (pairs + 1))
                copy(qkT[:, 0, :], ps[0][:, :], scale=gains[:, (16 if dilated else 18):(17 if dilated else 19)]).then_inc(pair_out, 1)
                width = T if dilated else M
                copy(qkT[:, 1, 0:width], ps[1][:, 0:width], scale=gains[:, (17 if dilated else 19):(18 if dilated else 20)]).then_inc(pair_out, 1)

                def exponential(j):
                    keys = (j % NT + 1) * P if dilated else M
                    act.wait_ge(max_ready, n0 + (j + 1))
                    src = logits[:, j % 2, 0:keys] if dilated else ps[2 + j % 2][:, 0:keys]
                    nc.scalar.activation(probs[:, j % 2, 0:keys], src, ACT.Exp, bias=small[:, 284 + j % 2:285 + j % 2],
                                         accum_out=small[:, 288 + j % 2:289 + j % 2]).then_inc(exp_done, 1)

                def gate(j):
                    if dilated:
                        act.wait_ge(gate_done, n0 + (j + 1))
                        nc.scalar.activation(ps[6 + j % 2][:, :], ps[6 + j % 2][:, :], ACT.Tanh, scale=0.5).then_inc(gate_tanh, 1)

                gate(0)
                exponential(0)
                for j in range(UNITS):
                    if j + 1 < UNITS:
                        exponential(j + 1)
                        gate(j + 1)
                    keys = (j % NT + 1) * P if dilated else M
                    act.wait_ge(pT_done, n0 + (j + 1))
                    copy(probsT[:, j % 2, 0:keys], ps[4][:, 0:keys]).then_inc(pT_out, 1)

            with act.Fori(0, A_PAIRS) as i:
                attention(i, True)
            with act.Fori(0, C_PAIRS) as i:
                attention(i, False)

            for k in range(KD):
                act.wait_ge(yT_done, k + 1)
                copy(yT[:, k, :], ps[k % 4][:, :]).then_inc(yT_out, 1)

            for t in range(NT):
                act.wait_ge(x1_ready, 2 * t + 2)
                nc.scalar.activation(u_tok[:, t, :], x_tok[:, t, :], ACT.Square,
                                     accum_out=small[:, t:t + 1]).then_inc(x1_squared, 1)
                act.wait_ge(x1_squared, t + 1)
                nc.scalar.activation(small[:, 6 + t:7 + t], small[:, t:t + 1], ACT.Sqrt, bias=gains[:, 20:21],
                                     scale=1.0 / D).then_inc(x1_rooted, 1)
            for t in range(NT):
                act.wait_ge(uT_done, t + 1)
                for half in range(2):
                    copy(uT[:, 4 * half:4 * half + 4, t * P:(t + 1) * P],
                         view(ps[2 * (t % 2) + half][:, :], 4, P)).then_inc(uT_out, 1)
            act.wait_ge(r_done, 1)
            nc.scalar.activation(view(ps[4][:, 0:NT * E], NT, E), view(ps[4][:, 0:NT * E], NT, E), ACT.Tanh, scale=0.5).then_inc(r_tanh, 1)
            for t in range(NT):
                act.wait_ge(s_up, t + 1)
                nc.scalar.activation(s_tanh[:, t % 2, :], ps[t % 2][:, 0:FH], ACT.Tanh, scale=0.5).then_inc(s_tanhed, 1)
                act.wait_ge(s_hidT_done, t + 1)
                copy(s_hidT[:, t % 2, :, :], view(ps[5][:, 0:2 * P], 2, P)).then_inc(s_hidT_out, 1)

            def transposed_tokens(n, m):
                act.wait_ge(gT_done, m + 1)
                copy(gatheredT[:, n % 2, 0:4, :], view(ps[0][:, :], 4, P)).then_inc(gT_out_a, 1)

            def expert(n, m, more):
                act.wait_ge(up_done, m + 1)
                nc.scalar.activation(e_tanh[:, n % 2, :], ps[2][:, 0:FH], ACT.Tanh, scale=0.5).then_inc(tanh_done, 1)
                if more:
                    transposed_tokens(n + 1, m + 1)
                act.wait_ge(hidT_done, m + 1)
                copy(hidT[:, n % 2, :, :], view(ps[3][:, 0:2 * P], 2, P)).then_inc(hidT_out, 1)
                act.wait_ge(down_done, m + 1)
                if not isinstance(m, int) or m >= 2:
                    act.wait_ge(added, m * 16 - 16)
                copy(y_out[:, n % 2, 0:512], ps[4][:, :]).then_inc(y_out_a, 1)

            def expert_pass(m0):
                transposed_tokens(0, m0)
                for n in range(SLOTS):
                    expert(n, m0 + n, True)
                with act.Fori(1, E // SLOTS - 1) as g:
                    for n in range(SLOTS):
                        expert(n, m0 + (g * SLOTS + n), True)
                for n in range(SLOTS):
                    expert(n, m0 + (E - SLOTS + n), n + 1 < SLOTS)

            expert_pass(0)
            fullest = act.value_load(most_i[0:1, 0:1], min_val=0, max_val=T)
            with act.If(fullest > P):
                with act.Fori(0, PASSES - 1) as r:
                    expert_pass(r * E + E)

        @block.vector
        def _(dve):
            v = nc.vector
            steps = [0]

            def then(ins):
                steps[0] += 1
                ins.then_inc(v_step, 1)
                dve.wait_ge(v_step, steps[0])

            dve.wait_ge(x_rooted, 1)
            then(v.reciprocal(small[:, 12:16], small[:, 6:10]))
            for t in range(NT):
                v.tensor_scalar(xn[:, t, :], x_tok[:, t, :], small[:, 12 + t:13 + t], None, ALU.mult).then_inc(x_normed, 1)
            dve.wait_ge(x_rooted, 2)
            then(v.reciprocal(small[:, 16:18], small[:, 10:12]))
            for t in range(NM):
                v.tensor_scalar(mem[:, t, :], mem[:, t, :], small[:, 16 + t:17 + t], None, ALU.mult).then_inc(mem_normed, 1)
            dve.wait_ge(c_in[3], 16 * 8)
            for column in (16, 18):
                then(v.tensor_scalar(gains[:, column:column + 1], gains[:, column:column + 1], HD ** -0.5, None, ALU.mult))
            dve.wait_ge(c_in[4], 16)
            then(v.tensor_tensor(lb[:, 4:6], lb[:, 0:2], lb[:, 2:4], ALU.max))
            then(v.tensor_tensor(lb[:, 0:2], lb[:, 0:2], lb[:, 4:6], ALU.subtract))
            v.tensor_tensor(lb[:, 2:4], lb[:, 2:4], lb[:, 4:6], ALU.subtract).then_inc(lb_in_exp, 1)
            dve.wait_ge(lb_exp, 1)
            then(v.tensor_tensor(lb[:, 4:6], lb[:, 0:2], lb[:, 2:4], ALU.add))
            then(v.reciprocal(lb[:, 6:8], lb[:, 4:6]))
            then(v.tensor_tensor(lb[:, 4:6], lb[:, 0:2], lb[:, 6:8], ALU.mult))
            then(v.tensor_scalar(lb[:, 6:8], lb[:, 4:6], -1.0, 1.0, ALU.mult, ALU.add))
            dve.wait_ge(f_exp, 1)
            then(v.tensor_scalar(expo[0][:, :, :], expo[0][:, :, :], 1.0, None, ALU.add))
            then(v.reciprocal(kT[:, :, :], expo[0][:, :, :]))
            for b in range(2):
                ins = v.tensor_scalar(fT[:, b, :], kT[:, b, :], lb[:, 6 + b:7 + b], lb[:, 4 + b:5 + b], ALU.mult, ALU.add)
                then(ins)
            then(v.tensor_scalar(kT[:, :, :], fT[:, :, :], -1.0, 1.0, ALU.mult, ALU.add))
            v.tensor_copy(small[:, 310:311], small[:, 0:1]).then_inc(f_ready, 1)
            dve.wait_ge(q_tanh, 1)
            then(v.scalar_tensor_tensor(qT[:, :, :], expo[1][:, :, :], 1.0, qT[:, :, :], ALU.add, ALU.mult))
            then(v.tensor_scalar(qT[:, :, :], qT[:, :, :], 0.5 * HD ** -0.5, None, ALU.mult))
            dve.wait_ge(log_ready, 1)
            dve.wait_ge(c_in[0], 16)
            for b in range(2):
                for c in range(NT):
                    last = v.tensor_tensor_scan(bT[:, b, c * P:(c + 1) * P], ones, fT[:, b, c * P:(c + 1) * P],
                                                0.0, ALU.mult, ALU.add)
            then(last)

            def differences(j):
                m = 1 << (LEVELS - 1 - j) if j < LEVELS else P // 2
                ref = m - 1 if j < LEVELS else P - 1
                b_v = bT.rearrange("p b (n m) -> p (b n) m", m=2 * m)
                e_v = expo[j % 2].rearrange("p b (n m) -> p (b n) m", m=2 * m)
                n = 2 * T // (2 * m)
                v.tensor_tensor(e_v, b_v, bcast(b_v[:, :, ref:ref + 1], P, n, 2 * m), ALU.subtract).then_inc(diff_ready, 1)

            def products(j):
                dve.wait_ge(expo_ready, 2 * (j + 1))
                if 2 <= j < LEVELS + 1:
                    dve.wait_ge(level_done, 4 * (j - 1))
                elif j == LEVELS + 1:
                    dve.wait_ge(level_done, 4 * (j - 2))
                if j < LEVELS:
                    m = 1 << (LEVELS - 1 - j)
                    e_v, o_v, k_v, q_v = (a.rearrange("p b (n m) -> p (b n) m", m=2 * m) for a in (expo[j % 2], kq[j % 2], kT, qT))
                    then(v.tensor_tensor(o_v[:, :, 0:m], e_v[:, :, 0:m], k_v[:, :, 0:m], ALU.mult))
                    v.tensor_tensor(o_v[:, :, m:2 * m], e_v[:, :, m:2 * m], q_v[:, :, m:2 * m], ALU.mult).then_inc(kq_ready, 1)
                else:
                    v.tensor_tensor(kq[j % 2][:, :, :], expo[j % 2][:, :, :], (kT if j == LEVELS else qT)[:, :, :],
                                    ALU.mult).then_inc(kq_ready, 1)

            def take_level(j):
                if j > 0:
                    reach = 1 << (LEVELS - j)
                    then(v.tensor_scalar(mask[:, j % 2, :].bitcast(I32), level, float(reach), None, ALU.is_lt))
                for c in range(NT):
                    dve.wait_ge(level_done, 4 * j + c + 1)
                    src = view(ps[4 + c][:, :], 4, P)
                    if j == 0:
                        v.scalar_tensor_tensor(scores[:, 4 * c:4 * c + 4, :], bcast(level[:, None, :], P, 4, P), float(P), src,
                                               ALU.is_lt, ALU.mult).then_inc(level_taken, 1)
                    else:
                        m_v = mask[:, j % 2, :].bitcast(I32)
                        v.copy_predicated(scores[:, 4 * c:4 * c + 4, :], bcast(m_v[:, None, :], P, 4, P), src).then_inc(level_taken, 1)
                dve.wait_ge(level_taken, 4 * (j + 1))

            differences(0)
            differences(1)
            products(0)
            for n, (a, name) in enumerate(((qa, "qa"), (ka, "ka"))):
                dve.wait_ge(unit_out, number[name, NT - 1] + 1)
                then(v.tensor_tensor(squares[:, n, :, :], a[:, :, :], a[:, :, :], ALU.mult))
                v.tensor_reduce(small[:, 20 + 24 * n:44 + 24 * n], squares[:, n, :, :].rearrange("p t (h e) -> p (t h) e", e=HD),
                                AX.X, ALU.add).then_inc(qk_summed, 1)
            dve.wait_ge(unit_out, number["bias", 5] + 1)
            then(v.memset(state[:, :, :, :], 0.0))
            for j in range(LEVELS + 1):
                if j + 1 <= LEVELS + 1:
                    products(j + 1)
                if j + 2 <= LEVELS:
                    differences(j + 2)
                take_level(j)
                if j == 0:
                    dve.wait_ge(qk_rooted, 1)
                    then(v.reciprocal(small[:, 116:164], small[:, 68:116]))
            for c in range(NT - 1):
                dve.wait_ge(inc_done, c + 1)
                for b in range(2):
                    for hh in range(2):
                        rows = slice(hh * HD, (hh + 1) * HD)
                        col = b * 2 * VD + hh * VD
                        inc = ps[4 + c][rows, col:col + VD]
                        cols = slice(hh * VD, (hh + 1) * VD)
                        if c == 0:
                            ins = v.tensor_copy(state[rows, 0, b, cols], inc)
                        else:
                            ins = v.scalar_tensor_tensor(state[rows, c, b, cols], state[rows, c - 1, b, cols],
                                                         expo[(LEVELS + 1) % 2][rows, b, c * P + P - 1:c * P + P], inc,
                                                         ALU.mult, ALU.add)
                        if hh == 0:
                            then(ins)
                        else:
                            ins.then_inc(state_ready, 1)
                dve.wait_ge(state_ready, 2 * (c + 1))
            dve.wait_ge(unit_out, len(units))
            then(v.tensor_tensor(o_sq[:, :, :], o_tok[:, :, :], o_tok[:, :, :], ALU.mult))
            v.tensor_reduce(small[:, 164:180], o_sq.rearrange("p t (h e) -> p (t h) e", e=VD), AX.X, ALU.add).then_inc(o_summed, 1)
            q_sq, k_sq = view(c_sq[:, 0:1024], NT, CW), view(c_sq[:, 1024:1536], NM, CW)
            then(v.tensor_tensor(q_sq, qc[:, :, :], qc[:, :, :], ALU.mult))
            v.tensor_reduce(small[:, 212:228], q_sq.rearrange("p t (h e) -> p (t h) e", e=HD), AX.X, ALU.add).then_inc(c_summed, 1)
            then(v.tensor_tensor(k_sq, kv[:, :, 0:CW], kv[:, :, 0:CW], ALU.mult))
            v.tensor_reduce(small[:, 228:236], k_sq.rearrange("p t (h e) -> p (t h) e", e=HD), AX.X, ALU.add).then_inc(c_summed, 1)
            dve.wait_ge(o_rooted, 1)
            then(v.reciprocal(small[:, 196:212], small[:, 180:196]))
            o_v = o_tok.rearrange("p t (h e) -> p (t h) e", e=VD)
            then(v.tensor_tensor(o_v, o_v, bcast(small[:, 196:212, None], P, 16, VD), ALU.mult))
            dve.wait_ge(c_in[7], 16)
            then(v.tensor_tensor(o_tok[:, :, :], o_tok[:, :, :], bcast(out_norm[:, None, :], P, NT, BV), ALU.mult))
            dve.wait_ge(og_tanh, 1)
            then(v.scalar_tensor_tensor(o_gate[:, :, :], o_gate[:, :, :], 1.0, og[:, :, :], ALU.add, ALU.mult))
            then(v.scalar_tensor_tensor(ib[:, :, :], o_tok[:, :, :], 0.5, o_gate[:, :, :], ALU.mult, ALU.mult))
            dve.wait_ge(c_rooted, 1)
            then(v.reciprocal(small[:, 260:284], small[:, 236:260]))

            loop_steps = [0, 0]

            def attention(i, dilated, base):
                pairs = 0 if dilated else A_PAIRS
                n0 = i * UNITS + pairs * UNITS
                k = [0]

                def then(ins):
                    k[0] += 1
                    ins.then_inc(v_step, 1)
                    dve.wait_ge(v_step, base + k[0])

                q_src, k_src = (qa, ka) if dilated else (qc, kv)
                heads = 6 if dilated else 4
                roots = [(small[:, 116:140], small[:, 140:164]), (small[:, 260:276], small[:, 276:284])][not dilated]
                for which, (src, root) in enumerate(zip((q_src, k_src), roots)):
                    tiles = NM if which and not dilated else NT
                    o_v = staging[:, which, 0:tiles, :].rearrange("p t (h e) -> p t h e", e=HD)
                    for t in range(tiles):
                        s_v = src[:, t, bass.ds(i * P, P)].rearrange("p (h e) -> p h e", e=HD)
                        r_v = root[:, bass.ds(i * 2 + t * heads, 2)]
                        v.tensor_tensor(o_v[:, t], s_v, bcast(r_v.unsqueeze(2), P, 2, HD), ALU.mult).then_inc(staged, 1)

                def maximum(j):
                    keys = (j % NT + 1) * P if dilated else M
                    dve.wait_ge(qk_done, n0 + (j + 1))
                    src = ps[2 + j % 2][:, 0:keys]
                    if dilated:
                        start = (NT - 1 - j % NT) * P
                        table_h = bias[:, bass.ds(i * 2 + j // NT, 1), start:T].rearrange("p a b -> p (a b)")
                        then(v.tensor_tensor(logits[:, j % 2, 0:keys], src, table_h, ALU.add))
                        src = logits[:, j % 2, 0:keys]
                    v.tensor_reduce(small[:, 284 + j % 2:285 + j % 2], src, AX.X, ALU.max, negate=True).then_inc(max_ready, 1)

                def gate(j):
                    if dilated:
                        dve.wait_ge(gate_tanh, n0 + (j + 1))
                        v.tensor_scalar(gates[:, bass.ds(i * UNITS + j, 1), :].rearrange("p a b -> p (a b)"),
                                        ps[6 + j % 2][:, :], 0.5, 0.5, ALU.mult, ALU.add).then_inc(gate_out, 1)

                gate(0)
                maximum(0)
                for j in range(UNITS):
                    if j + 1 < UNITS:
                        maximum(j + 1)
                        gate(j + 1)
                    dve.wait_ge(exp_done, n0 + (j + 1))
                    then(v.reciprocal(small[:, 292 + j % 2:293 + j % 2], small[:, 288 + j % 2:289 + j % 2]))
                    dve.wait_ge(pv_done, n0 + (j + 1))
                    dst = q_src[:, j % NT, bass.ds(i * P + (j // NT) * HD, HD)]
                    v.tensor_scalar(dst, ps[j % 2][:, 0:HD], small[:, 292 + j % 2:293 + j % 2], None,
                                    ALU.mult).then_inc(y_done, 1)
                return k[0]

            a_turn, c_turn = 2 * UNITS, UNITS
            with dve.Fori(0, A_PAIRS) as i:
                assert attention(i, True, i * a_turn + steps[0]) == a_turn
            steps[0] += A_PAIRS * a_turn
            with dve.Fori(0, C_PAIRS) as i:
                assert attention(i, False, i * c_turn + steps[0]) == c_turn
            steps[0] += C_PAIRS * c_turn

            for m in range(KD):
                for br in range(3):
                    n = 3 * m + br
                    dve.wait_ge(mix_done, n + 1)
                    g = gates[:, br * KD + m, :]
                    v.tensor_tensor(g, g, ps[4 + n % 4][:, :], ALU.mult).then_inc(mix_taken, 1)
                dve.wait_ge(mix_taken, 3 * m + 3)
                then(v.tensor_tensor(gates[:, m, :], gates[:, m, :], gates[:, KD + m, :], ALU.add))
                v.tensor_tensor(gates[:, m, :], gates[:, m, :], gates[:, 2 * KD + m, :], ALU.add).then_inc(mixed, 1)
            for n in range(2 * NT):
                t, half = n // 2, n % 2
                dve.wait_ge(x1_done, n + 1)
                x_v = x_tok[:, t, half * 512:(half + 1) * 512]
                v.tensor_tensor(x_v, x_v, ps[n % 4][:, :], ALU.add).then_inc(x1_ready, 1)
            dve.wait_ge(c_in[11], 16)
            for t in range(NT):
                dve.wait_ge(x1_rooted, t + 1)
                then(v.reciprocal(small[:, 12 + t:13 + t], small[:, 6 + t:7 + t]))
                v.scalar_tensor_tensor(u_tok[:, t, :], x_tok[:, t, :], small[:, 12 + t:13 + t], ffn_gain, ALU.mult,
                                       ALU.mult).then_inc(u_ready, 1)

            def shared(t):
                dve.wait_ge(s_tanhed, t + 1)
                then(v.scalar_tensor_tensor(s_tanh[:, t % 2, :], s_tanh[:, t % 2, :], 1.0, ps[t % 2][:, 0:FH], ALU.add, ALU.mult))
                v.scalar_tensor_tensor(s_hid[:, t % 2, :], s_tanh[:, t % 2, :], 0.5, ps[t % 2][:, FH:2 * FH], ALU.mult,
                                       ALU.mult).then_inc(s_hidden, 1)
                for half in range(2):
                    dve.wait_ge(s_down, 2 * t + half + 1)
                    x_v = x_tok[:, t, half * 512:(half + 1) * 512]
                    ins = v.tensor_tensor(x_v, x_v, ps[2 + half][:, :], ALU.add)
                    if half:
                        ins.then_inc(out_ready, 1)
                    else:
                        then(ins)

            dve.wait_ge(r_tanh, 1)
            dve.wait_ge(c_in[9], 32)
            r_ps = view(ps[4][:, 0:NT * E], NT, E)
            then(v.tensor_scalar(score, r_ps, 0.5, 0.5, ALU.mult, ALU.add))
            then(v.tensor_tensor(choice, score, bcast(router_bias[:, None, :], P, NT, E), ALU.add))
            best = view(rs[:, 0:256], NT * GROUPS, 8)
            for n in range(NT * GROUPS):
                t, g = divmod(n, GROUPS)
                last = v.max(best[:, n, :], choice[:, t, g * 8:(g + 1) * 8])
            then(last)
            group_score = view(rs[:, 256:288], NT, GROUPS)
            then(v.tensor_tensor(rs[:, 256:288], best[:, :, 0:1].rearrange("p n a -> p (n a)"),
                                 best[:, :, 1:2].rearrange("p n a -> p (n a)"), ALU.add))
            group_top, group_at = view(rs[:, 288:320], NT, 8), view(rs[:, 320:352], NT, 8)
            for t in range(NT):
                last = v.max(group_top[:, t, :], group_score[:, t, :])
            then(last)
            for t in range(NT):
                last = v.max_index(group_at[:, t, :].bitcast(U32), group_top[:, t, :], group_score[:, t, :])
            then(last)
            group_f = view(rs[:, 352:384], NT, 8)
            then(v.tensor_copy(rs[:, 352:384], rs[:, 320:352].bitcast(U32)))
            group_hit = view(rs[:, 384:512], NT, GROUPS, TOP_GROUPS)
            for t in range(NT):
                last = v.tensor_tensor(group_hit[:, t], bcast(counting[:, 0:GROUPS, None], P, GROUPS, TOP_GROUPS),
                                       bcast(group_f[:, t, None, 0:TOP_GROUPS], P, GROUPS, TOP_GROUPS), ALU.is_equal)
            then(last)
            group_mask = view(rs[:, 512:544], NT, GROUPS)
            then(v.tensor_reduce(rs[:, 512:544], group_hit.rearrange("p t g k -> p (t g) k"), AX.X, ALU.add))
            then(v.tensor_scalar(rs[:, 544:576], rs[:, 512:544], -MASKED, MASKED, ALU.mult, ALU.add))
            m_v, c_v = (a.rearrange("p t (g k) -> p (t g) k", k=8) for a in (masked, choice))
            then(v.tensor_tensor(m_v, c_v, bcast(rs[:, 512:544, None], P, 32, 8), ALU.mult))
            then(v.tensor_tensor(m_v, m_v, bcast(rs[:, 544:576, None], P, 32, 8), ALU.add))
            top8 = view(rs[:, 576:608], NT, 8)
            for t in range(NT):
                last = v.max(top8[:, t, :], masked[:, t, :])
            then(last)
            for t in range(NT):
                last = v.match_replace(masked2[:, t, :], top8[:, t, :], masked[:, t, :], 3 * MASKED)
            then(last)
            v.tensor_scalar(picked, masked2, 2 * MASKED, None, ALU.is_lt).then_inc(picked_ready, 1)
            dve.wait_ge(picked_ready, 1)
            then(v.tensor_tensor(weight, score, picked, ALU.mult))
            then(v.tensor_reduce(rs[:, 608:612], weight, AX.X, ALU.add))
            then(v.reciprocal(rs[:, 612:616], rs[:, 608:612]))
            then(v.tensor_scalar(rs[:, 612:616], rs[:, 612:616], ROUTED_SCALE, None, ALU.mult))
            dve.wait_ge(c_in[9], 32)
            for t in range(NT):
                v.tensor_scalar(route_in[:, t, :, 1], weight[:, t, :], rs[:, 612 + t:613 + t], 0.5, ALU.mult, ALU.mult)
                last = v.tensor_scalar(route_in[:, t, :, 0], picked[:, t, :], 0.0, rs[:, 616 + t:617 + t], ALU.mult, ALU.add)
            then(last)
            dve.wait_ge(place_done, 1)
            p_v = view(ps[4][:, 256:256 + NT * E], NT, E)
            then(v.scalar_tensor_tensor(place, p_v, 1.0, picked, ALU.add, ALU.mult))
            then(v.tensor_scalar(place, place, -1.0, None, ALU.add))
            then(v.tensor_reduce(most, ps[5][:, 256:256 + E], AX.X, ALU.max))
            v.tensor_copy(most_i, most).then_inc(routed, 1)
            for t in range(NT):
                shared(t)

            def expert(n, m, e, more, more2, more3, base, k):
                def then(ins):
                    k[0] += 1
                    ins.then_inc(v_step, 1)
                    dve.wait_ge(v_step, base + k[0])

                dve.wait_ge(tanh_done, m + 1)
                then(v.scalar_tensor_tensor(e_act[:, n % 2, :], e_tanh[:, n % 2, :], 1.0, ps[2][:, 0:FH], ALU.add, ALU.mult))
                v.scalar_tensor_tensor(hid[:, n % 2, :], e_act[:, n % 2, :], slot_w[:, n % 4:n % 4 + 1], ps[2][:, FH:2 * FH],
                                       ALU.mult, ALU.mult).then_inc(hid_ready, 1)
                if more:
                    transposed_tokens(n + 1, m + 1)
                if more2:
                    read_route(n + 2, m + 2)
                if more3:
                    choose(n + 3, m + 3, e + 3)
                dve.wait_ge(down_done, m + 1)
                if not isinstance(m, int) or m >= 2:
                    dve.wait_ge(added, m * 16 - 16)
                v.tensor_copy(y_out[:, n % 2, 512:1024], ps[6][:, :]).then_inc(y_out_v, 1)

            def transposed_tokens(n, m):
                dve.wait_ge(gT_done, m + 1)
                v.tensor_copy(gatheredT[:, n % 2, 4:8, :], view(ps[1][:, :], 4, P)).then_inc(gT_out_v, 1)

            def read_route(n, m):
                dve.wait_ge(route_done, m + 1)
                if not isinstance(m, int) or m >= 4:
                    dve.wait_ge(added, m * 16 - 48)
                v.tensor_copy(slot_w[:, n % 4:n % 4 + 1], ps[7][:, 1:2])
                v.tensor_scalar(index[:, n % 4:n % 4 + 1], ps[7][:, 0:1], NO_TOKEN, None,
                                ALU.add).then_inc(index_ready, 1)

            def choose(n, m, e):
                if not isinstance(m, int) or m >= 2:
                    dve.wait_ge(route_done, m - 1)
                for t in range(NT):
                    v.tensor_scalar(select[:, n % 2, t, :], counting, place[:, t, bass.ds(e, 1)], None,
                                    ALU.is_equal).then_inc(sel_ready, 1)

            def expert_pass(m0, base):
                choose(0, m0, 0)
                choose(1, m0 + 1, 1)
                read_route(0, m0)
                read_route(1, m0 + 1)
                transposed_tokens(0, m0)
                choose(2, m0 + 2, 2)
                k = [0]
                for n in range(SLOTS):
                    expert(n, m0 + n, n, True, True, True, base, k)
                turn = k[0]
                with dve.Fori(1, E // SLOTS - 1) as g:
                    k = [0]
                    for n in range(SLOTS):
                        expert(n, m0 + (g * SLOTS + n), g * SLOTS + n, True, True, True, base + g * turn, k)
                    assert k[0] == turn
                k = [0]
                for n in range(SLOTS):
                    expert(n, m0 + (E - SLOTS + n), E - SLOTS + n, n + 1 < SLOTS, n + 2 < SLOTS, n + 3 < SLOTS,
                           base + (E // SLOTS - 1) * turn, k)
                return E // SLOTS * turn

            total = expert_pass(0, steps[0])
            fullest = dve.value_load(most_i[0:1, 0:1], min_val=0, max_val=T)
            with dve.If(fullest > P):
                with dve.Fori(0, PASSES - 1) as r:
                    start = r * (total + 1) + (steps[0] + total)
                    v.tensor_scalar(place, place, -float(P), None, ALU.add).then_inc(v_step, 1)
                    dve.wait_ge(v_step, start + 1)
                    expert_pass(r * E + E, start + 1)

        @block.tensor
        def _(pe):
            mm = nc.tensor.matmul
            tr = nc.tensor.transpose
            pe.wait_ge(c_in[0], 16)
            pe.wait_ge(c_in[5], 16)
            pe.wait_ge(c_in[6], 16)
            pe.wait_ge(c_in[8], 2)
            n = 0
            for kind, k in plan:
                if kind == "level":
                    left, right = (kT, qT) if k == LEVELS else (kq[k % 2], kq[k % 2])
                    if k < LEVELS:
                        pe.wait_ge(kq_ready, k + 1)
                    for q in range(4):
                        if k > 0:
                            pe.wait_ge(level_taken, 4 * (k - 1) + q + 1)
                        rows = slice(q % 2 * HD, (q % 2 + 1) * HD)
                        for z in range(4):
                            b, c = z % 2, q // 2 * 2 + z // 2
                            last = mm(ps[4 + q][:, z * P:(z + 1) * P], left[rows, b, c * P:(c + 1) * P],
                                      right[rows, b, c * P:(c + 1) * P], start=True, stop=True)
                        last.then_inc(level_done, 1)
                    continue
                if kind == "increments":
                    pe.wait_ge(unit_out, number["kdT", 1] + 1)
                    pe.wait_ge(level_taken, 4 * (LEVELS + 1))
                    for c in range(NT - 1):
                        for b in range(2):
                            last = mm(ps[4 + c][:, b * 2 * VD:(b + 1) * 2 * VD], kdT[:, b, c * P:(c + 1) * P],
                                      ib[:, c, b * 2 * VD:(b + 1) * 2 * VD], start=True, stop=True)
                        last.then_inc(inc_done, 1)
                    continue
                bank = ps[n % 4]
                if n >= 4:
                    pe.wait_ge(unit_out, n - 3)
                if kind in group_of and k in (0, 2) :
                    pe.wait_ge(ring_in[group_of[kind] % 3], ring_value(group_of[kind]))
                if kind == "hT":
                    if k == 0:
                        pe.wait_ge(x_normed, NT)
                    for t in range(NT):
                        last = tr(bank[:, t * P:(t + 1) * P], xn[:, t, k * P:(k + 1) * P], ident)
                elif kind == "memT":
                    if k == 0:
                        pe.wait_ge(mem_normed, NM)
                    for t in range(NM):
                        last = tr(bank[:, t * P:(t + 1) * P], mem[:, t, k * P:(k + 1) * P], ident)
                elif kind == "table":
                    lo, hi = k * T, min(SPAN, (k + 1) * T)
                    last = mm(bank[0:6, 0:hi - lo], rel[0:33, :], bucket[0:33, lo:hi], start=True, stop=True)
                elif kind == "qf":
                    pe.wait_ge(unit_out, KD)
                    for kk in range(KD):
                        last = mm(bank[:, :], ring[:, 0, kk, k * P:(k + 1) * P], hT[:, kk, :], start=kk == 0, stop=kk == KD - 1)
                elif kind == "bias":
                    if k == 0:
                        pe.wait_ge(hankel_in, 16 * 6)
                    last = mm(bank[:, :], flip, hankel[:, k, :], start=True, stop=True)
                elif kind == "kv":
                    pe.wait_ge(unit_out, number["memT", KD - 1] + 1)
                    for kk in range(KD):
                        last = mm(bank[:, :], memT[:, kk, k * P:(k + 1) * P], ring[:, 0, kk, :], start=kk == 0, stop=kk == KD - 1)
                elif kind == "kdT":
                    if k == 0:
                        pe.wait_ge(kq_ready, LEVELS + 1)
                    for c in range(NT - 1):
                        last = tr(bank[:, c * P:(c + 1) * P], kq[LEVELS % 2][:, k, c * P:(c + 1) * P], ident)
                elif kind == "o":
                    pe.wait_ge(kq_ready, LEVELS + 2)
                    if k > 0:
                        pe.wait_ge(state_ready, 2 * k)
                    for b in range(2):
                        if k > 0:
                            mm(bank[:, b * 2 * VD:(b + 1) * 2 * VD], kq[(LEVELS + 1) % 2][:, b, k * P:(k + 1) * P],
                               state[:, k - 1, b, :], start=True, stop=False)
                        for hh in range(2):
                            h = 2 * b + hh
                            last = mm(bank[:, h * VD:(h + 1) * VD], scores[:, score_at(k, h), :],
                                      ib[:, k, h * VD:(h + 1) * VD], start=k == 0, stop=k == 0 or hh == 1)
                else:
                    width = token_major[kind][1]
                    for kk in range(KD):
                        last = mm(bank[:, 0:width], hT[:, kk, k * P:(k + 1) * P], ring[:, group_of[kind] % 3, kk, 0:width],
                                  start=kk == 0, stop=kk == KD - 1)
                last.then_inc(unit_done, 1)
                n += 1
                if kind in group_of and (kind, k) in (("qf", 1), ("qa", 3), ("ka", 3), ("va", 3), ("ib", 3), ("og", 3), ("kv", 1), ("qc", 3)):
                    pe.wait_ge(unit_done, n)
                    pe.sem_inc(w_used, 1)

            def attention(i, dilated):
                pairs = 0 if dilated else A_PAIRS
                n0 = i * UNITS + pairs * UNITS
                k_tiles = NT if dilated else NM
                width = k_tiles * P
                pe.wait_ge(staged, (i * (2 * NT) if dilated else i * (NT + NM)) + (A_PAIRS * 2 * NT * (not dilated) + NT + k_tiles))
                for which, tiles in ((0, NT), (1, k_tiles)):
                    for t in range(tiles):
                        last = tr(ps[which][:, t * P:(t + 1) * P], staging[:, which, t, :], ident)
                last.then_inc(pair_done, 1)

                def gate(j):
                    if not dilated:
                        return
                    if j % NT == 0:
                        pe.wait_ge(ring_in[j // NT], i * 16 + 64)
                    if j >= 2:
                        pe.wait_ge(gate_out, n0 + (j - 1))
                    for kk in range(KD):
                        last = mm(ps[6 + j % 2][:, :], ring[:, j // NT, kk, (j % NT) * P:(j % NT + 1) * P], hT[:, kk, :],
                                  start=kk == 0, stop=kk == KD - 1)
                    last.then_inc(gate_done, 1)

                def scores_of(j):
                    hh, t = divmod(j, NT)
                    keys = (t + 1) * P if dilated else M
                    rows = slice(hh * HD, (hh + 1) * HD)
                    if j >= 2:
                        pe.wait_ge(max_ready if dilated else exp_done, n0 + (j - 1))
                    mm(ps[2 + j % 2][:, 0:keys], qkT[rows, 0, t * P:(t + 1) * P], qkT[rows, 1, 0:keys], start=True,
                       stop=True).then_inc(qk_done, 1)

                gate(0)
                pe.wait_ge(pair_out, i * 2 + (2 * pairs + 2))
                scores_of(0)
                for j in range(UNITS):
                    hh, t = divmod(j, NT)
                    if j + 1 < UNITS:
                        scores_of(j + 1)
                        gate(j + 1)
                    tiles = t + 1 if dilated else NM
                    pe.wait_ge(exp_done, n0 + (j + 1))
                    for kt in range(tiles):
                        last = tr(ps[4][:, kt * P:(kt + 1) * P], probs[:, j % 2, kt * P:(kt + 1) * P], ident)
                    last.then_inc(pT_done, 1)
                    pe.wait_ge(pT_out, n0 + (j + 1))
                    if j >= 2:
                        pe.wait_ge(y_done, n0 + (j - 1))
                    for kt in range(tiles):
                        values = (va[:, kt, bass.ds(i * P + hh * HD, HD)] if dilated
                                  else kv[:, kt, bass.ds(i * P + (CW + hh * HD), HD)])
                        last = mm(ps[j % 2][:, 0:HD], probsT[:, j % 2, kt * P:(kt + 1) * P], values,
                                  start=kt == 0, stop=kt == tiles - 1)
                    last.then_inc(pv_done, 1)

            with pe.Fori(0, A_PAIRS) as i:
                attention(i, True)
            with pe.Fori(0, C_PAIRS) as i:
                attention(i, False)

            pe.wait_ge(y_done, (A_PAIRS + C_PAIRS) * UNITS)
            pe.wait_ge(pT_out, (A_PAIRS + C_PAIRS) * UNITS)
            for k in range(KD):
                if k >= 4:
                    pe.wait_ge(yT_out, k - 3)
                src, col = (qa, k) if k < 3 else (ib, k - 3) if k < 6 else (qc, k - 6)
                for t in range(NT):
                    last = tr(ps[k % 4][:, t * P:(t + 1) * P], src[:, t, col * P:(col + 1) * P], ident)
                last.then_inc(yT_done, 1)
            pe.wait_ge(yT_out, KD)
            for n in range(3):
                pe.wait_ge(branch_in[n], 16)
            for m in range(KD):
                for br, (w, first, blocks) in enumerate(((w_a, 0, 3), (w_b, 3, 3), (w_c, 6, 2))):
                    n = 3 * m + br
                    if n >= 4:
                        pe.wait_ge(mix_taken, n - 3)
                    for kk in range(blocks):
                        last = mm(ps[4 + n % 4][:, :], w[:, kk, m * P:(m + 1) * P], yT[:, first + kk, :], start=kk == 0, stop=kk == blocks - 1)
                    last.then_inc(mix_done, 1)
            pe.wait_ge(mixed, KD)
            pe.wait_ge(branch_in[3], 16)
            for n in range(2 * NT):
                t, half = n // 2, n % 2
                if n >= 4:
                    pe.wait_ge(x1_ready, n - 3)
                for kk in range(KD):
                    last = mm(ps[n % 4][:, :], gates[:, kk, t * P:(t + 1) * P], w_out[:, kk, half * 512:(half + 1) * 512],
                              start=kk == 0, stop=kk == KD - 1)
                last.then_inc(x1_done, 1)
            pe.wait_ge(x1_ready, 2 * NT)
            for t in range(NT):
                pe.wait_ge(u_ready, t + 1)
                if t >= 2:
                    pe.wait_ge(uT_out, 2 * (t - 1))
                for k in range(KD):
                    last = tr(ps[2 * (t % 2) + k // 4][:, (k % 4) * P:(k % 4 + 1) * P], u_tok[:, t, k * P:(k + 1) * P], ident)
                last.then_inc(uT_done, 1)
            pe.wait_ge(uT_out, 2 * NT)
            pe.wait_ge(c_in[10], 16)
            for t in range(NT):
                for kk in range(KD):
                    last = mm(ps[4][:, t * E:(t + 1) * E], uT[:, kk, t * P:(t + 1) * P], w_router[:, kk, :], start=kk == 0, stop=kk == KD - 1)
            last.then_inc(r_done, 1)

            pe.wait_ge(shared_in[0], 16)
            pe.wait_ge(shared_in[1], 16)
            for t in range(NT + 1):
                if t < NT:
                    if t >= 2:
                        pe.wait_ge(s_hidden, t - 1)
                    for kk in range(KD):
                        last = mm(ps[t % 2][:, :], uT[:, kk, t * P:(t + 1) * P], w_sup[:, kk, :], start=kk == 0, stop=kk == KD - 1)
                    last.then_inc(s_up, 1)
                if t == 1:
                    pe.wait_ge(picked_ready, 1)
                    for tt in range(NT):
                        for other in range(tt + 1):
                            last = mm(ps[4][:, 256 + tt * E:256 + (tt + 1) * E], before if other == tt else ones, picked[:, other, :],
                                      start=other == 0, stop=other == tt)
                    for other in range(NT):
                        last = mm(ps[5][:, 256:256 + E], ones, picked[:, other, :], start=other == 0, stop=other == NT - 1)
                    last.then_inc(place_done, 1)
                    pe.wait_ge(routed, 1)
                if t > 0:
                    q = t - 1
                    pe.wait_ge(s_hidden, q + 1)
                    for f in range(2):
                        last = tr(ps[5][:, f * P:(f + 1) * P], s_hid[:, q % 2, f * P:(f + 1) * P], ident)
                    last.then_inc(s_hidT_done, 1)
                    pe.wait_ge(s_hidT_out, q + 1)
                    if q > 0:
                        pe.wait_ge(out_ready, q)
                    for half in range(2):
                        for f in range(2):
                            last = mm(ps[2 + half][:, :], s_hidT[:, q % 2, f, :], w_sdn[:, f, half * 512:(half + 1) * 512],
                                      start=f == 0, stop=f == 1)
                        last.then_inc(s_down, 1)
            pe.wait_ge(out_ready, NT)

            def route(n, m, e):
                pe.wait_ge(sel_ready, m * NT + NT)
                if not isinstance(m, int) or m >= 1:
                    pe.wait_ge(index_ready, m)
                for t in range(NT):
                    last = mm(ps[7][:, 0:2], select[:, n % 2, t, :],
                              route_in[:, t, bass.ds(e, 1), :].rearrange("p a b -> p (a b)"), start=t == 0, stop=t == NT - 1)
                last.then_inc(route_done, 1)

            def transpose_tokens(n, m, turn):
                pe.wait_ge(gather_in[n % 2], turn * 16 + 16)
                for k in range(KD):
                    last = tr(ps[k // 4][:, (k % 4) * P:(k % 4 + 1) * P], gathered[:, n % 2, k * P:(k + 1) * P], ident)
                last.then_inc(gT_done, 1)

            def expert(n, m, e, turn, slot_turn, more, more2):
                pe.wait_ge(up_in[n], slot_turn * 16 + 16)
                pe.wait_ge(gT_out_a, m + 1)
                pe.wait_ge(gT_out_v, m + 1)
                for kk in range(KD):
                    last = mm(ps[2][:, :], gatheredT[:, n % 2, kk, :], w_up[n][:, kk, :], start=kk == 0, stop=kk == KD - 1)
                last.then_inc(up_done, 1)
                if more:
                    transpose_tokens(n + 1, m + 1, turn + (n + 1) // 2)
                pe.wait_ge(hid_ready, m + 1)
                for f in range(2):
                    last = tr(ps[3][:, f * P:(f + 1) * P], hid[:, n % 2, f * P:(f + 1) * P], ident)
                last.then_inc(hidT_done, 1)
                if more2:
                    route(n + 2, m + 2, e + 2)
                pe.wait_ge(dn_in[n], slot_turn * 16 + 16)
                pe.wait_ge(hidT_out, m + 1)
                if not isinstance(m, int) or m >= 1:
                    pe.wait_ge(y_out_a, m)
                    pe.wait_ge(y_out_v, m)
                for half in range(2):
                    for f in range(2):
                        last = mm(ps[4 + 2 * half][:, :], hidT[:, n % 2, f, :], w_dn[n][:, f, half * 512:(half + 1) * 512],
                                  start=f == 0, stop=f == 1)
                last.then_inc(down_done, 1)

            def expert_pass(m0, pair0, round0):
                route(0, m0, 0)
                route(1, m0 + 1, 1)
                transpose_tokens(0, m0, pair0)
                for n in range(SLOTS):
                    expert(n, m0 + n, n, pair0, round0, True, True)
                with pe.Fori(1, E // SLOTS - 1) as g:
                    for n in range(SLOTS):
                        expert(n, m0 + (g * SLOTS + n), g * SLOTS + n, pair0 + g * (SLOTS // 2), round0 + g, True, True)
                for n in range(SLOTS):
                    expert(n, m0 + (E - SLOTS + n), E - SLOTS + n, pair0 + (E - SLOTS) // 2, round0 + (E // SLOTS - 1),
                           n + 1 < SLOTS, n + 2 < SLOTS)

            expert_pass(0, 0, 0)
            fullest = pe.value_load(most_i[0:1, 0:1], min_val=0, max_val=T)
            with pe.If(fullest > P):
                with pe.Fori(0, PASSES - 1) as r:
                    expert_pass(r * E + E, r * (E // 2) + E // 2, r * (E // SLOTS) + E // SLOTS)


_INS = ['x', 'mem', 'attn_norm_g', 'w_in', 'q_norm_a', 'k_norm_a', 'rel_bias', 'lb_logits', 'out_norm_b',
        'mem_norm_g', 'w_mem_kv', 'q_norm_c', 'k_norm_c', 'w_branch_a', 'w_branch_b', 'w_branch_c', 'w_out',
        'ffn_norm_g', 'w_router', 'router_bias', 'w_exp_up', 'w_exp_down', 'w_shared_up', 'w_shared_down']


def kernel(**inputs):
    import concourse.bacc as _bacc
    from concourse.bass_utils import run_bass_kernel_spmd as _run

    nc = _bacc.Bacc("TRN2", target_bir_lowering=False, num_devices=1)
    arrays, io, const = {}, {}, {}
    for name in _INS:
        a = np.ascontiguousarray(inputs[name])
        arrays[f"in_{name}_dram"] = a
        io[name] = nc.dram_tensor(f"in_{name}_dram", a.shape, mybir.dt.from_np(a.dtype), kind="ExternalInput").ap()
    for name, a in shape_constants().items():
        arrays[f"const_{name}_dram"] = a
        const[name] = nc.dram_tensor(f"const_{name}_dram", a.shape, mybir.dt.from_np(a.dtype), kind="ExternalInput").ap()
    out = nc.dram_tensor("out_0_dram", (1, T, D), F32, kind="ExternalOutput").ap()
    u_dram = nc.dram_tensor("u_rows", (T, D), F32).ap()
    table_dram = nc.dram_tensor("distance_table", (6, SPAN), F32).ap()
    build(nc, io, out, const, u_dram, table_dram)
    r = _run(nc, [arrays], core_ids=[0])
    return r.results[0]["out_0_dram"]
```

```python
from contextlib import ExitStack

import numpy as np

import concourse.bass as bass
from concourse import mybir

F32 = mybir.dt.float32
F32R = mybir.dt.float32r
I32 = mybir.dt.int32
U32 = mybir.dt.uint32
ALU = mybir.AluOpType
ACT = mybir.ActivationFunctionType
AX = mybir.AxisListType

P = 128
D, T, M = 1024, 512, 256
KD, NT, NM = D // P, T // P, M // P
HD = 64
AW, BK, BV, CW = 6 * HD, 4 * HD, 4 * 96, 4 * HD
VD = 96
EPS = 1e-6
LEVELS = 7
E, FH = 64, 256
GROUPS, TOP_GROUPS, TOP_K = 8, 4, 8
ROUTED_SCALE = 2.5
MASKED = -1e30
SPAN = T + P
QA, KA, VA, QB, IB, OG, QC, GATES = 0, 384, 768, 1152, 1664, 2048, 2432, 2688
A_PAIRS, C_PAIRS = 3, 2
UNITS = 2 * NT
ROWS = 96
PASSES = -(-T // ROWS)
TURN = 4
BLOCKS = 3
RAW, SPLIT = 6, 4
NO_TOKEN = 4096.0


def shape_constants():
    i = np.arange(P)
    r, c = i[:, None], i[None, :]
    level = np.where(c >= r, np.bitwise_xor(r, c), 1000)
    square = np.stack([r == c, r + c == P - 1, np.broadcast_to(c, (P, P)), r < c, np.ones((P, P)), level], 1)
    d = T - 1 - np.arange(SPAN)
    times = ((d >= 0) & (d <= 128)).astype(int) + ((d >= 0) & (d % 4 == 0)) + ((d >= 0) & (d % 16 == 0))
    far = 16 + (np.log(np.maximum(d, 1).astype(np.float32) / np.float32(16)) / np.float32(np.log(128.0))
                * np.float32(16)).astype(np.int32)
    bucket = np.where(d < 16, d, np.minimum(far, 31))
    hot = (bucket[None, :] == np.arange(32)[:, None]) & (times > 0)[None, :]
    last = np.where(times > 0, np.log(np.maximum(times, 1)), MASKED)
    tokens = np.stack([i + P * t - NO_TOKEN for t in range(NT)], 1)
    return {
        "square": np.ascontiguousarray(square, dtype=np.float32),
        "bucket": np.concatenate([hot, last[None, :]], 0).astype(np.float32),
        "tokens": np.ascontiguousarray(tokens, dtype=np.float32),
    }


def view(a, *shape):
    names = "abcd"[:len(shape)]
    return a if len(shape) == 1 else a.rearrange(
        f"p ({' '.join(names)}) -> p {' '.join(names)}", **dict(zip(names[1:], shape[1:])))


def bcast(a, *shape):
    return a.broadcast_to(list(shape))


def build(nc, io, out, const, u_dram, table_dram, debug=None):
    ctx = ExitStack()
    with ctx:
        def sem(name):
            return ctx.enter_context(nc.semaphore(name))

        words = 53200
        arena_base = -(-nc.sbuf_base // 32) * 32
        arena = ctx.enter_context(nc.sbuf_tensor("arena", [P, words], F32))
        top = [0]

        def at(offset, *shape):
            return view(arena[:, offset:offset + int(np.prod(shape))], *shape)

        def take(*shape):
            offset = top[0]
            top[0] += int(np.prod(shape))
            assert top[0] <= words, top[0]
            return offset

        square = at(take(6, P), 6, P)
        ident, flip, counting, before, ones, level = (square[:, n, :] for n in range(6))
        gains = at(take(32), 32)
        lb = at(take(8), 8)
        small = at(take(320), 320)
        x_at = take(NT, D)
        x_tok = at(x_at, NT, D)
        hT_at = take(KD, T)
        hT = at(hT_at, KD, T)
        bias_at = take(6, T)
        bias = at(bias_at, 6, T)
        ring_at = take(3, KD, T)
        ring = at(ring_at, 3, KD, T)
        gates_at = take(3 * KD, T)
        gates = at(gates_at, 3 * KD, T)
        qa_at, ka_at, va_at = take(NT, AW), take(NT, AW), take(NT, AW)
        qa, ka, va = (at(o, NT, AW) for o in (qa_at, ka_at, va_at))
        kv = at(take(NM, 2 * CW), NM, 2 * CW)
        ib_at, og_at = take(NT, BV), take(NT, BV)
        ib, og = at(ib_at, NT, BV), at(og_at, NT, BV)
        qc = at(take(NT, CW), NT, CW)
        staging_at = take(2, NT, P)
        staging = at(staging_at, 2, NT, P)
        qkT_at = take(2, T)
        qkT = at(qkT_at, 2, T)
        logits_at = take(2, T)
        logits, probs, probsT = at(logits_at, 2, T), at(take(2, T), 2, T), at(take(2, T), 2, T)
        w_router = at(take(KD, E), KD, E)
        out_norm = at(take(BV), BV)

        xn = at(qa_at, NT, D)
        squares = at(ib_at, 2, NT, AW)
        hankel = at(logits_at, 6, T)
        bucket = at(staging_at, SPAN)
        table = at(qkT_at, SPAN)
        scores = at(logits_at, 16, P)
        kdT = at(logits_at + 2048, 2, 3 * P)
        mask = at(staging_at, 2, P)
        state = at(staging_at + 256, NT - 1, 2, 2 * VD)
        mem = at(gates_at, NM, D)
        memT = at(gates_at + 2048, KD, M)
        rec = gates_at + 4096
        fT, qT, kT, bT = (at(rec + n * 1024, 2, T) for n in range(4))
        expo = [at(rec + (4 + n) * 1024, 2, T) for n in range(2)]
        kq = [at(rec + (6 + n) * 1024, 2, T) for n in range(2)]
        o_tok = at(rec, NT, BV)
        o_sq = at(rec + 2048, NT, BV)
        o_gate = at(rec + 4096, NT, BV)
        c_sq = at(rec + 6144, 2048)
        w_a = at(ring_at + 2 * KD * T, 3, D)
        w_b, w_c = at(hT_at, 3, D), at(hT_at + 3 * D, 2, D)
        ffn_gain = at(hT_at + 5 * D, D)
        w_out = at(ring_at, KD, D)
        yT = at(ka_at, KD, T)
        uT = at(hT_at, KD, T)
        u_tok = at(gates_at + 4096, NT, D)
        w_sup = at(gates_at + 8192, KD, 2 * FH)
        w_sdn = at(ka_at, 2, D)
        s_hid = at(ka_at + 2048, 2, FH)
        s_hidT = at(ka_at + 2560, 2, 2, P)
        s_tanh = at(ka_at + 3072, 2, FH)
        ro = [at(ib_at + n * 256, NT, E) for n in range(16)]
        (score, choice, masked, masked2, picked, weight, place) = ro[0:7]
        router_bias = at(ib_at + 11 * 256, E)
        rs = at(ib_at + 11 * 256 + E, 1024)
        def rounded(name, offset, *shape):
            n = int(np.prod(shape))
            tensor = nc.alloc_sbuf_tensor_at(name, [P, n], F32R, offset=arena_base + 4 * offset)
            return view(tensor[:, 0:n], *shape)

        route_in = rounded("route_in", ib_at + 7 * 256, NT, E, 4)
        raw = at(ring_at, RAW, 4, 512)
        split = [rounded(f"split{n}", o, 2, 4, 512) for n, o in
                 enumerate((gates_at, gates_at + 4096, gates_at + 8192, x_at))]
        gathered = at(staging_at, 2, D)
        y_out = at(logits_at, 2, D)
        select = rounded("select", logits_at + 2048, 2, NT, ROWS)
        gatheredT = rounded("gatheredT", bias_at, 2, 2, KD, ROWS)
        hidT = rounded("hidT", logits_at + 2048 + 2 * NT * ROWS, 2, 2, 2 * ROWS)
        hid = at(qa_at, 2, FH)
        e_tanh = at(qa_at + 512, 2, FH)
        e_act = at(qa_at + 1024, 2, FH)
        index = small[:, 300:304].bitcast(U32)
        slot_w = small[:, 304:308]
        most = small[:, 308:309]
        most_i = small[:, 309:310].bitcast(I32)

        rel = small[:, 312:318]
        ps = [ctx.enter_context(nc.psum_tensor(f"bank{n}", [P, 512], F32)) for n in range(8)]

        c_in = [sem(f"const_in{n}") for n in range(12)]
        x_in = [sem(f"x_in{t}") for t in range(NT)]
        mem_in = sem("mem_in")
        ring_in = [sem(f"ring_in{s}") for s in range(3)]
        table_out, hankel_in = sem("table_out"), sem("hankel_in")
        w_used = sem("w_used")
        x_squared, x_rooted, x_normed, mem_normed = map(sem, ("x_squared", "x_rooted", "x_normed", "mem_normed"))
        unit_done, unit_out = sem("unit_done"), sem("unit_out")
        v_step, a_step = sem("v_step"), sem("a_step")
        lb_in_exp, lb_exp = sem("lb_in_exp"), sem("lb_exp")
        f_exp, f_ready, q_tanh, log_ready = map(sem, ("f_exp", "f_ready", "q_tanh", "log_ready"))
        diff_ready, expo_ready, kq_ready = map(sem, ("diff_ready", "expo_ready", "kq_ready"))
        level_done, level_taken = sem("level_done"), sem("level_taken")
        inc_done, state_ready = sem("inc_done"), sem("state_ready")
        qk_squared, qk_summed, qk_rooted = sem("qk_squared"), sem("qk_summed"), sem("qk_rooted")
        o_summed, o_rooted, og_tanh, c_summed, c_rooted = map(sem, ("o_summed", "o_rooted", "og_tanh", "c_summed", "c_rooted"))
        staged, pair_done, pair_out = map(sem, ("staged", "pair_done", "pair_out"))
        qk_done, max_ready, exp_done, pT_done, pT_out, pv_done, y_done = map(
            sem, ("qk_done", "max_ready", "exp_done", "pT_done", "pT_out", "pv_done", "y_done"))
        gate_done, gate_tanh, gate_out = map(sem, ("gate_done", "gate_tanh", "gate_out"))
        branch_in = [sem(f"branch_in{n}") for n in range(4)]
        yT_done, yT_out, mix_done, mix_taken, mixed = map(sem, ("yT_done", "yT_out", "mix_done", "mix_taken", "mixed"))
        x1_done, x1_ready, x1_squared, x1_rooted, u_ready = map(sem, ("x1_done", "x1_ready", "x1_squared", "x1_rooted", "u_ready"))
        u_stored, uT_done, uT_out = map(sem, ("u_stored", "uT_done", "uT_out"))
        shared_in = [sem("shared_up_in"), sem("shared_down_in")]
        r_done, r_tanh, picked_ready, place_done, routed = map(sem, ("r_done", "r_tanh", "picked_ready", "place_done", "routed"))
        s_up, s_tanhed, s_hidden, s_hidT_done, s_hidT_out, s_down, out_ready, out_stored = map(
            sem, ("s_up", "s_tanhed", "s_hidden", "s_hidT_done", "s_hidT_out", "s_down", "out_ready", "out_stored"))
        raw_in = [sem(f"raw_in{s}") for s in range(RAW)]
        high_done, low_done, block_used = sem("high_done"), sem("low_done"), sem("block_used")
        sel_ready, route_done, index_ready = map(sem, ("sel_ready", "route_done", "index_ready"))
        gather_in = [sem(f"gather_in{n}") for n in range(2)]
        gT_done, gT_high, gT_low = map(sem, ("gT_done", "gT_high", "gT_low"))
        tanh_done, act_ready, hid_ready, hidT_done, hidT_high, hidT_low = map(
            sem, ("tanh_done", "act_ready", "hid_ready", "hidT_done", "hidT_high", "hidT_low"))
        y_ready, added, cleared = map(sem, ("y_ready", "added", "cleared"))

        groups = [(QB, 512), (QA, 384), (KA, 384), (VA, 384), (IB, 384), (OG, 384), (None, 512), (QC, 256)]
        plan = [("hT", k) for k in range(KD)] + [("table", 0), ("table", 1)]
        plan += [("qf", b) for b in (2, 3, 0, 1)]
        plan += [("qa", t) for t in range(NT)] + [("ka", t) for t in range(NT)] + [("bias", h) for h in range(6)]
        plan += [("level", 0)] + [("va", t) for t in range(NT)] + [("level", 1)] + [("ib", t) for t in range(NT)]
        plan += [("level", 2)] + [("og", t) for t in range(NT)] + [("level", 3)] + [("memT", k) for k in range(KD)]
        plan += [("level", 4), ("kv", 0), ("level", 5), ("kv", 1), ("level", 6)]
        plan += [("qc", t) for t in range(NT)] + [("level", 7), ("kdT", 0), ("kdT", 1), ("increments", 0)]
        plan += [("o", c) for c in range(NT)]
        units = [u for u in plan if u[0] not in ("level", "increments")]
        number = {u: n for n, u in enumerate(units)}
        group_of = {"qf": 0, "qa": 1, "ka": 2, "va": 3, "ib": 4, "og": 5, "kv": 6, "qc": 7}
        token_major = {"qa": (qa, AW), "ka": (ka, AW), "va": (va, AW), "ib": (ib, BV), "og": (og, BV), "qc": (qc, CW)}

        def score_at(c, h):
            return (c // 2 * 2 + h % 2) * 4 + c % 2 * 2 + h // 2

        def ring_value(g):
            return 16 * (g // 3 + 1)

        block = ctx.enter_context(nc.Block())

        @block.sync
        def _(sp):
            sp.dma_start(square[:, :, :], const["square"]).then_inc(c_in[0], 16)
            for t in range(NT):
                sp.dma_start(x_tok[:, t, :], io["x"][0, t * P:(t + 1) * P, :]).then_inc(x_in[t], 16)
            w_in = io["w_in"][0].rearrange("(k p) n -> p k n", p=P)

            def load_group(g):
                column, width = groups[g]
                if g >= 3:
                    sp.wait_ge(w_used, g - 2)
                src = (io["w_mem_kv"][0].rearrange("(k p) n -> p k n", p=P) if column is None
                       else w_in[:, :, column:column + width])
                sp.dma_start(ring[:, g % 3, :, 0:width], src).then_inc(ring_in[g % 3], 16)

            load_group(0)
            load_group(1)
            sp.dma_start(mem[:, :, :], io["mem"][0].rearrange("(t p) d -> p t d", p=P)).then_inc(mem_in, 16)
            load_group(2)
            sp.wait_ge(unit_out, number["table", 1] + 1)
            sp.dma_start(table_dram, table[0:6, :]).then_inc(table_out, 16)
            sp.wait_ge(table_out, 16)
            for h in range(6):
                src = bass.AP(table_dram.tensor, h * SPAN, [[1, P], [1, T]])
                sp.dma_start(hankel[:, h, :], src).then_inc(hankel_in, 16)
            for g in range(3, len(groups)):
                load_group(g)
            sp.wait_ge(w_used, 6)
            sp.dma_start(w_a[:, :, :], io["w_branch_a"][0].rearrange("(k p) n -> p k n", p=P)).then_inc(branch_in[0], 16)
            sp.dma_start(w_router[:, :, :], io["w_router"][0].rearrange("(k p) n -> p k n", p=P)).then_inc(c_in[10], 16)
            sp.wait_ge(w_used, 7)
            sp.dma_start(ring[:, 0, :, :], w_in[:, :, GATES:GATES + 512]).then_inc(ring_in[0], 16)
            sp.wait_ge(w_used, 8)
            sp.dma_start(ring[:, 1, :, :], w_in[:, :, GATES + 512:GATES + 1024]).then_inc(ring_in[1], 16)
            with sp.Fori(0, A_PAIRS - 1) as i:
                for s in range(2):
                    sp.wait_ge(gate_done, i * UNITS + (s + 1) * NT)
                    src = w_in[:, :, bass.ds(i * 1024 + (GATES + 1024 + s * 512), 512)]
                    sp.dma_start(ring[:, s, :, :], src).then_inc(ring_in[s], 16)
            sp.wait_ge(gate_done, A_PAIRS * UNITS)
            sp.wait_ge(max_ready, A_PAIRS * UNITS)
            sp.dma_start(w_b[:, :, :], io["w_branch_b"][0].rearrange("(k p) n -> p k n", p=P)).then_inc(branch_in[1], 16)
            sp.dma_start(w_c[:, :, :], io["w_branch_c"][0].rearrange("(k p) n -> p k n", p=P)).then_inc(branch_in[2], 16)
            sp.dma_start(w_out[:, :, :], io["w_out"][0].rearrange("(k p) n -> p k n", p=P)).then_inc(branch_in[3], 16)
            sp.dma_start(ffn_gain, bcast(io["ffn_norm_g"], P, D)).then_inc(c_in[11], 16)
            sp.wait_ge(yT_done, KD)
            sp.dma_start(router_bias, bcast(io["router_bias"], P, E)).then_inc(c_in[9], 16)
            sp.dma_start(rs[:, 616:620], const["tokens"]).then_inc(c_in[9], 16)
            sp.wait_ge(mixed, KD)
            sp.dma_start(w_sup[:, :, :], io["w_shared_up"][0].rearrange("(k p) n -> p k n", p=P)).then_inc(shared_in[0], 16)
            sp.wait_ge(mix_done, 3 * KD)
            sp.dma_start(w_sdn[:, :, :], io["w_shared_down"][0].rearrange("(k p) n -> p k n", p=P)).then_inc(shared_in[1], 16)
            for t in range(NT):
                sp.wait_ge(u_ready, t + 1)
                sp.dma_start(u_dram[t * P:(t + 1) * P, :], u_tok[:, t, :]).then_inc(u_stored, 16)

            up_src = io["w_exp_up"][0].rearrange("e (k p) n -> p e k n", p=P)
            dn_src = io["w_exp_down"][0].rearrange("e (k p) (h n) -> p e k h n", p=P, n=512)

            def load_expert(e, n, u0, first=False):
                for j in range(BLOCKS):
                    if not first:
                        sp.wait_ge(low_done, u0 + (j - RAW + 1))
                    s = (BLOCKS * n + j) % RAW
                    if j < 2:
                        sp.dma_start(raw[:, s, :, :], up_src[:, e, 4 * j:4 * j + 4, :]).then_inc(raw_in[s], 16)
                    else:
                        sp.dma_start(raw[:, s, :, :].rearrange("p (k h) n -> p k (h n)", h=2),
                                     dn_src[:, e].rearrange("p k h n -> p k (h n)")).then_inc(raw_in[s], 16)

            sp.wait_ge(x1_done, 2 * NT)
            load_expert(0, 0, 0, True)
            load_expert(1, 1, 3, True)
            for t in range(NT):
                sp.wait_ge(out_ready, t + 1)
                sp.dma_start(out[0, t * P:(t + 1) * P, :], x_tok[:, t, :]).then_inc(out_stored, 16)
            load_expert(2, 2, 6)
            load_expert(3, 3, 9)
            with sp.Fori(1, E // TURN) as g:
                for n in range(TURN):
                    load_expert(g * TURN + n, n, g * (BLOCKS * TURN) + BLOCKS * n)
            sp.wait_ge(routed, 1)
            fullest = sp.value_load(most_i[0:1, 0:1], min_val=0, max_val=T)
            with sp.If(fullest > ROWS):
                with sp.Fori(1, PASSES) as r:
                    with sp.If(fullest > r * ROWS):
                        with sp.Fori(0, E // TURN) as g:
                            for n in range(TURN):
                                load_expert(g * TURN + n, n, r * (BLOCKS * E) + (g * (BLOCKS * TURN) + BLOCKS * n))

        @block.gpsimd
        def _(pool):
            pool.dma_start(gains[:, 0:8], io["attn_norm_g"][0].rearrange("(k p) -> p k", p=P),
                           allow_slow_non_contiguous=True).then_inc(c_in[1], 16)
            pool.dma_start(gains[:, 8:16], io["mem_norm_g"][0].rearrange("(k p) -> p k", p=P),
                           allow_slow_non_contiguous=True).then_inc(c_in[2], 16)
            for n, name in enumerate(("q_norm_a", "k_norm_a", "q_norm_c", "k_norm_c")):
                for half in range(2):
                    pool.dma_start(gains[half * HD:(half + 1) * HD, 16 + n:17 + n], io[name].rearrange("a p -> p a"),
                                   allow_slow_non_contiguous=True).then_inc(c_in[3], 16)
            pool.dma_start(lb[:, 0:4], io["lb_logits"].rearrange("r (b p) -> p (r b)", p=P),
                           allow_slow_non_contiguous=True).then_inc(c_in[4], 16)
            pool.dma_start(rel[0:32, :], io["rel_bias"]).then_inc(c_in[5], 16)
            pool.dma_start(bucket[0:33, :], const["bucket"]).then_inc(c_in[6], 16)
            pool.dma_start(out_norm, bcast(io["out_norm_b"], P, BV)).then_inc(c_in[7], 16)
            pool.memset(gains[:, 20:21], EPS).then_inc(c_in[8], 1)
            pool.wait_ge(c_in[8], 1)
            pool.memset(rel[32:33, :], 1.0).then_inc(c_in[8], 1)

            pool.wait_ge(y_done, (A_PAIRS + C_PAIRS) * UNITS)
            pool.wait_ge(x1_done, 1)
            pool.memset(gathered[:, :, :], 0.0).then_inc(cleared, 1)
            bound = pool.to_reg(T - 1)
            count = pool.alloc_register("experts_done")
            target = pool.alloc_register("wait_value")
            out_rows = out.rearrange("a t d -> (a t) d")

            def wait_count(semaphore, scale, plus):
                pool.reg_mul(target, count, scale) if scale != 1 else pool.reg_mov(target, count)
                pool.reg_add(target, target, plus)
                pool.wait_ge(cleared, 1)
                pool.wait_ge(semaphore, target)

            def gather(n, ahead):
                wait_count(index_ready, 1, ahead + 1)
                if ahead >= 2:
                    wait_count(gT_done, 1, ahead - 1)
                pool.indirect_dma_start(gathered[0:ROWS, n % 2, :], None, u_dram,
                                        bass.IndirectOffsetOnAxis(ap=index[0:ROWS, n % 4:n % 4 + 1], axis=0),
                                        bounds_check=bound, oob_is_err=False).then_inc(gather_in[n % 2], 16)

            def scatter(n, first=False):
                wait_count(y_ready, 1, 1)
                if not first:
                    wait_count(added, 16, 0)
                pool.indirect_dma_start(out_rows, bass.IndirectOffsetOnAxis(ap=index[0:ROWS, n % 4:n % 4 + 1], axis=0),
                                        y_out[0:ROWS, n % 2, :], None, bounds_check=bound, oob_is_err=False,
                                        compute_op=ALU.add).then_inc(added, 16)
                pool.reg_add(count, count, 1)

            def expert_pass(first):
                gather(0, 0)
                gather(1, 1)
                for n in range(TURN):
                    gather(n + 2, 2)
                    scatter(n, first and n == 0)
                with pool.Fori(1, E // TURN - 1):
                    for n in range(TURN):
                        gather(n + 2, 2)
                        scatter(n)
                for n in range(TURN):
                    if n + 2 < TURN:
                        gather(n + 2, 2)
                    scatter(n)

            pool.reg_mov(count, 0)
            pool.wait_ge(cleared, 1)
            pool.wait_ge(u_stored, 16 * NT)
            pool.wait_ge(out_stored, 16 * NT)
            expert_pass(True)
            fullest = pool.value_load(most_i[0:1, 0:1], min_val=0, max_val=T)
            pool.wait_ge(added, 16 * E)
            with pool.If(fullest > ROWS):
                with pool.Fori(1, PASSES) as r:
                    with pool.If(fullest > r * ROWS):
                        expert_pass(False)
                        wait_count(added, 16, 0)

        @block.scalar
        def _(act):
            def copy(o, i, **kw):
                return nc.scalar.activation(o, i, ACT.Copy, **kw)

            act.wait_ge(c_in[8], 2)
            for t in range(NT):
                act.wait_ge(x_in[t], 16)
                nc.scalar.activation(xn[:, t, :], x_tok[:, t, :], ACT.Square,
                                     accum_out=small[:, t:t + 1]).then_inc(x_squared, 1)
            act.wait_ge(x_squared, NT)
            nc.scalar.activation(small[:, 6:10], small[:, 0:4], ACT.Sqrt, bias=gains[:, 20:21],
                                 scale=1.0 / D).then_inc(x_rooted, 1)
            act.wait_ge(mem_in, 16)
            for t in range(NM):
                nc.scalar.activation(memT[:, 0:4, :].rearrange("p a b -> p (a b)") if t == 0 else
                                     memT[:, 4:8, :].rearrange("p a b -> p (a b)"), mem[:, t, :], ACT.Square,
                                     accum_out=small[:, 4 + t:5 + t]).then_inc(x_squared, 1)
            act.wait_ge(x_squared, NT + NM)
            nc.scalar.activation(small[:, 10:12], small[:, 4:6], ACT.Sqrt, bias=gains[:, 20:21],
                                 scale=1.0 / D).then_inc(x_rooted, 1)
            act.wait_ge(lb_in_exp, 1)
            nc.scalar.activation(lb[:, 0:4], lb[:, 0:4], ACT.Exp).then_inc(lb_exp, 1)

            def exponents(j):
                if j <= LEVELS:
                    act.wait_ge(diff_ready, j + 1)
                e = expo[j % 2]
                if j < LEVELS:
                    m = 1 << (LEVELS - 1 - j)
                    v = e.rearrange("p b (n m) -> p (b n) m", m=2 * m)
                    nc.scalar.activation(v[:, :, 0:m], v[:, :, 0:m], ACT.Exp, scale=-1.0).then_inc(expo_ready, 1)
                    nc.scalar.activation(v[:, :, m:2 * m], v[:, :, m:2 * m], ACT.Exp).then_inc(expo_ready, 1)
                elif j == LEVELS:
                    nc.scalar.activation(e, e, ACT.Exp, scale=-1.0).then_inc(expo_ready, 2)
                else:
                    act.wait_ge(kq_ready, j - 1)
                    nc.scalar.activation(e, bT[:, :, :], ACT.Exp).then_inc(expo_ready, 2)

            def forget_gate():
                act.wait_ge(unit_out, number["qf", 3] + 1)
                nc.scalar.activation(expo[0][:, :, :], fT[:, :, :], ACT.Exp, scale=-1.0).then_inc(f_exp, 1)
                act.wait_ge(unit_out, number["qf", 1] + 1)
                nc.scalar.activation(expo[1][:, :, :], qT[:, :, :], ACT.Tanh, scale=0.5).then_inc(q_tanh, 1)
                act.wait_ge(f_ready, 1)
                nc.scalar.activation(fT[:, :, :], fT[:, :, :], ACT.Ln).then_inc(log_ready, 1)

            def roots_a():
                act.wait_ge(qk_summed, 2)
                nc.scalar.activation(small[:, 68:116], small[:, 20:68], ACT.Sqrt, bias=gains[:, 20:21],
                                     scale=1.0 / HD).then_inc(qk_rooted, 1)

            between = {("qa", 0): [forget_gate], ("va", 1): [roots_a]}
            for j, unit in enumerate((("ka", 2), ("bias", 3), ("va", 3), ("ib", 3), ("og", 3), ("memT", 6), ("kv", 0),
                                      ("qc", 1), ("qc", 3))):
                between[unit] = [lambda j=j: exponents(j)]
            act.wait_ge(c_in[1], 16)
            act.wait_ge(c_in[2], 16)
            for n, (kind, k) in enumerate(units):
                for extra in between.get((kind, k), ()):
                    extra()
                bank = ps[n % 4]
                if kind == "ib" and k == 0:
                    act.wait_ge(qk_summed, 2)
                act.wait_ge(unit_done, n + 1)
                if kind == "hT":
                    ins = copy(hT[:, k, :], bank[:, :], scale=gains[:, k:k + 1])
                elif kind == "memT":
                    ins = copy(memT[:, k, :], bank[:, 0:M], scale=gains[:, 8 + k:9 + k])
                elif kind == "table":
                    ins = copy(table[0:6, k * T:min(SPAN, (k + 1) * T)], bank[0:6, 0:min(T, SPAN - k * T)])
                elif kind == "qf":
                    ins = copy((qT, fT)[k // 2][:, k % 2, :], bank[:, :])
                elif kind == "bias":
                    ins = copy(bias[:, k, :], bank[:, :])
                elif kind == "kv":
                    ins = copy(kv[:, k, :], bank[:, :])
                elif kind == "kdT":
                    ins = copy(kdT[:, k, :], bank[:, 0:3 * P])
                elif kind == "o":
                    ins = copy(o_tok[:, k, :], bank[:, 0:BV])
                else:
                    dst, width = token_major[kind]
                    ins = copy(dst[:, k, :], bank[:, 0:width])
                ins.then_inc(unit_out, 1)

            act.wait_ge(state_ready, 6)
            act.wait_ge(unit_out, len(units))
            nc.scalar.activation(o_gate[:, :, :], og[:, :, :], ACT.Tanh, scale=0.5).then_inc(og_tanh, 1)
            act.wait_ge(o_summed, 1)
            nc.scalar.activation(small[:, 180:196], small[:, 164:180], ACT.Sqrt, bias=gains[:, 20:21],
                                 scale=1.0 / VD).then_inc(o_rooted, 1)
            act.wait_ge(c_summed, 2)
            nc.scalar.activation(small[:, 236:260], small[:, 212:236], ACT.Sqrt, bias=gains[:, 20:21],
                                 scale=1.0 / HD).then_inc(c_rooted, 1)

            def attention(i, dilated):
                pairs = 0 if dilated else A_PAIRS
                n0 = i * UNITS + pairs * UNITS
                act.wait_ge(pair_done, i + (pairs + 1))
                copy(qkT[:, 0, :], ps[0][:, :], scale=gains[:, (16 if dilated else 18):(17 if dilated else 19)]).then_inc(pair_out, 1)
                width = T if dilated else M
                copy(qkT[:, 1, 0:width], ps[1][:, 0:width], scale=gains[:, (17 if dilated else 19):(18 if dilated else 20)]).then_inc(pair_out, 1)

                def exponential(j):
                    keys = (j % NT + 1) * P if dilated else M
                    act.wait_ge(max_ready, n0 + (j + 1))
                    src = logits[:, j % 2, 0:keys] if dilated else ps[2 + j % 2][:, 0:keys]
                    nc.scalar.activation(probs[:, j % 2, 0:keys], src, ACT.Exp, bias=small[:, 284 + j % 2:285 + j % 2],
                                         accum_out=small[:, 288 + j % 2:289 + j % 2]).then_inc(exp_done, 1)

                def gate(j):
                    if dilated:
                        act.wait_ge(gate_done, n0 + (j + 1))
                        nc.scalar.activation(ps[6 + j % 2][:, :], ps[6 + j % 2][:, :], ACT.Tanh, scale=0.5).then_inc(gate_tanh, 1)

                gate(0)
                exponential(0)
                for j in range(UNITS):
                    if j + 1 < UNITS:
                        exponential(j + 1)
                        gate(j + 1)
                    keys = (j % NT + 1) * P if dilated else M
                    act.wait_ge(pT_done, n0 + (j + 1))
                    copy(probsT[:, j % 2, 0:keys], ps[4][:, 0:keys]).then_inc(pT_out, 1)

            with act.Fori(0, A_PAIRS) as i:
                attention(i, True)
            with act.Fori(0, C_PAIRS) as i:
                attention(i, False)

            for k in range(KD):
                act.wait_ge(yT_done, k + 1)
                copy(yT[:, k, :], ps[k % 4][:, :]).then_inc(yT_out, 1)

            for t in range(NT):
                act.wait_ge(x1_ready, 2 * t + 2)
                nc.scalar.activation(u_tok[:, t, :], x_tok[:, t, :], ACT.Square,
                                     accum_out=small[:, t:t + 1]).then_inc(x1_squared, 1)
                act.wait_ge(x1_squared, t + 1)
                nc.scalar.activation(small[:, 6 + t:7 + t], small[:, t:t + 1], ACT.Sqrt, bias=gains[:, 20:21],
                                     scale=1.0 / D).then_inc(x1_rooted, 1)
            for t in range(NT):
                act.wait_ge(uT_done, t + 1)
                for half in range(2):
                    copy(uT[:, 4 * half:4 * half + 4, t * P:(t + 1) * P],
                         view(ps[2 * (t % 2) + half][:, :], 4, P)).then_inc(uT_out, 1)
            act.wait_ge(r_done, 1)
            nc.scalar.activation(view(ps[4][:, 0:NT * E], NT, E), view(ps[4][:, 0:NT * E], NT, E), ACT.Tanh, scale=0.5).then_inc(r_tanh, 1)
            for t in range(NT):
                act.wait_ge(s_up, t + 1)
                nc.scalar.activation(s_tanh[:, t % 2, :], ps[t % 2][:, 0:FH], ACT.Tanh, scale=0.5).then_inc(s_tanhed, 1)
                act.wait_ge(s_hidT_done, t + 1)
                copy(s_hidT[:, t % 2, :, :], view(ps[5][:, 0:2 * P], 2, P)).then_inc(s_hidT_out, 1)

            def high(n, j, u, round0):
                q = BLOCKS * n + j
                if isinstance(u, int) and u < SPLIT:
                    free = ((x1_done, 2 * NT), (u_stored, 16 * NT), (s_up, NT), (out_stored, 16 * NT))[u]
                    act.wait_ge(*free)
                    if u == 1:
                        act.wait_ge(uT_done, NT)
                else:
                    act.wait_ge(block_used, u - (SPLIT - 1))
                act.wait_ge(raw_in[q % RAW], round0 * 16 + 16 * (q // RAW + 1))
                copy(split[q % SPLIT][:, 0], raw[:, q % RAW]).then_inc(high_done, 1)

            def high_tokens(n, m):
                act.wait_ge(gT_done, m + 1)
                for half in range(2):
                    copy(gatheredT[:, n % 2, 0, 4 * half:4 * half + 4, :],
                         view(ps[half][:, 0:4 * ROWS], 4, ROWS)).then_inc(gT_high, 1)

            def expert(n, m, u, round0, more):
                if more:
                    high(n + 1, 0, u + 3, round0)
                    high(n + 1, 1, u + 4, round0)
                act.wait_ge(block_used, u + 2)
                nc.scalar.activation(e_tanh[0:ROWS, n % 2, :], ps[2][0:ROWS, 0:FH], ACT.Tanh, scale=0.5).then_inc(tanh_done, 1)
                act.wait_ge(hidT_done, m + 1)
                copy(hidT[:, n % 2, 0, :], ps[3][:, 0:2 * ROWS]).then_inc(hidT_high, 1)
                if more:
                    high_tokens(n + 1, m + 1)
                    high(n + 1, 2, u + 5, round0)
                act.wait_ge(block_used, u + 3)
                if not isinstance(m, int) or m >= 2:
                    act.wait_ge(added, m * 16 - 16)
                copy(y_out[0:ROWS, n % 2, 0:512], ps[4][0:ROWS, :])
                copy(y_out[0:ROWS, n % 2, 512:1024], ps[6][0:ROWS, :]).then_inc(y_ready, 1)

            def expert_pass(m0, u0, rounds):
                for j in range(BLOCKS):
                    high(0, j, u0 + j, rounds)
                high_tokens(0, m0)
                for n in range(TURN):
                    expert(n, m0 + n, u0 + BLOCKS * n, rounds, True)
                with act.Fori(1, E // TURN - 1) as g:
                    for n in range(TURN):
                        expert(n, m0 + (g * TURN + n), u0 + (g * (BLOCKS * TURN) + BLOCKS * n), rounds + g * 2, True)
                last = E - TURN
                for n in range(TURN):
                    expert(n, m0 + (last + n), u0 + BLOCKS * (last + n), rounds + last // 2, n + 1 < TURN)

            expert_pass(0, 0, 0)
            fullest = act.value_load(most_i[0:1, 0:1], min_val=0, max_val=T)
            with act.If(fullest > ROWS):
                with act.Fori(1, PASSES) as r:
                    with act.If(fullest > r * ROWS):
                        expert_pass(r * E, r * (BLOCKS * E), r * (E // 2))

        @block.vector
        def _(dve):
            v = nc.vector
            steps = [0]

            def then(ins):
                steps[0] += 1
                ins.then_inc(v_step, 1)
                dve.wait_ge(v_step, steps[0])

            dve.wait_ge(x_rooted, 1)
            then(v.reciprocal(small[:, 12:16], small[:, 6:10]))
            for t in range(NT):
                v.tensor_scalar(xn[:, t, :], x_tok[:, t, :], small[:, 12 + t:13 + t], None, ALU.mult).then_inc(x_normed, 1)
            dve.wait_ge(x_rooted, 2)
            then(v.reciprocal(small[:, 16:18], small[:, 10:12]))
            for t in range(NM):
                v.tensor_scalar(mem[:, t, :], mem[:, t, :], small[:, 16 + t:17 + t], None, ALU.mult).then_inc(mem_normed, 1)
            dve.wait_ge(c_in[3], 16 * 8)
            for column in (16, 18):
                then(v.tensor_scalar(gains[:, column:column + 1], gains[:, column:column + 1], HD ** -0.5, None, ALU.mult))
            dve.wait_ge(c_in[4], 16)
            then(v.tensor_tensor(lb[:, 4:6], lb[:, 0:2], lb[:, 2:4], ALU.max))
            then(v.tensor_tensor(lb[:, 0:2], lb[:, 0:2], lb[:, 4:6], ALU.subtract))
            v.tensor_tensor(lb[:, 2:4], lb[:, 2:4], lb[:, 4:6], ALU.subtract).then_inc(lb_in_exp, 1)
            dve.wait_ge(lb_exp, 1)
            then(v.tensor_tensor(lb[:, 4:6], lb[:, 0:2], lb[:, 2:4], ALU.add))
            then(v.reciprocal(lb[:, 6:8], lb[:, 4:6]))
            then(v.tensor_tensor(lb[:, 4:6], lb[:, 0:2], lb[:, 6:8], ALU.mult))
            then(v.tensor_scalar(lb[:, 6:8], lb[:, 4:6], -1.0, 1.0, ALU.mult, ALU.add))
            dve.wait_ge(f_exp, 1)
            then(v.tensor_scalar(expo[0][:, :, :], expo[0][:, :, :], 1.0, None, ALU.add))
            then(v.reciprocal(kT[:, :, :], expo[0][:, :, :]))
            for b in range(2):
                ins = v.tensor_scalar(fT[:, b, :], kT[:, b, :], lb[:, 6 + b:7 + b], lb[:, 4 + b:5 + b], ALU.mult, ALU.add)
                then(ins)
            then(v.tensor_scalar(kT[:, :, :], fT[:, :, :], -1.0, 1.0, ALU.mult, ALU.add))
            v.tensor_copy(small[:, 310:311], small[:, 0:1]).then_inc(f_ready, 1)
            dve.wait_ge(q_tanh, 1)
            then(v.scalar_tensor_tensor(qT[:, :, :], expo[1][:, :, :], 1.0, qT[:, :, :], ALU.add, ALU.mult))
            then(v.tensor_scalar(qT[:, :, :], qT[:, :, :], 0.5 * HD ** -0.5, None, ALU.mult))
            dve.wait_ge(log_ready, 1)
            dve.wait_ge(c_in[0], 16)
            for b in range(2):
                for c in range(NT):
                    last = v.tensor_tensor_scan(bT[:, b, c * P:(c + 1) * P], ones, fT[:, b, c * P:(c + 1) * P],
                                                0.0, ALU.mult, ALU.add)
            then(last)

            def differences(j):
                m = 1 << (LEVELS - 1 - j) if j < LEVELS else P // 2
                ref = m - 1 if j < LEVELS else P - 1
                b_v = bT.rearrange("p b (n m) -> p (b n) m", m=2 * m)
                e_v = expo[j % 2].rearrange("p b (n m) -> p (b n) m", m=2 * m)
                n = 2 * T // (2 * m)
                v.tensor_tensor(e_v, b_v, bcast(b_v[:, :, ref:ref + 1], P, n, 2 * m), ALU.subtract).then_inc(diff_ready, 1)

            def products(j):
                dve.wait_ge(expo_ready, 2 * (j + 1))
                if 2 <= j < LEVELS + 1:
                    dve.wait_ge(level_done, 4 * (j - 1))
                elif j == LEVELS + 1:
                    dve.wait_ge(level_done, 4 * (j - 2))
                if j < LEVELS:
                    m = 1 << (LEVELS - 1 - j)
                    e_v, o_v, k_v, q_v = (a.rearrange("p b (n m) -> p (b n) m", m=2 * m) for a in (expo[j % 2], kq[j % 2], kT, qT))
                    then(v.tensor_tensor(o_v[:, :, 0:m], e_v[:, :, 0:m], k_v[:, :, 0:m], ALU.mult))
                    v.tensor_tensor(o_v[:, :, m:2 * m], e_v[:, :, m:2 * m], q_v[:, :, m:2 * m], ALU.mult).then_inc(kq_ready, 1)
                else:
                    v.tensor_tensor(kq[j % 2][:, :, :], expo[j % 2][:, :, :], (kT if j == LEVELS else qT)[:, :, :],
                                    ALU.mult).then_inc(kq_ready, 1)

            def take_level(j):
                if j > 0:
                    reach = 1 << (LEVELS - j)
                    then(v.tensor_scalar(mask[:, j % 2, :].bitcast(I32), level, float(reach), None, ALU.is_lt))
                for c in range(NT):
                    dve.wait_ge(level_done, 4 * j + c + 1)
                    src = view(ps[4 + c][:, :], 4, P)
                    if j == 0:
                        v.scalar_tensor_tensor(scores[:, 4 * c:4 * c + 4, :], bcast(level[:, None, :], P, 4, P), float(P), src,
                                               ALU.is_lt, ALU.mult).then_inc(level_taken, 1)
                    else:
                        m_v = mask[:, j % 2, :].bitcast(I32)
                        v.copy_predicated(scores[:, 4 * c:4 * c + 4, :], bcast(m_v[:, None, :], P, 4, P), src).then_inc(level_taken, 1)
                dve.wait_ge(level_taken, 4 * (j + 1))

            differences(0)
            differences(1)
            products(0)
            for n, (a, name) in enumerate(((qa, "qa"), (ka, "ka"))):
                dve.wait_ge(unit_out, number[name, NT - 1] + 1)
                then(v.tensor_tensor(squares[:, n, :, :], a[:, :, :], a[:, :, :], ALU.mult))
                v.tensor_reduce(small[:, 20 + 24 * n:44 + 24 * n], squares[:, n, :, :].rearrange("p t (h e) -> p (t h) e", e=HD),
                                AX.X, ALU.add).then_inc(qk_summed, 1)
            dve.wait_ge(unit_out, number["bias", 5] + 1)
            then(v.memset(state[:, :, :, :], 0.0))
            for j in range(LEVELS + 1):
                if j + 1 <= LEVELS + 1:
                    products(j + 1)
                if j + 2 <= LEVELS:
                    differences(j + 2)
                take_level(j)
                if j == 0:
                    dve.wait_ge(qk_rooted, 1)
                    then(v.reciprocal(small[:, 116:164], small[:, 68:116]))
            for c in range(NT - 1):
                dve.wait_ge(inc_done, c + 1)
                for b in range(2):
                    for hh in range(2):
                        rows = slice(hh * HD, (hh + 1) * HD)
                        col = b * 2 * VD + hh * VD
                        inc = ps[4 + c][rows, col:col + VD]
                        cols = slice(hh * VD, (hh + 1) * VD)
                        if c == 0:
                            ins = v.tensor_copy(state[rows, 0, b, cols], inc)
                        else:
                            ins = v.scalar_tensor_tensor(state[rows, c, b, cols], state[rows, c - 1, b, cols],
                                                         expo[(LEVELS + 1) % 2][rows, b, c * P + P - 1:c * P + P], inc,
                                                         ALU.mult, ALU.add)
                        if hh == 0:
                            then(ins)
                        else:
                            ins.then_inc(state_ready, 1)
                dve.wait_ge(state_ready, 2 * (c + 1))
            dve.wait_ge(unit_out, len(units))
            then(v.tensor_tensor(o_sq[:, :, :], o_tok[:, :, :], o_tok[:, :, :], ALU.mult))
            v.tensor_reduce(small[:, 164:180], o_sq.rearrange("p t (h e) -> p (t h) e", e=VD), AX.X, ALU.add).then_inc(o_summed, 1)
            q_sq, k_sq = view(c_sq[:, 0:1024], NT, CW), view(c_sq[:, 1024:1536], NM, CW)
            then(v.tensor_tensor(q_sq, qc[:, :, :], qc[:, :, :], ALU.mult))
            v.tensor_reduce(small[:, 212:228], q_sq.rearrange("p t (h e) -> p (t h) e", e=HD), AX.X, ALU.add).then_inc(c_summed, 1)
            then(v.tensor_tensor(k_sq, kv[:, :, 0:CW], kv[:, :, 0:CW], ALU.mult))
            v.tensor_reduce(small[:, 228:236], k_sq.rearrange("p t (h e) -> p (t h) e", e=HD), AX.X, ALU.add).then_inc(c_summed, 1)
            dve.wait_ge(o_rooted, 1)
            then(v.reciprocal(small[:, 196:212], small[:, 180:196]))
            o_v = o_tok.rearrange("p t (h e) -> p (t h) e", e=VD)
            then(v.tensor_tensor(o_v, o_v, bcast(small[:, 196:212, None], P, 16, VD), ALU.mult))
            dve.wait_ge(c_in[7], 16)
            then(v.tensor_tensor(o_tok[:, :, :], o_tok[:, :, :], bcast(out_norm[:, None, :], P, NT, BV), ALU.mult))
            dve.wait_ge(og_tanh, 1)
            then(v.scalar_tensor_tensor(o_gate[:, :, :], o_gate[:, :, :], 1.0, og[:, :, :], ALU.add, ALU.mult))
            then(v.scalar_tensor_tensor(ib[:, :, :], o_tok[:, :, :], 0.5, o_gate[:, :, :], ALU.mult, ALU.mult))
            dve.wait_ge(c_rooted, 1)
            then(v.reciprocal(small[:, 260:284], small[:, 236:260]))

            loop_steps = [0, 0]

            def attention(i, dilated, base):
                pairs = 0 if dilated else A_PAIRS
                n0 = i * UNITS + pairs * UNITS
                k = [0]

                def then(ins):
                    k[0] += 1
                    ins.then_inc(v_step, 1)
                    dve.wait_ge(v_step, base + k[0])

                q_src, k_src = (qa, ka) if dilated else (qc, kv)
                heads = 6 if dilated else 4
                roots = [(small[:, 116:140], small[:, 140:164]), (small[:, 260:276], small[:, 276:284])][not dilated]
                for which, (src, root) in enumerate(zip((q_src, k_src), roots)):
                    tiles = NM if which and not dilated else NT
                    o_v = staging[:, which, 0:tiles, :].rearrange("p t (h e) -> p t h e", e=HD)
                    for t in range(tiles):
                        s_v = src[:, t, bass.ds(i * P, P)].rearrange("p (h e) -> p h e", e=HD)
                        r_v = root[:, bass.ds(i * 2 + t * heads, 2)]
                        v.tensor_tensor(o_v[:, t], s_v, bcast(r_v.unsqueeze(2), P, 2, HD), ALU.mult).then_inc(staged, 1)

                def maximum(j):
                    keys = (j % NT + 1) * P if dilated else M
                    dve.wait_ge(qk_done, n0 + (j + 1))
                    src = ps[2 + j % 2][:, 0:keys]
                    if dilated:
                        start = (NT - 1 - j % NT) * P
                        table_h = bias[:, bass.ds(i * 2 + j // NT, 1), start:T].rearrange("p a b -> p (a b)")
                        then(v.tensor_tensor(logits[:, j % 2, 0:keys], src, table_h, ALU.add))
                        src = logits[:, j % 2, 0:keys]
                    v.tensor_reduce(small[:, 284 + j % 2:285 + j % 2], src, AX.X, ALU.max, negate=True).then_inc(max_ready, 1)

                def gate(j):
                    if dilated:
                        dve.wait_ge(gate_tanh, n0 + (j + 1))
                        v.tensor_scalar(gates[:, bass.ds(i * UNITS + j, 1), :].rearrange("p a b -> p (a b)"),
                                        ps[6 + j % 2][:, :], 0.5, 0.5, ALU.mult, ALU.add).then_inc(gate_out, 1)

                gate(0)
                maximum(0)
                for j in range(UNITS):
                    if j + 1 < UNITS:
                        maximum(j + 1)
                        gate(j + 1)
                    dve.wait_ge(exp_done, n0 + (j + 1))
                    then(v.reciprocal(small[:, 292 + j % 2:293 + j % 2], small[:, 288 + j % 2:289 + j % 2]))
                    dve.wait_ge(pv_done, n0 + (j + 1))
                    dst = q_src[:, j % NT, bass.ds(i * P + (j // NT) * HD, HD)]
                    v.tensor_scalar(dst, ps[j % 2][:, 0:HD], small[:, 292 + j % 2:293 + j % 2], None,
                                    ALU.mult).then_inc(y_done, 1)
                return k[0]

            a_turn, c_turn = 2 * UNITS, UNITS
            with dve.Fori(0, A_PAIRS) as i:
                assert attention(i, True, i * a_turn + steps[0]) == a_turn
            steps[0] += A_PAIRS * a_turn
            with dve.Fori(0, C_PAIRS) as i:
                assert attention(i, False, i * c_turn + steps[0]) == c_turn
            steps[0] += C_PAIRS * c_turn

            for m in range(KD):
                for br in range(3):
                    n = 3 * m + br
                    dve.wait_ge(mix_done, n + 1)
                    g = gates[:, br * KD + m, :]
                    v.tensor_tensor(g, g, ps[4 + n % 4][:, :], ALU.mult).then_inc(mix_taken, 1)
                dve.wait_ge(mix_taken, 3 * m + 3)
                then(v.tensor_tensor(gates[:, m, :], gates[:, m, :], gates[:, KD + m, :], ALU.add))
                v.tensor_tensor(gates[:, m, :], gates[:, m, :], gates[:, 2 * KD + m, :], ALU.add).then_inc(mixed, 1)
            for n in range(2 * NT):
                t, half = n // 2, n % 2
                dve.wait_ge(x1_done, n + 1)
                x_v = x_tok[:, t, half * 512:(half + 1) * 512]
                v.tensor_tensor(x_v, x_v, ps[n % 4][:, :], ALU.add).then_inc(x1_ready, 1)
            dve.wait_ge(c_in[11], 16)
            for t in range(NT):
                dve.wait_ge(x1_rooted, t + 1)
                then(v.reciprocal(small[:, 12 + t:13 + t], small[:, 6 + t:7 + t]))
                v.scalar_tensor_tensor(u_tok[:, t, :], x_tok[:, t, :], small[:, 12 + t:13 + t], ffn_gain, ALU.mult,
                                       ALU.mult).then_inc(u_ready, 1)

            def shared(t):
                dve.wait_ge(s_tanhed, t + 1)
                then(v.scalar_tensor_tensor(s_tanh[:, t % 2, :], s_tanh[:, t % 2, :], 1.0, ps[t % 2][:, 0:FH], ALU.add, ALU.mult))
                v.scalar_tensor_tensor(s_hid[:, t % 2, :], s_tanh[:, t % 2, :], 0.5, ps[t % 2][:, FH:2 * FH], ALU.mult,
                                       ALU.mult).then_inc(s_hidden, 1)
                for half in range(2):
                    dve.wait_ge(s_down, 2 * t + half + 1)
                    x_v = x_tok[:, t, half * 512:(half + 1) * 512]
                    ins = v.tensor_tensor(x_v, x_v, ps[2 + half][:, :], ALU.add)
                    if half:
                        ins.then_inc(out_ready, 1)
                    else:
                        then(ins)

            dve.wait_ge(r_tanh, 1)
            dve.wait_ge(c_in[9], 32)
            r_ps = view(ps[4][:, 0:NT * E], NT, E)
            then(v.tensor_scalar(score, r_ps, 0.5, 0.5, ALU.mult, ALU.add))
            then(v.tensor_tensor(choice, score, bcast(router_bias[:, None, :], P, NT, E), ALU.add))
            best = view(rs[:, 0:256], NT * GROUPS, 8)
            for n in range(NT * GROUPS):
                t, g = divmod(n, GROUPS)
                last = v.max(best[:, n, :], choice[:, t, g * 8:(g + 1) * 8])
            then(last)
            group_score = view(rs[:, 256:288], NT, GROUPS)
            then(v.tensor_tensor(rs[:, 256:288], best[:, :, 0:1].rearrange("p n a -> p (n a)"),
                                 best[:, :, 1:2].rearrange("p n a -> p (n a)"), ALU.add))
            group_top, group_at = view(rs[:, 288:320], NT, 8), view(rs[:, 320:352], NT, 8)
            for t in range(NT):
                last = v.max(group_top[:, t, :], group_score[:, t, :])
            then(last)
            for t in range(NT):
                last = v.max_index(group_at[:, t, :].bitcast(U32), group_top[:, t, :], group_score[:, t, :])
            then(last)
            group_f = view(rs[:, 352:384], NT, 8)
            then(v.tensor_copy(rs[:, 352:384], rs[:, 320:352].bitcast(U32)))
            group_hit = view(rs[:, 384:512], NT, GROUPS, TOP_GROUPS)
            for t in range(NT):
                last = v.tensor_tensor(group_hit[:, t], bcast(counting[:, 0:GROUPS, None], P, GROUPS, TOP_GROUPS),
                                       bcast(group_f[:, t, None, 0:TOP_GROUPS], P, GROUPS, TOP_GROUPS), ALU.is_equal)
            then(last)
            group_mask = view(rs[:, 512:544], NT, GROUPS)
            then(v.tensor_reduce(rs[:, 512:544], group_hit.rearrange("p t g k -> p (t g) k"), AX.X, ALU.add))
            then(v.tensor_scalar(rs[:, 544:576], rs[:, 512:544], -MASKED, MASKED, ALU.mult, ALU.add))
            m_v, c_v = (a.rearrange("p t (g k) -> p (t g) k", k=8) for a in (masked, choice))
            then(v.tensor_tensor(m_v, c_v, bcast(rs[:, 512:544, None], P, 32, 8), ALU.mult))
            then(v.tensor_tensor(m_v, m_v, bcast(rs[:, 544:576, None], P, 32, 8), ALU.add))
            top8 = view(rs[:, 576:608], NT, 8)
            for t in range(NT):
                last = v.max(top8[:, t, :], masked[:, t, :])
            then(last)
            for t in range(NT):
                last = v.match_replace(masked2[:, t, :], top8[:, t, :], masked[:, t, :], 3 * MASKED)
            then(last)
            v.tensor_scalar(picked, masked2, 2 * MASKED, None, ALU.is_lt).then_inc(picked_ready, 1)
            dve.wait_ge(picked_ready, 1)
            then(v.tensor_tensor(weight, score, picked, ALU.mult))
            then(v.tensor_reduce(rs[:, 608:612], weight, AX.X, ALU.add))
            then(v.reciprocal(rs[:, 612:616], rs[:, 608:612]))
            then(v.tensor_scalar(rs[:, 612:616], rs[:, 612:616], ROUTED_SCALE, None, ALU.mult))
            then(v.memset(route_in.bitcast(F32), 0.0))
            for t in range(NT):
                v.tensor_scalar(route_in[:, t, :, 0], picked[:, t, :], 0.0, rs[:, 616 + t:617 + t], ALU.mult, ALU.add)
                last = v.tensor_scalar(weight[:, t, :], weight[:, t, :], rs[:, 612 + t:613 + t], 0.5, ALU.mult, ALU.mult)
            then(last)
            then(v.tensor_copy(route_in[:, :, :, 1], weight))
            then(v.tensor_tensor(route_in[:, :, :, 2], weight, route_in[:, :, :, 1].bitcast(F32), ALU.subtract))
            dve.wait_ge(place_done, 1)
            p_v = view(ps[4][:, 256:256 + NT * E], NT, E)
            then(v.scalar_tensor_tensor(place, p_v, 1.0, picked, ALU.add, ALU.mult))
            then(v.tensor_scalar(place, place, -1.0, None, ALU.add))
            then(v.tensor_reduce(most, ps[5][:, 256:256 + E], AX.X, ALU.max))
            v.tensor_copy(most_i, most).then_inc(routed, 1)
            for t in range(NT):
                shared(t)

            def low(n, j, u):
                q = BLOCKS * n + j
                dve.wait_ge(high_done, u + 1)
                both = split[q % SPLIT]
                v.tensor_tensor(both[:, 1], raw[:, q % RAW], both[:, 0].bitcast(F32), ALU.subtract).then_inc(low_done, 1)

            def low_tokens(n, m):
                for half in range(2):
                    dve.wait_ge(gT_high, m * 2 + half + 1)
                    parts = gatheredT[:, n % 2, :, 4 * half:4 * half + 4, :]
                    v.tensor_tensor(parts[:, 1], view(ps[half][:, 0:4 * ROWS], 4, ROWS), parts[:, 0].bitcast(F32),
                                    ALU.subtract).then_inc(gT_low, 1)

            def read_route(n, m):
                dve.wait_ge(route_done, m + 1)
                if not isinstance(m, int) or m >= 4:
                    dve.wait_ge(added, m * 16 - 48)
                v.tensor_reduce(slot_w[0:ROWS, n % 4:n % 4 + 1], ps[7][0:ROWS, 1:3], AX.X, ALU.add)
                v.tensor_scalar(index[0:ROWS, n % 4:n % 4 + 1], ps[7][0:ROWS, 0:1], NO_TOKEN, None,
                                ALU.add).then_inc(index_ready, 1)

            def choose(n, m, e):
                if not isinstance(m, int) or m >= 2:
                    dve.wait_ge(route_done, m - 1)
                v.tensor_tensor(select[:, n % 2, :, :], bcast(counting[:, None, 0:ROWS], P, NT, ROWS),
                                bcast(place[:, :, bass.ds(e, 1)], P, NT, ROWS), ALU.is_equal).then_inc(sel_ready, 1)

            def expert(n, m, e, u, more, more2, more3):
                if more:
                    low(n + 1, 0, u + 3)
                dve.wait_ge(tanh_done, m + 1)
                v.scalar_tensor_tensor(e_act[0:ROWS, n % 2, :], e_tanh[0:ROWS, n % 2, :], 1.0, ps[2][0:ROWS, 0:FH], ALU.add,
                                       ALU.mult).then_inc(act_ready, 1)
                dve.wait_ge(act_ready, m + 1)
                v.scalar_tensor_tensor(hid[0:ROWS, n % 2, :], e_act[0:ROWS, n % 2, :], slot_w[0:ROWS, n % 4:n % 4 + 1],
                                       ps[2][0:ROWS, FH:2 * FH], ALU.mult, ALU.mult).then_inc(hid_ready, 1)
                dve.wait_ge(hidT_high, m + 1)
                parts = hidT[:, n % 2, :, :]
                v.tensor_tensor(parts[:, 1], ps[3][:, 0:2 * ROWS], parts[:, 0].bitcast(F32), ALU.subtract).then_inc(hidT_low, 1)
                if more:
                    low_tokens(n + 1, m + 1)
                    low(n + 1, 1, u + 4)
                if more2:
                    read_route(n + 2, m + 2)
                if more3:
                    choose(n + 3, m + 3, e + 3)
                if more:
                    low(n + 1, 2, u + 5)

            def expert_pass(m0, u0):
                choose(0, m0, 0)
                choose(1, m0 + 1, 1)
                read_route(0, m0)
                read_route(1, m0 + 1)
                choose(2, m0 + 2, 2)
                for j in range(BLOCKS):
                    low(0, j, u0 + j)
                low_tokens(0, m0)
                for n in range(TURN):
                    expert(n, m0 + n, n, u0 + BLOCKS * n, True, True, True)
                with dve.Fori(1, E // TURN - 1) as g:
                    for n in range(TURN):
                        expert(n, m0 + (g * TURN + n), g * TURN + n, u0 + (g * (BLOCKS * TURN) + BLOCKS * n), True, True, True)
                last = E - TURN
                for n in range(TURN):
                    expert(n, m0 + (last + n), last + n, u0 + BLOCKS * (last + n), n + 1 < TURN, n + 2 < TURN, n + 3 < TURN)

            expert_pass(0, 0)
            fullest = dve.value_load(most_i[0:1, 0:1], min_val=0, max_val=T)
            with dve.If(fullest > ROWS):
                with dve.Fori(1, PASSES) as r:
                    with dve.If(fullest > r * ROWS):
                        v.tensor_scalar(place, place, -float(ROWS), None, ALU.add).then_inc(v_step, 1)
                        dve.wait_ge(v_step, r + steps[0])
                        expert_pass(r * E, r * (BLOCKS * E))

        @block.tensor
        def _(pe):
            mm = nc.tensor.matmul
            tr = nc.tensor.transpose
            pe.wait_ge(c_in[0], 16)
            pe.wait_ge(c_in[5], 16)
            pe.wait_ge(c_in[6], 16)
            pe.wait_ge(c_in[8], 2)
            n = 0
            for kind, k in plan:
                if kind == "level":
                    left, right = (kT, qT) if k == LEVELS else (kq[k % 2], kq[k % 2])
                    if k < LEVELS:
                        pe.wait_ge(kq_ready, k + 1)
                    for q in range(4):
                        if k > 0:
                            pe.wait_ge(level_taken, 4 * (k - 1) + q + 1)
                        rows = slice(q % 2 * HD, (q % 2 + 1) * HD)
                        for z in range(4):
                            b, c = z % 2, q // 2 * 2 + z // 2
                            last = mm(ps[4 + q][:, z * P:(z + 1) * P], left[rows, b, c * P:(c + 1) * P],
                                      right[rows, b, c * P:(c + 1) * P], start=True, stop=True)
                        last.then_inc(level_done, 1)
                    continue
                if kind == "increments":
                    pe.wait_ge(unit_out, number["kdT", 1] + 1)
                    pe.wait_ge(level_taken, 4 * (LEVELS + 1))
                    for c in range(NT - 1):
                        for b in range(2):
                            last = mm(ps[4 + c][:, b * 2 * VD:(b + 1) * 2 * VD], kdT[:, b, c * P:(c + 1) * P],
                                      ib[:, c, b * 2 * VD:(b + 1) * 2 * VD], start=True, stop=True)
                        last.then_inc(inc_done, 1)
                    continue
                bank = ps[n % 4]
                if n >= 4:
                    pe.wait_ge(unit_out, n - 3)
                if kind in group_of and k in (0, 2) :
                    pe.wait_ge(ring_in[group_of[kind] % 3], ring_value(group_of[kind]))
                if kind == "hT":
                    if k == 0:
                        pe.wait_ge(x_normed, NT)
                    for t in range(NT):
                        last = tr(bank[:, t * P:(t + 1) * P], xn[:, t, k * P:(k + 1) * P], ident)
                elif kind == "memT":
                    if k == 0:
                        pe.wait_ge(mem_normed, NM)
                    for t in range(NM):
                        last = tr(bank[:, t * P:(t + 1) * P], mem[:, t, k * P:(k + 1) * P], ident)
                elif kind == "table":
                    lo, hi = k * T, min(SPAN, (k + 1) * T)
                    last = mm(bank[0:6, 0:hi - lo], rel[0:33, :], bucket[0:33, lo:hi], start=True, stop=True)
                elif kind == "qf":
                    pe.wait_ge(unit_out, KD)
                    for kk in range(KD):
                        last = mm(bank[:, :], ring[:, 0, kk, k * P:(k + 1) * P], hT[:, kk, :], start=kk == 0, stop=kk == KD - 1)
                elif kind == "bias":
                    if k == 0:
                        pe.wait_ge(hankel_in, 16 * 6)
                    last = mm(bank[:, :], flip, hankel[:, k, :], start=True, stop=True)
                elif kind == "kv":
                    pe.wait_ge(unit_out, number["memT", KD - 1] + 1)
                    for kk in range(KD):
                        last = mm(bank[:, :], memT[:, kk, k * P:(k + 1) * P], ring[:, 0, kk, :], start=kk == 0, stop=kk == KD - 1)
                elif kind == "kdT":
                    if k == 0:
                        pe.wait_ge(kq_ready, LEVELS + 1)
                    for c in range(NT - 1):
                        last = tr(bank[:, c * P:(c + 1) * P], kq[LEVELS % 2][:, k, c * P:(c + 1) * P], ident)
                elif kind == "o":
                    pe.wait_ge(kq_ready, LEVELS + 2)
                    if k > 0:
                        pe.wait_ge(state_ready, 2 * k)
                    for b in range(2):
                        if k > 0:
                            mm(bank[:, b * 2 * VD:(b + 1) * 2 * VD], kq[(LEVELS + 1) % 2][:, b, k * P:(k + 1) * P],
                               state[:, k - 1, b, :], start=True, stop=False)
                        for hh in range(2):
                            h = 2 * b + hh
                            last = mm(bank[:, h * VD:(h + 1) * VD], scores[:, score_at(k, h), :],
                                      ib[:, k, h * VD:(h + 1) * VD], start=k == 0, stop=k == 0 or hh == 1)
                else:
                    width = token_major[kind][1]
                    for kk in range(KD):
                        last = mm(bank[:, 0:width], hT[:, kk, k * P:(k + 1) * P], ring[:, group_of[kind] % 3, kk, 0:width],
                                  start=kk == 0, stop=kk == KD - 1)
                last.then_inc(unit_done, 1)
                n += 1
                if kind in group_of and (kind, k) in (("qf", 1), ("qa", 3), ("ka", 3), ("va", 3), ("ib", 3), ("og", 3), ("kv", 1), ("qc", 3)):
                    pe.wait_ge(unit_done, n)
                    pe.sem_inc(w_used, 1)

            def attention(i, dilated):
                pairs = 0 if dilated else A_PAIRS
                n0 = i * UNITS + pairs * UNITS
                k_tiles = NT if dilated else NM
                width = k_tiles * P
                pe.wait_ge(staged, (i * (2 * NT) if dilated else i * (NT + NM)) + (A_PAIRS * 2 * NT * (not dilated) + NT + k_tiles))
                for which, tiles in ((0, NT), (1, k_tiles)):
                    for t in range(tiles):
                        last = tr(ps[which][:, t * P:(t + 1) * P], staging[:, which, t, :], ident)
                last.then_inc(pair_done, 1)

                def gate(j):
                    if not dilated:
                        return
                    if j % NT == 0:
                        pe.wait_ge(ring_in[j // NT], i * 16 + 64)
                    if j >= 2:
                        pe.wait_ge(gate_out, n0 + (j - 1))
                    for kk in range(KD):
                        last = mm(ps[6 + j % 2][:, :], ring[:, j // NT, kk, (j % NT) * P:(j % NT + 1) * P], hT[:, kk, :],
                                  start=kk == 0, stop=kk == KD - 1)
                    last.then_inc(gate_done, 1)

                def scores_of(j):
                    hh, t = divmod(j, NT)
                    keys = (t + 1) * P if dilated else M
                    rows = slice(hh * HD, (hh + 1) * HD)
                    if j >= 2:
                        pe.wait_ge(max_ready if dilated else exp_done, n0 + (j - 1))
                    mm(ps[2 + j % 2][:, 0:keys], qkT[rows, 0, t * P:(t + 1) * P], qkT[rows, 1, 0:keys], start=True,
                       stop=True).then_inc(qk_done, 1)

                gate(0)
                pe.wait_ge(pair_out, i * 2 + (2 * pairs + 2))
                scores_of(0)
                for j in range(UNITS):
                    hh, t = divmod(j, NT)
                    if j + 1 < UNITS:
                        scores_of(j + 1)
                        gate(j + 1)
                    tiles = t + 1 if dilated else NM
                    pe.wait_ge(exp_done, n0 + (j + 1))
                    for kt in range(tiles):
                        last = tr(ps[4][:, kt * P:(kt + 1) * P], probs[:, j % 2, kt * P:(kt + 1) * P], ident)
                    last.then_inc(pT_done, 1)
                    pe.wait_ge(pT_out, n0 + (j + 1))
                    if j >= 2:
                        pe.wait_ge(y_done, n0 + (j - 1))
                    for kt in range(tiles):
                        values = (va[:, kt, bass.ds(i * P + hh * HD, HD)] if dilated
                                  else kv[:, kt, bass.ds(i * P + (CW + hh * HD), HD)])
                        last = mm(ps[j % 2][:, 0:HD], probsT[:, j % 2, kt * P:(kt + 1) * P], values,
                                  start=kt == 0, stop=kt == tiles - 1)
                    last.then_inc(pv_done, 1)

            with pe.Fori(0, A_PAIRS) as i:
                attention(i, True)
            with pe.Fori(0, C_PAIRS) as i:
                attention(i, False)

            pe.wait_ge(y_done, (A_PAIRS + C_PAIRS) * UNITS)
            pe.wait_ge(pT_out, (A_PAIRS + C_PAIRS) * UNITS)
            for k in range(KD):
                if k >= 4:
                    pe.wait_ge(yT_out, k - 3)
                src, col = (qa, k) if k < 3 else (ib, k - 3) if k < 6 else (qc, k - 6)
                for t in range(NT):
                    last = tr(ps[k % 4][:, t * P:(t + 1) * P], src[:, t, col * P:(col + 1) * P], ident)
                last.then_inc(yT_done, 1)
            pe.wait_ge(yT_out, KD)
            for n in range(3):
                pe.wait_ge(branch_in[n], 16)
            for m in range(KD):
                for br, (w, first, blocks) in enumerate(((w_a, 0, 3), (w_b, 3, 3), (w_c, 6, 2))):
                    n = 3 * m + br
                    if n >= 4:
                        pe.wait_ge(mix_taken, n - 3)
                    for kk in range(blocks):
                        last = mm(ps[4 + n % 4][:, :], w[:, kk, m * P:(m + 1) * P], yT[:, first + kk, :], start=kk == 0, stop=kk == blocks - 1)
                    last.then_inc(mix_done, 1)
            pe.wait_ge(mixed, KD)
            pe.wait_ge(branch_in[3], 16)
            for n in range(2 * NT):
                t, half = n // 2, n % 2
                if n >= 4:
                    pe.wait_ge(x1_ready, n - 3)
                for kk in range(KD):
                    last = mm(ps[n % 4][:, :], gates[:, kk, t * P:(t + 1) * P], w_out[:, kk, half * 512:(half + 1) * 512],
                              start=kk == 0, stop=kk == KD - 1)
                last.then_inc(x1_done, 1)
            pe.wait_ge(x1_ready, 2 * NT)
            for t in range(NT):
                pe.wait_ge(u_ready, t + 1)
                if t >= 2:
                    pe.wait_ge(uT_out, 2 * (t - 1))
                for k in range(KD):
                    last = tr(ps[2 * (t % 2) + k // 4][:, (k % 4) * P:(k % 4 + 1) * P], u_tok[:, t, k * P:(k + 1) * P], ident)
                last.then_inc(uT_done, 1)
            pe.wait_ge(uT_out, 2 * NT)
            pe.wait_ge(c_in[10], 16)
            for t in range(NT):
                for kk in range(KD):
                    last = mm(ps[4][:, t * E:(t + 1) * E], uT[:, kk, t * P:(t + 1) * P], w_router[:, kk, :], start=kk == 0, stop=kk == KD - 1)
            last.then_inc(r_done, 1)

            pe.wait_ge(shared_in[0], 16)
            pe.wait_ge(shared_in[1], 16)
            for t in range(NT + 1):
                if t < NT:
                    if t >= 2:
                        pe.wait_ge(s_hidden, t - 1)
                    for kk in range(KD):
                        last = mm(ps[t % 2][:, :], uT[:, kk, t * P:(t + 1) * P], w_sup[:, kk, :], start=kk == 0, stop=kk == KD - 1)
                    last.then_inc(s_up, 1)
                if t == 1:
                    pe.wait_ge(picked_ready, 1)
                    for tt in range(NT):
                        for other in range(tt + 1):
                            last = mm(ps[4][:, 256 + tt * E:256 + (tt + 1) * E], before if other == tt else ones, picked[:, other, :],
                                      start=other == 0, stop=other == tt)
                    for other in range(NT):
                        last = mm(ps[5][:, 256:256 + E], ones, picked[:, other, :], start=other == 0, stop=other == NT - 1)
                    last.then_inc(place_done, 1)
                    pe.wait_ge(routed, 1)
                if t > 0:
                    q = t - 1
                    pe.wait_ge(s_hidden, q + 1)
                    for f in range(2):
                        last = tr(ps[5][:, f * P:(f + 1) * P], s_hid[:, q % 2, f * P:(f + 1) * P], ident)
                    last.then_inc(s_hidT_done, 1)
                    pe.wait_ge(s_hidT_out, q + 1)
                    if q > 0:
                        pe.wait_ge(out_ready, q)
                    for half in range(2):
                        for f in range(2):
                            last = mm(ps[2 + half][:, :], s_hidT[:, q % 2, f, :], w_sdn[:, f, half * 512:(half + 1) * 512],
                                      start=f == 0, stop=f == 1)
                        last.then_inc(s_down, 1)
            pe.wait_ge(out_ready, NT)

            def route(n, m, e):
                pe.wait_ge(sel_ready, m + 1)
                if not isinstance(m, int) or m >= 1:
                    pe.wait_ge(index_ready, m)
                for t in range(NT):
                    last = mm(ps[7][0:ROWS, 0:4], select[:, n % 2, t, :],
                              route_in[:, t, bass.ds(e, 1), :].rearrange("p a b -> p (a b)"), start=t == 0, stop=t == NT - 1)
                last.then_inc(route_done, 1)

            def transpose_tokens(n, m, turn):
                pe.wait_ge(gather_in[n % 2], turn * 16 + 16)
                for k in range(KD):
                    last = tr(ps[k // 4][:, (k % 4) * ROWS:(k % 4 + 1) * ROWS], gathered[0:ROWS, n % 2, k * P:(k + 1) * P],
                              ident[0:ROWS, 0:ROWS])
                last.then_inc(gT_done, 1)

            def products(bank, left, right, first, last):
                for q, (a, b) in enumerate(((0, 0), (1, 0), (0, 1))):
                    ins = mm(bank, left[a], right[b], start=first and q == 0, stop=last and q == 2)
                return ins

            def expert(n, m, e, u, turn, more, more2):
                pe.wait_ge(gT_low, m * 2 + 2)
                for j in range(2):
                    pe.wait_ge(low_done, u + (j + 1))
                    both = split[(BLOCKS * n + j) % SPLIT]
                    for kk in range(4):
                        k = 4 * j + kk
                        last = products(ps[2][0:ROWS, :], [gatheredT[:, n % 2, part, k, :] for part in range(2)],
                                        [both[:, part, kk, :] for part in range(2)], k == 0, k == KD - 1)
                    last.then_inc(block_used, 1)
                if more:
                    transpose_tokens(n + 1, m + 1, turn + (n + 1) // 2)
                pe.wait_ge(hid_ready, m + 1)
                for f in range(2):
                    last = tr(ps[3][:, f * ROWS:(f + 1) * ROWS], hid[0:ROWS, n % 2, f * P:(f + 1) * P], ident[0:ROWS, 0:ROWS])
                last.then_inc(hidT_done, 1)
                if more2:
                    route(n + 2, m + 2, e + 2)
                pe.wait_ge(low_done, u + 3)
                pe.wait_ge(hidT_low, m + 1)
                if not isinstance(m, int) or m >= 1:
                    pe.wait_ge(y_ready, m)
                both = split[(BLOCKS * n + 2) % SPLIT]
                for half in range(2):
                    for f in range(2):
                        last = products(ps[4 + 2 * half][0:ROWS, :], [hidT[:, n % 2, part, f * ROWS:(f + 1) * ROWS] for part in range(2)],
                                        [both[:, part, 2 * f + half, :] for part in range(2)], f == 0, f == 1)
                last.then_inc(block_used, 1)

            def expert_pass(m0, u0, pair0):
                route(0, m0, 0)
                route(1, m0 + 1, 1)
                transpose_tokens(0, m0, pair0)
                for n in range(TURN):
                    expert(n, m0 + n, n, u0 + BLOCKS * n, pair0, True, True)
                with pe.Fori(1, E // TURN - 1) as g:
                    for n in range(TURN):
                        expert(n, m0 + (g * TURN + n), g * TURN + n, u0 + (g * (BLOCKS * TURN) + BLOCKS * n),
                               pair0 + g * (TURN // 2), True, True)
                last = E - TURN
                for n in range(TURN):
                    expert(n, m0 + (last + n), last + n, u0 + BLOCKS * (last + n), pair0 + last // 2, n + 1 < TURN, n + 2 < TURN)

            expert_pass(0, 0, 0)
            fullest = pe.value_load(most_i[0:1, 0:1], min_val=0, max_val=T)
            with pe.If(fullest > ROWS):
                with pe.Fori(1, PASSES) as r:
                    with pe.If(fullest > r * ROWS):
                        expert_pass(r * E, r * (BLOCKS * E), r * (E // 2))


_INS = ['x', 'mem', 'attn_norm_g', 'w_in', 'q_norm_a', 'k_norm_a', 'rel_bias', 'lb_logits', 'out_norm_b',
        'mem_norm_g', 'w_mem_kv', 'q_norm_c', 'k_norm_c', 'w_branch_a', 'w_branch_b', 'w_branch_c', 'w_out',
        'ffn_norm_g', 'w_router', 'router_bias', 'w_exp_up', 'w_exp_down', 'w_shared_up', 'w_shared_down']


def kernel(**inputs):
    import concourse.bacc as _bacc
    from concourse.bass_utils import run_bass_kernel_spmd as _run

    nc = _bacc.Bacc("TRN2", target_bir_lowering=False, num_devices=1)
    arrays, io, const = {}, {}, {}
    for name in _INS:
        a = np.ascontiguousarray(inputs[name])
        arrays[f"in_{name}_dram"] = a
        io[name] = nc.dram_tensor(f"in_{name}_dram", a.shape, mybir.dt.from_np(a.dtype), kind="ExternalInput").ap()
    for name, a in shape_constants().items():
        arrays[f"const_{name}_dram"] = a
        const[name] = nc.dram_tensor(f"const_{name}_dram", a.shape, mybir.dt.from_np(a.dtype), kind="ExternalInput").ap()
    out = nc.dram_tensor("out_0_dram", (1, T, D), F32, kind="ExternalOutput").ap()
    u_dram = nc.dram_tensor("u_rows", (T, D), F32).ap()
    table_dram = nc.dram_tensor("distance_table", (6, SPAN), F32).ap()
    build(nc, io, out, const, u_dram, table_dram)
    r = _run(nc, [arrays], core_ids=[0])
    return r.results[0]["out_0_dram"]
```

```python
from contextlib import ExitStack

import numpy as np

import concourse.bass as bass
from concourse import mybir

F32 = mybir.dt.float32
F32R = mybir.dt.float32r
I32 = mybir.dt.int32
U32 = mybir.dt.uint32
ALU = mybir.AluOpType
ACT = mybir.ActivationFunctionType
AX = mybir.AxisListType

P = 128
D, T, M = 1024, 512, 256
KD, NT, NM = D // P, T // P, M // P
HD = 64
AW, BK, BV, CW = 6 * HD, 4 * HD, 4 * 96, 4 * HD
VD = 96
EPS = 1e-6
LEVELS = 7
E, FH = 64, 256
GROUPS, TOP_GROUPS, TOP_K = 8, 4, 8
ROUTED_SCALE = 2.5
MASKED = -1e30
SPAN = T + P
QA, KA, VA, QB, IB, OG, QC, GATES = 0, 384, 768, 1152, 1664, 2048, 2432, 2688
A_PAIRS, C_PAIRS = 3, 2
UNITS = 2 * NT
ROWS = 96
PASSES = -(-T // ROWS)
TURN = 4
BLOCKS = 3
RAW, SPLIT = 6, 6
LEAD = 5
NO_TOKEN = 4096.0


def shape_constants():
    i = np.arange(P)
    r, c = i[:, None], i[None, :]
    level = np.where(c >= r, np.bitwise_xor(r, c), 1000)
    square = np.stack([r == c, r + c == P - 1, np.broadcast_to(c, (P, P)), r < c, np.ones((P, P)), level], 1)
    d = T - 1 - np.arange(SPAN)
    times = ((d >= 0) & (d <= 128)).astype(int) + ((d >= 0) & (d % 4 == 0)) + ((d >= 0) & (d % 16 == 0))
    far = 16 + (np.log(np.maximum(d, 1).astype(np.float32) / np.float32(16)) / np.float32(np.log(128.0))
                * np.float32(16)).astype(np.int32)
    bucket = np.where(d < 16, d, np.minimum(far, 31))
    hot = (bucket[None, :] == np.arange(32)[:, None]) & (times > 0)[None, :]
    last = np.where(times > 0, np.log(np.maximum(times, 1)), MASKED)
    tokens = np.stack([i + P * t - NO_TOKEN for t in range(NT)], 1)
    return {
        "square": np.ascontiguousarray(square, dtype=np.float32),
        "bucket": np.concatenate([hot, last[None, :]], 0).astype(np.float32),
        "tokens": np.ascontiguousarray(tokens, dtype=np.float32),
    }


def ahead(n, last):
    return min(max(BLOCKS * (TURN - n) - LEAD, 0), BLOCKS) if last else BLOCKS


def view(a, *shape):
    names = "abcd"[:len(shape)]
    return a if len(shape) == 1 else a.rearrange(
        f"p ({' '.join(names)}) -> p {' '.join(names)}", **dict(zip(names[1:], shape[1:])))


def bcast(a, *shape):
    return a.broadcast_to(list(shape))


def build(nc, io, out, const, u_dram, table_dram, debug=None):
    ctx = ExitStack()
    with ctx:
        def sem(name):
            return ctx.enter_context(nc.semaphore(name))

        words = 53200
        arena_base = -(-nc.sbuf_base // 32) * 32
        arena = ctx.enter_context(nc.sbuf_tensor("arena", [P, words], F32))
        top = [0]

        def at(offset, *shape):
            return view(arena[:, offset:offset + int(np.prod(shape))], *shape)

        def take(*shape):
            offset = top[0]
            top[0] += int(np.prod(shape))
            assert top[0] <= words, top[0]
            return offset

        square = at(take(6, P), 6, P)
        ident, flip, counting, before, ones, level = (square[:, n, :] for n in range(6))
        gains = at(take(32), 32)
        lb = at(take(8), 8)
        small = at(take(320), 320)
        x_at = take(NT, D)
        x_tok = at(x_at, NT, D)
        hT_at = take(KD, T)
        bias_at = take(6, T)
        bias = at(bias_at, 6, T)
        ring_at = take(3, KD, T)
        gates_at = take(3 * KD, T)
        gates = at(gates_at, 3 * KD, T)
        qa_at, ka_at, va_at = take(NT, AW), take(NT, AW), take(NT, AW)
        qa, ka, va = (at(o, NT, AW) for o in (qa_at, ka_at, va_at))
        kv_at = take(NM, 2 * CW)
        kv = at(kv_at, NM, 2 * CW)
        ib_at, og_at = take(NT, BV), take(NT, BV)
        ib, og = at(ib_at, NT, BV), at(og_at, NT, BV)
        qc = at(take(NT, CW), NT, CW)
        staging_at = take(2, NT, P)
        staging = at(staging_at, 2, NT, P)
        qkT_at = take(2, T)
        qkT = at(qkT_at, 2, T)
        logits_at = take(2, T)
        logits, probs, probsT = at(logits_at, 2, T), at(take(2, T), 2, T), at(take(2, T), 2, T)
        w_router = at(take(KD, E), KD, E)
        gain_rows = at(take(P), P)
        out_norm = at(take(BV), BV)

        xn = at(qa_at, NT, D)
        squares = at(ib_at, 2, NT, AW)
        hankel = at(logits_at, 6, T)
        bucket = at(staging_at, SPAN)
        table = at(qkT_at, SPAN)
        scores = at(logits_at, 16, P)
        kdT = at(logits_at + 2048, 2, 3 * P)
        mask = at(staging_at, 2, P)
        state = at(staging_at + 256, NT - 1, 2, 2 * VD)
        mem = at(kv_at, NM, D)
        rec = gates_at + 4096
        fT, qT, kT, bT = (at(rec + n * 1024, 2, T) for n in range(4))
        expo = [at(rec + (4 + n) * 1024, 2, T) for n in range(2)]
        kq = [at(rec + (6 + n) * 1024, 2, T) for n in range(2)]
        o_tok = at(rec, NT, BV)
        o_sq = at(rec + 2048, NT, BV)
        o_gate = at(gates_at, NT, BV)
        c_sq = at(gates_at + 2048, 1536)
        ffn_gain = at(bias_at + 1024, D)
        u_tok = at(gates_at + 4096, NT, D)
        s_hid = at(qa_at, NT, FH)
        ro = [at(ib_at + n * 256, NT, E) for n in range(16)]
        (score, choice, masked, masked2, picked, weight, place) = ro[0:7]
        router_bias = at(ib_at + 11 * 256, E)
        rs = at(ib_at + 11 * 256 + E, 1024)

        def rounded(name, offset, *shape):
            n = int(np.prod(shape))
            tensor = nc.alloc_sbuf_tensor_at(name, [P, n], F32R, offset=arena_base + 4 * offset)
            return view(tensor[:, 0:n], *shape)

        def rounded_pair(name, offsets, *shape):
            return [rounded(f"{name}_{part}", o, *shape) for part, o in zip(("high", "low"), offsets)]

        hT = rounded_pair("hT", (hT_at, x_at), KD, T)
        memT = rounded_pair("memT", (gates_at, gates_at + 2048), KD, M)
        yT = rounded_pair("yT", (ka_at, hT_at), KD, T)
        mixT_halves = [rounded_pair(f"mixT{h}", (gates_at + 2048 * h, staging_at + 2048 * h), KD // 2, T) for h in range(2)]
        mixT = [[mixT_halves[k // 4][part][:, k % 4, :] for k in range(KD)] for part in range(2)]
        uT = rounded_pair("uT", (hT_at, ka_at), KD, T)
        routerT = rounded_pair("w_router", (bias_at, bias_at + 512), KD, E)
        s_hidT = [at(qa_at + 1024 + 256 * n, 2 * P) for n in range(2)]
        s_down_w = at(logits_at, 2, D)
        front_raw = [arena[:, ring_at + 2048 * n:ring_at + 2048 * (n + 1)] for n in range(2)]
        front_split = [rounded(f"front_split{n}", ring_at + 4096 * (n + 1), 2, 2048) for n in range(2)]
        s_up_split = [rounded(f"s_up_split{n}", o, 2, 2048) for n, o in enumerate((gates_at + 8192, gates_at))]
        r_sig = at(ib_at + 2 * 256, T)
        route_in = rounded("route_in", ib_at + 7 * 256, NT, E, 4)
        raw = [at(ring_at + 2048 * n, 4, 512) for n in (2, 3, 4, 5, 0, 1)]
        split = [rounded(f"split{n}", o, 2, 4, 512) for n, o in
                 enumerate((gates_at, gates_at + 4096, gates_at + 8192, hT_at, ka_at, x_at))]
        gathered = at(staging_at, 2, D)
        y_out = at(logits_at, 2, D)
        select = rounded("select", logits_at + 2048, 2, NT, ROWS)
        gatheredT = rounded("gatheredT", bias_at, 2, 2, KD, ROWS)
        hidT = rounded("hidT", logits_at + 2048 + 2 * NT * ROWS, 2, 2, 2 * ROWS)
        hid = at(qa_at, 2, FH)
        e_tanh = at(qa_at + 512, 2, FH)
        e_act = at(qa_at + 1024, 2, FH)
        index = small[:, 300:304].bitcast(U32)
        add_index = small[:, 292:296].bitcast(U32)
        slot_w = small[:, 304:308]
        most = small[:, 308:309]
        most_i = small[:, 309:310].bitcast(I32)

        rel = small[:, 312:318]
        eps = small[:, 298:299]
        ps = [ctx.enter_context(nc.psum_tensor(f"bank{n}", [P, 512], F32)) for n in range(8)]

        c_in = [sem(f"const_in{n}") for n in range(12)]
        x_in = [sem(f"x_in{t}") for t in range(NT)]
        mem_in = sem("mem_in")
        front_in = [sem(f"front_in{s}") for s in range(2)]
        front_high, front_low, front_used = map(sem, ("front_high", "front_low", "front_used"))
        f_done, f_high, f_low, gains_done, gains_out = map(sem, ("f_done", "f_high", "f_low", "gains_done", "gains_out"))
        table_out, hankel_in = sem("table_out"), sem("hankel_in")
        x_squared, x_rooted, x_normed, mem_normed = map(sem, ("x_squared", "x_rooted", "x_normed", "mem_normed"))
        unit_done, unit_out = sem("unit_done"), sem("unit_out")
        v_step, a_step = sem("v_step"), sem("a_step")
        lb_in_exp, lb_exp = sem("lb_in_exp"), sem("lb_exp")
        f_exp, f_ready, q_tanh, log_ready = map(sem, ("f_exp", "f_ready", "q_tanh", "log_ready"))
        diff_ready, expo_ready, kq_ready = map(sem, ("diff_ready", "expo_ready", "kq_ready"))
        level_done, level_taken = sem("level_done"), sem("level_taken")
        inc_done, state_ready = sem("inc_done"), sem("state_ready")
        qk_squared, qk_summed, qk_rooted = sem("qk_squared"), sem("qk_summed"), sem("qk_rooted")
        o_summed, o_rooted, og_tanh, c_summed, c_rooted = map(sem, ("o_summed", "o_rooted", "og_tanh", "c_summed", "c_rooted"))
        staged, pair_done, pair_out = map(sem, ("staged", "pair_done", "pair_out"))
        qk_done, max_ready, exp_done, pT_done, pT_out, pv_done, y_done = map(
            sem, ("qk_done", "max_ready", "exp_done", "pT_done", "pT_out", "pv_done", "y_done"))
        gate_done, gate_tanh, gate_out = map(sem, ("gate_done", "gate_tanh", "gate_out"))
        x_again, s_down_in = sem("x_again"), sem("s_down_in")
        yT_done, yT_high, yT_low, mix_done, mix_taken, mixed, mixT_high, mixT_low = map(
            sem, ("yT_done", "yT_high", "yT_low", "mix_done", "mix_taken", "mixed", "mixT_high", "mixT_low"))
        x1_done, x1_ready, x1_squared, x1_rooted, u_ready = map(sem, ("x1_done", "x1_ready", "x1_squared", "x1_rooted", "u_ready"))
        u_stored, uT_done, uT_high, uT_low, router_high, router_low = map(
            sem, ("u_stored", "uT_done", "uT_high", "uT_low", "router_high", "router_low"))
        r_done, r_tanh, r_turned, picked_ready, place_done, routed = map(sem, ("r_done", "r_tanh", "r_turned", "picked_ready", "place_done", "routed"))
        s_up, s_tanhed, s_hidden, s_hidT_done, s_hidT_out, s_down, out_ready, out_stored = map(
            sem, ("s_up", "s_tanhed", "s_hidden", "s_hidT_done", "s_hidT_out", "s_down", "out_ready", "out_stored"))
        raw_in = [sem(f"raw_in{s}") for s in range(RAW)]
        high_done, low_done, block_used = sem("high_done"), sem("low_done"), sem("block_used")
        sel_ready, route_done, index_ready = map(sem, ("sel_ready", "route_done", "index_ready"))
        gather_in = [sem(f"gather_in{n}") for n in range(2)]
        gT_done, gT_high, gT_low = map(sem, ("gT_done", "gT_high", "gT_low"))
        tanh_done, act_ready, hid_ready, hidT_done, hidT_high, hidT_low = map(
            sem, ("tanh_done", "act_ready", "hid_ready", "hidT_done", "hidT_high", "hidT_low"))
        y_ready, added, cleared = map(sem, ("y_ready", "added", "cleared"))

        groups = [("qf", QB, 512), ("qa", QA, AW), ("ka", KA, AW), ("va", VA, AW), ("ib", IB, BV), ("og", OG, BV),
                  ("kv", None, 2 * CW), ("qc", QC, CW)]
        G0, B0, O0, S0 = 16, 28, 32, 36

        def block_shape(w):
            if w < G0:
                return 4, groups[w // 2][2]
            return (8, 256) if w < O0 else (4, 512)

        def raw_block(w):
            a, b = block_shape(w)
            return view(front_raw[w % 2][:, 0:a * b], a, b)

        def split_block(w):
            a, b = block_shape(w)
            both = s_up_split[w - S0] if w >= S0 else front_split[w % 2]
            return [view(both[:, part, 0:a * b], a, b) for part in range(2)]

        tiles_of = {"kv": NM}
        plan = [("table", 0), ("table", 1), ("group", 0)] + [("bias", h) for h in range(6)]
        for g in range(1, len(groups)):
            plan += [("group", g), ("level", g - 1)]
        plan += [("level", LEVELS), ("kdT", 0), ("kdT", 1), ("increments", 0)] + [("o", c) for c in range(NT)]
        units = []
        for kind, k in plan:
            if kind == "group":
                units += [(groups[k][0], t) for t in range(tiles_of.get(groups[k][0], NT))]
            elif kind not in ("level", "increments"):
                units.append((kind, k))
        number = {u: n for n, u in enumerate(units)}
        token_major = {"qa": (qa, AW), "ka": (ka, AW), "va": (va, AW), "ib": (ib, BV), "og": (og, BV), "qc": (qc, CW)}

        def group_done(g):
            return number[groups[g][0], tiles_of.get(groups[g][0], NT) - 1] + 1

        def score_at(c, h):
            return (c // 2 * 2 + h % 2) * 4 + c % 2 * 2 + h // 2

        def used(w):
            if w < G0:
                return (unit_done, group_done(w // 2)) if w % 2 else (front_used, w // 2 + 1)
            if w < B0:
                return gate_done, 2 * (w - G0) + 2
            if w < O0:
                return mix_done, 3 * (2 * (w - B0) + 2)
            return (x1_done, NT * ((w - O0) // 2 + 1)) if w % 2 else (front_used, G0 // 2 + (w - O0) // 2 + 1)

        block = ctx.enter_context(nc.Block())

        @block.sync
        def _(sp):
            for t in range(NT):
                sp.dma_start(x_tok[:, t, :], io["x"][0, t * P:(t + 1) * P, :]).then_inc(x_in[t], 16)
            sp.dma_start(square[:, :, :], const["square"]).then_inc(c_in[0], 16)
            w_in = io["w_in"][0].rearrange("(k p) n -> p k n", p=P)
            w_kv = io["w_mem_kv"][0].rearrange("(k p) n -> p k n", p=P)
            w_branch = io["w_branches"].rearrange("(k p) n -> p k n", p=P)
            w_out = io["w_out"][0].rearrange("(k p) n -> p k n", p=P)
            w_sup = io["w_shared_up"][0].rearrange("(k p) n -> p k n", p=P)
            w_sdn = io["w_shared_down"][0].rearrange("(k p) n -> p k n", p=P)

            def load_block(w):
                if w >= 2:
                    sp.wait_ge(front_low, w - 1)
                if w < G0:
                    _, column, width = groups[w // 2]
                    k0 = 4 * (w % 2)
                    src = w_kv[:, k0:k0 + 4, :] if column is None else w_in[:, k0:k0 + 4, column:column + width]
                elif w < B0:
                    src = w_in[:, :, GATES + 256 * (w - G0):GATES + 256 * (w - G0 + 1)]
                elif w < O0:
                    src = w_branch[:, :, 256 * (w - B0):256 * (w - B0 + 1)]
                elif w < S0:
                    half, k0 = (w - O0) // 2, 4 * (w % 2)
                    src = w_out[:, k0:k0 + 4, half * 512:(half + 1) * 512]
                else:
                    src = w_sup[:, 4 * (w - S0):4 * (w - S0) + 4, :]
                sp.dma_start(raw_block(w), src).then_inc(front_in[w % 2], 16)

            sp.wait_ge(x_in[NT - 1], 16)
            load_block(0)
            sp.dma_start(mem[:, :, :], io["mem"][0].rearrange("(t p) d -> p t d", p=P)).then_inc(mem_in, 16)
            load_block(1)
            sp.wait_ge(unit_out, number["table", 1] + 1)
            sp.dma_start(table_dram, table[0:6, :]).then_inc(table_out, 16)
            sp.wait_ge(table_out, 16)
            for h in range(6):
                src = bass.AP(table_dram.tensor, h * SPAN, [[1, P], [1, T]])
                sp.dma_start(hankel[:, h, :], src).then_inc(hankel_in, 16)
            for w in range(2, G0 + 2):
                load_block(w)
            sp.dma_start(w_router[:, :, :], io["w_router"][0].rearrange("(k p) n -> p k n", p=P)).then_inc(c_in[10], 16)
            with sp.Fori(0, (B0 - G0) // 2 - 1) as i:
                for q in range(2):
                    sp.wait_ge(front_low, i * 2 + (G0 + q + 1))
                    src = w_in[:, :, bass.ds(i * 512 + (GATES + 256 * (q + 2)), 256)]
                    sp.dma_start(raw_block(G0 + q), src).then_inc(front_in[q], 16)
            for w in range(B0, O0):
                load_block(w)
            sp.wait_ge(gate_done, A_PAIRS * UNITS)
            sp.wait_ge(max_ready, A_PAIRS * UNITS)
            sp.dma_start(ffn_gain, bcast(io["ffn_norm_g"], P, D)).then_inc(c_in[11], 16)
            sp.dma_start(x_tok[:, :, :], io["x"][0].rearrange("(t p) d -> p t d", p=P)).then_inc(x_again, 16)
            sp.wait_ge(yT_done, KD)
            sp.dma_start(router_bias, bcast(io["router_bias"], P, E)).then_inc(c_in[9], 16)
            sp.dma_start(rs[:, 616:620], const["tokens"]).then_inc(c_in[9], 16)
            for w in range(O0, S0 + 2):
                load_block(w)
            for t in range(NT):
                sp.wait_ge(u_ready, t + 1)
                sp.dma_start(u_dram[t * P:(t + 1) * P, :], u_tok[:, t, :]).then_inc(u_stored, 16)
            sp.wait_ge(x1_done, 2 * NT)
            sp.dma_start(s_down_w[:, :, :], w_sdn).then_inc(s_down_in, 16)

            up_src = io["w_exp_up"][0].rearrange("e (k p) n -> p e k n", p=P)
            dn_src = io["w_exp_down"][0].rearrange("e (k p) (h n) -> p e k h n", p=P, n=512)

            def load_expert(e, n, u0):
                for j in range(BLOCKS):
                    load_expert_block(e, n, j, u0)

            def load_expert_block(e, n, j, u0):
                s = (BLOCKS * n + j) % RAW
                if not isinstance(u0, int) or u0 + j >= RAW:
                    sp.wait_ge(low_done, u0 + (j - RAW + 1))
                elif s < 4:
                    sp.wait_ge(x1_done, 2 * NT)
                else:
                    sp.wait_ge(front_low, S0 + s - 3)
                if j < 2:
                    sp.dma_start(raw[s], up_src[:, e, 4 * j:4 * j + 4, :]).then_inc(raw_in[s], 16)
                else:
                    sp.dma_start(raw[s].rearrange("p (k h) n -> p k (h n)", h=2),
                                 dn_src[:, e].rearrange("p k h n -> p k (h n)")).then_inc(raw_in[s], 16)

            load_expert(0, 0, 0)
            load_expert(1, 1, 3)
            load_expert_block(2, 2, 0, 6)
            load_expert_block(2, 2, 1, 6)
            for t in range(NT):
                sp.wait_ge(out_ready, t + 1)
                sp.dma_start(out[0, t * P:(t + 1) * P, :], x_tok[:, t, :]).then_inc(out_stored, 16)
            load_expert_block(2, 2, 2, 6)
            load_expert(3, 3, 9)
            with sp.Fori(1, E // TURN) as g:
                for n in range(TURN):
                    load_expert(g * TURN + n, n, g * (BLOCKS * TURN) + BLOCKS * n)
            sp.wait_ge(routed, 1)
            fullest = sp.value_load(most_i[0:1, 0:1], min_val=0, max_val=T)
            with sp.If(fullest > ROWS):
                with sp.Fori(1, PASSES) as r:
                    with sp.If(fullest > r * ROWS):
                        with sp.Fori(0, E // TURN) as g:
                            for n in range(TURN):
                                load_expert(g * TURN + n, n, r * (BLOCKS * E) + (g * (BLOCKS * TURN) + BLOCKS * n))

        @block.gpsimd
        def _(pool):
            pool.memset(eps, EPS).then_inc(c_in[8], 1)
            for n, (name, r0) in enumerate((("attn_norm_g", 0), ("mem_norm_g", 8), ("lb_logits", 20))):
                src = io[name].rearrange("a (k p) -> (a k) p", p=P)
                pool.dma_start(gain_rows[r0:r0 + src.shape[0], :], src).then_inc(c_in[1], 16)
            for n, name in enumerate(("q_norm_a", "k_norm_a", "q_norm_c", "k_norm_c")):
                for half in range(2):
                    pool.dma_start(gain_rows[16 + n:17 + n, half * HD:(half + 1) * HD], io[name]).then_inc(c_in[1], 16)
            pool.dma_start(rel[0:32, :], io["rel_bias"]).then_inc(c_in[5], 16)
            pool.dma_start(bucket[0:33, :], const["bucket"]).then_inc(c_in[6], 16)
            pool.dma_start(out_norm, bcast(io["out_norm_b"], P, BV)).then_inc(c_in[7], 16)
            pool.wait_ge(c_in[8], 1)
            pool.memset(rel[32:33, :], 1.0).then_inc(c_in[8], 1)

            pool.wait_ge(y_done, (A_PAIRS + C_PAIRS) * UNITS)
            pool.wait_ge(x1_done, 2 * NT)
            pool.memset(gathered[:, :, :], 0.0).then_inc(cleared, 1)
            bound = pool.to_reg(T - 1)
            count = pool.alloc_register("experts_done")
            target = pool.alloc_register("wait_value")
            out_rows = out.rearrange("a t d -> (a t) d")

            def wait_count(semaphore, scale, plus):
                pool.reg_mul(target, count, scale) if scale != 1 else pool.reg_mov(target, count)
                pool.reg_add(target, target, plus)
                pool.wait_ge(cleared, 1)
                pool.wait_ge(semaphore, target)

            def gather(n, ahead):
                wait_count(index_ready, 1, ahead + 1)
                if ahead >= 2:
                    wait_count(gT_done, 1, ahead - 1)
                pool.indirect_dma_start(gathered[0:ROWS, n % 2, :], None, u_dram,
                                        bass.IndirectOffsetOnAxis(ap=index[0:ROWS, n % 4:n % 4 + 1], axis=0),
                                        bounds_check=bound, oob_is_err=False).then_inc(gather_in[n % 2], 16)

            def scatter(n, first=False):
                wait_count(y_ready, 1, 1)
                if not first:
                    wait_count(added, 16, 0)
                pool.indirect_dma_start(out_rows, bass.IndirectOffsetOnAxis(ap=add_index[0:ROWS, n % 4:n % 4 + 1], axis=0),
                                        y_out[0:ROWS, n % 2, :], None, bounds_check=bound, oob_is_err=False,
                                        compute_op=ALU.add).then_inc(added, 16)
                pool.reg_add(count, count, 1)

            def expert_pass(first):
                gather(0, 0)
                gather(1, 1)
                gather(2, 2)
                for n in range(TURN):
                    gather(n + 3, 3)
                    if first and n == 0:
                        pool.wait_ge(out_stored, 16 * NT)
                    scatter(n, first and n == 0)
                with pool.Fori(1, E // TURN - 1):
                    for n in range(TURN):
                        gather(n + 3, 3)
                        scatter(n)
                for n in range(TURN):
                    if n + 3 < TURN:
                        gather(n + 3, 3)
                    scatter(n)

            pool.reg_mov(count, 0)
            pool.wait_ge(cleared, 1)
            pool.wait_ge(u_stored, 16 * NT)
            expert_pass(True)
            fullest = pool.value_load(most_i[0:1, 0:1], min_val=0, max_val=T)
            pool.wait_ge(added, 16 * E)
            with pool.If(fullest > ROWS):
                with pool.Fori(1, PASSES) as r:
                    with pool.If(fullest > r * ROWS):
                        expert_pass(False)
                        wait_count(added, 16, 0)

        @block.scalar
        def _(act):
            def copy(o, i, **kw):
                return nc.scalar.activation(o, i, ACT.Copy, **kw)

            def high_block(w):
                if w >= S0:
                    act.wait_ge(*((mixed, KD) if w == S0 else (x1_done, 2 * NT)))
                elif w >= 2:
                    act.wait_ge(*used(w - 2))
                act.wait_ge(front_in[w % 2], 16 * (w // 2 + 1))
                copy(split_block(w)[0], raw_block(w)).then_inc(front_high, 1)

            act.wait_ge(c_in[8], 2)
            for t in range(NT):
                act.wait_ge(x_in[t], 16)
                nc.scalar.activation(xn[:, t, :], x_tok[:, t, :], ACT.Square,
                                     accum_out=small[:, t:t + 1]).then_inc(x_squared, 1)
            act.wait_ge(x_squared, NT)
            nc.scalar.activation(small[:, 6:10], small[:, 0:4], ACT.Sqrt, bias=eps,
                                 scale=1.0 / D).then_inc(x_rooted, 1)
            act.wait_ge(gains_done, 1)
            copy(gains[:, 0:24], ps[3][:, 0:24]).then_inc(gains_out, 1)
            for k in range(2):
                act.wait_ge(unit_done, k + 1)
                copy(table[0:6, k * T:min(SPAN, (k + 1) * T)], ps[k][0:6, 0:min(T, SPAN - k * T)]).then_inc(unit_out, 1)
            high_block(0)
            act.wait_ge(gains_out, 1)

            def feature_major(f):
                act.wait_ge(f_done, f + 1)
                dst, src = (hT[0][:, f, :], ps[4 + f % 4][:, :]) if f < KD else (memT[0][:, f - KD, :], ps[4 + f % 4][:, 0:M])
                copy(dst, src, scale=gains[:, f:f + 1]).then_inc(f_high, 1)

            for f in range(KD):
                feature_major(f)
            high_block(1)
            act.wait_ge(lb_in_exp, 1)
            nc.scalar.activation(lb[:, 0:4], lb[:, 0:4], ACT.Exp).then_inc(lb_exp, 1)
            act.wait_ge(mem_in, 16)
            for t in range(NM):
                nc.scalar.activation(at(gates_at + t * D, D), mem[:, t, :], ACT.Square,
                                     accum_out=small[:, 4 + t:5 + t]).then_inc(x_squared, 1)
            act.wait_ge(x_squared, NT + NM)
            nc.scalar.activation(small[:, 10:12], small[:, 4:6], ACT.Sqrt, bias=eps,
                                 scale=1.0 / D).then_inc(x_rooted, 1)

            def exponents(j):
                if j <= LEVELS:
                    act.wait_ge(diff_ready, j + 1)
                e = expo[j % 2]
                if j < LEVELS:
                    m = 1 << (LEVELS - 1 - j)
                    v = e.rearrange("p b (n m) -> p (b n) m", m=2 * m)
                    nc.scalar.activation(v[:, :, 0:m], v[:, :, 0:m], ACT.Exp, scale=-1.0).then_inc(expo_ready, 1)
                    nc.scalar.activation(v[:, :, m:2 * m], v[:, :, m:2 * m], ACT.Exp).then_inc(expo_ready, 1)
                elif j == LEVELS:
                    nc.scalar.activation(e, e, ACT.Exp, scale=-1.0).then_inc(expo_ready, 2)
                else:
                    act.wait_ge(kq_ready, j - 1)
                    nc.scalar.activation(e, bT[:, :, :], ACT.Exp).then_inc(expo_ready, 2)

            def forget_gate():
                act.wait_ge(unit_out, number["qf", 3] + 1)
                nc.scalar.activation(expo[0][:, :, :], fT[:, :, :], ACT.Exp, scale=-1.0).then_inc(f_exp, 1)
                nc.scalar.activation(expo[1][:, :, :], qT[:, :, :], ACT.Tanh, scale=0.5).then_inc(q_tanh, 1)

            def log_forget():
                act.wait_ge(f_ready, 1)
                nc.scalar.activation(fT[:, :, :], fT[:, :, :], ACT.Ln).then_inc(log_ready, 1)

            def roots_a():
                act.wait_ge(qk_summed, 2)
                nc.scalar.activation(small[:, 68:116], small[:, 20:68], ACT.Sqrt, bias=eps,
                                     scale=1.0 / HD).then_inc(qk_rooted, 1)

            def take_unit(kind, k):
                n = number[kind, k]
                bank = ps[n % 4]
                act.wait_ge(unit_done, n + 1)
                if kind == "qf":
                    ins = copy((qT, fT)[k // 2][:, k % 2, :], bank[:, :])
                elif kind == "bias":
                    ins = copy(bias[:, k, :], bank[:, :])
                elif kind == "kv":
                    ins = copy(kv[:, k, :], bank[:, :])
                elif kind == "kdT":
                    ins = copy(kdT[:, k, :], bank[:, 0:3 * P])
                elif kind == "o":
                    ins = copy(o_tok[:, k, :], bank[:, 0:BV])
                else:
                    dst, width = token_major[kind]
                    ins = copy(dst[:, k, :], bank[:, 0:width])
                ins.then_inc(unit_out, 1)

            for g, (kind, _, _) in enumerate(groups):
                high_block(2 * g + 2)
                if kind == "ib":
                    act.wait_ge(qk_summed, 2)
                for t in range(tiles_of.get(kind, NT)):
                    take_unit(kind, t)
                if g == 0:
                    for f in range(KD, 2 * KD):
                        feature_major(f)
                if g < len(groups) - 1:
                    high_block(2 * g + 3)
                if g == 0:
                    forget_gate()
                    for h in range(6):
                        take_unit("bias", h)
                    log_forget()
                    exponents(0)
                    exponents(1)
                else:
                    if kind == "va":
                        roots_a()
                    exponents(g + 1)
                if kind == "kv":
                    nc.scalar.activation(o_gate[:, :, :], og[:, :, :], ACT.Tanh, scale=0.5).then_inc(og_tanh, 1)
            for k in range(2):
                take_unit("kdT", k)
            high_block(2 * len(groups) + 1)
            act.wait_ge(c_summed, 2)
            nc.scalar.activation(small[:, 236:260], small[:, 212:236], ACT.Sqrt, bias=eps,
                                 scale=1.0 / HD).then_inc(c_rooted, 1)
            for k in range(NT):
                take_unit("o", k)

            act.wait_ge(o_summed, NT)
            nc.scalar.activation(small[:, 180:196], small[:, 164:180], ACT.Sqrt, bias=eps,
                                 scale=1.0 / VD).then_inc(o_rooted, 1)

            def attention(i, dilated):
                pairs = 0 if dilated else A_PAIRS
                n0 = i * UNITS + pairs * UNITS
                act.wait_ge(pair_done, i + (pairs + 1))
                copy(qkT[:, 0, :], ps[0][:, :], scale=gains[:, (16 if dilated else 18):(17 if dilated else 19)]).then_inc(pair_out, 1)
                width = T if dilated else M
                copy(qkT[:, 1, 0:width], ps[1][:, 0:width], scale=gains[:, (17 if dilated else 19):(18 if dilated else 20)]).then_inc(pair_out, 1)

                def exponential(j):
                    keys = (j % NT + 1) * P if dilated else M
                    act.wait_ge(max_ready, n0 + (j + 1))
                    src = logits[:, j % 2, 0:keys] if dilated else ps[2 + j % 2][:, 0:keys]
                    nc.scalar.activation(probs[:, j % 2, 0:keys], src, ACT.Exp, bias=small[:, 284 + j % 2:285 + j % 2],
                                         accum_out=small[:, 288 + j % 2:289 + j % 2]).then_inc(exp_done, 1)

                def gate(j):
                    if dilated:
                        act.wait_ge(gate_done, n0 + (j + 1))
                        nc.scalar.activation(ps[6 + j % 2][:, :], ps[6 + j % 2][:, :], ACT.Tanh, scale=0.5).then_inc(gate_tanh, 1)

                gate(0)
                exponential(0)
                for j in range(UNITS):
                    if j + 1 < UNITS:
                        exponential(j + 1)
                    keys = (j % NT + 1) * P if dilated else M
                    act.wait_ge(pT_done, n0 + (j + 1))
                    copy(probsT[:, j % 2, 0:keys], ps[4][:, 0:keys]).then_inc(pT_out, 1)
                    if j + 1 < UNITS:
                        gate(j + 1)
                    if dilated and j % 2 == 0:
                        q = j // 2
                        act.wait_ge(front_in[q % 2], i * 32 + 16 * ((G0 + 2 + q) // 2 + 1))
                        copy(split_block(G0 + q)[0], raw_block(G0 + q)).then_inc(front_high, 1)

            with act.Fori(0, A_PAIRS) as i:
                attention(i, True)
            with act.Fori(0, C_PAIRS) as i:
                attention(i, False)

            for k in range(KD):
                act.wait_ge(yT_done, k + 1)
                copy(yT[0][:, k, :], ps[k % 4][:, :]).then_inc(yT_high, 1)
            act.wait_ge(c_in[10], 16)
            copy(routerT[0], w_router).then_inc(router_high, 1)
            for m in range(KD):
                act.wait_ge(mixed, m + 1)
                copy(mixT[0][m], gates[:, KD + m, :]).then_inc(mixT_high, 1)
                if m % 2:
                    high_block(B0 + m // 2 + 2)
            for w in (O0 + 2, O0 + 3, S0):
                high_block(w)

            for t in range(NT):
                act.wait_ge(x1_ready, NT + t + 1)
                nc.scalar.activation(u_tok[:, t, :], x_tok[:, t, :], ACT.Square,
                                     accum_out=small[:, t:t + 1]).then_inc(x1_squared, 1)
                act.wait_ge(x1_squared, t + 1)
                nc.scalar.activation(small[:, 6 + t:7 + t], small[:, t:t + 1], ACT.Sqrt, bias=eps,
                                     scale=1.0 / D).then_inc(x1_rooted, 1)
            for t in range(NT):
                act.wait_ge(uT_done, t + 1)
                for half in range(2):
                    copy(uT[0][:, 4 * half:4 * half + 4, t * P:(t + 1) * P],
                         view(ps[2 * (t % 2) + half][:, :], 4, P)).then_inc(uT_high, 1)
            high_block(S0 + 1)
            act.wait_ge(r_done, 1)
            nc.scalar.activation(r_sig[0:E, :], ps[4][0:E, :], ACT.Tanh, scale=0.5).then_inc(r_tanh, 1)
            for t in range(NT):
                act.wait_ge(s_up, t + 1)
                nc.scalar.activation(s_hid[:, t, :], ps[t][:, 0:FH], ACT.Tanh, scale=0.5).then_inc(s_tanhed, 1)

            def shared():
                for t in range(NT):
                    act.wait_ge(s_hidT_done, t + 1)
                    if t >= 2:
                        act.wait_ge(s_down, 2 * (t - 1))
                    copy(s_hidT[t % 2], ps[6 - t % 2][:, 0:2 * P]).then_inc(s_hidT_out, 1)
                    if t < 2:
                        high(t, t, 0)

            def high(q, u, round0):
                if isinstance(u, int) and u < SPLIT:
                    free = ((s_up, NT), (u_stored, 16 * NT), (s_up, NT), (s_up, NT), (s_up, NT),
                            (out_stored, 16 * NT))[u]
                    act.wait_ge(*free)
                    if u == 1:
                        act.wait_ge(uT_done, NT)
                act.wait_ge(raw_in[q % RAW], round0 * 16 + 16 * (q // RAW + 1))
                copy(split[q % SPLIT][:, 0], raw[q % RAW]).then_inc(high_done, 1)

            def high_tokens(n, m):
                act.wait_ge(gT_done, m + 1)
                for half in range(2):
                    copy(gatheredT[:, n % 2, 0, 4 * half:4 * half + 4, :],
                         view(ps[half][:, 0:4 * ROWS], 4, ROWS)).then_inc(gT_high, 1)

            def gate_tanh_of(n, m, used):
                act.wait_ge(block_used, used)
                nc.scalar.activation(e_tanh[0:ROWS, n % 2, :], ps[2 + 3 * (n % 2)][0:ROWS, 0:FH], ACT.Tanh,
                                     scale=0.5).then_inc(tanh_done, 1)

            def result(n, m, used):
                act.wait_ge(block_used, used)
                if not isinstance(m, int) or m >= 2:
                    act.wait_ge(added, m * 16 - 16)
                copy(y_out[0:ROWS, n % 2, 0:512], ps[4][0:ROWS, :])
                copy(y_out[0:ROWS, n % 2, 512:1024], ps[6][0:ROWS, :]).then_inc(y_ready, 1)

            def expert(n, m, u, round0, start=False, last=False):
                q, blocks = BLOCKS * n + LEAD, ahead(n, last)
                act.wait_ge(hidT_done, m + 1)
                copy(hidT[:, n % 2, 0, :], ps[3][:, 0:2 * ROWS]).then_inc(hidT_high, 1)
                if not start:
                    result(n + 1, m - 1, u + 2)
                for j in range(min(blocks, 2)):
                    high(q + j, u + (LEAD + j), round0)
                if not last or n + 1 < TURN:
                    gate_tanh_of(n + 1, m + 1, u + 4)
                if not last or n + 2 < TURN:
                    high_tokens(n + 2, m + 2)
                if blocks > 2:
                    high(q + 2, u + (LEAD + 2), round0)

            def expert_pass(m0, u0, rounds, between=None):
                if between:
                    between()
                else:
                    high(0, u0, rounds)
                    high(1, u0 + 1, rounds)
                high_tokens(0, m0)
                high(2, u0 + 2, rounds)
                high(3, u0 + 3, rounds)
                gate_tanh_of(0, m0, u0 + 2)
                high_tokens(1, m0 + 1)
                high(4, u0 + 4, rounds)
                for n in range(TURN):
                    expert(n, m0 + n, u0 + BLOCKS * n, rounds, start=n == 0)
                with act.Fori(1, E // TURN - 1) as g:
                    for n in range(TURN):
                        expert(n, m0 + (g * TURN + n), u0 + (g * (BLOCKS * TURN) + BLOCKS * n), rounds + g * 2)
                last = E - TURN
                for n in range(TURN):
                    expert(n, m0 + (last + n), u0 + BLOCKS * (last + n), rounds + last // 2, last=True)
                result(TURN - 1, m0 + (E - 1), u0 + BLOCKS * E)

            expert_pass(0, 0, 0, shared)
            fullest = act.value_load(most_i[0:1, 0:1], min_val=0, max_val=T)
            with act.If(fullest > ROWS):
                with act.Fori(1, PASSES) as r:
                    with act.If(fullest > r * ROWS):
                        expert_pass(r * E, r * (BLOCKS * E), r * (E // 2))

        @block.vector
        def _(dve):
            v = nc.vector
            steps = [0]

            def then(ins):
                steps[0] += 1
                ins.then_inc(v_step, 1)
                dve.wait_ge(v_step, steps[0])

            def low_block(w):
                dve.wait_ge(front_high, w + 1)
                high_part, low_part = split_block(w)
                v.tensor_tensor(low_part, raw_block(w), high_part.bitcast(F32), ALU.subtract).then_inc(front_low, 1)

            def feature_major(f):
                dve.wait_ge(f_high, f + 1)
                parts, k, width = (hT, f, T) if f < KD else (memT, f - KD, M)
                v.scalar_tensor_tensor(parts[1][:, k, :], ps[4 + f % 4][:, 0:width], gains[:, f:f + 1],
                                       parts[0][:, k, :].bitcast(F32), ALU.mult, ALU.subtract).then_inc(f_low, 1)

            dve.wait_ge(x_rooted, 1)
            then(v.reciprocal(small[:, 12:16], small[:, 6:10]))
            for t in range(NT):
                v.tensor_scalar(xn[:, t, :], x_tok[:, t, :], small[:, 12 + t:13 + t], None, ALU.mult).then_inc(x_normed, 1)
            dve.wait_ge(gains_out, 1)
            then(v.tensor_tensor(lb[:, 4:6], gains[:, 20:22], gains[:, 22:24], ALU.max))
            then(v.tensor_tensor(lb[:, 0:2], gains[:, 20:22], lb[:, 4:6], ALU.subtract))
            v.tensor_tensor(lb[:, 2:4], gains[:, 22:24], lb[:, 4:6], ALU.subtract).then_inc(lb_in_exp, 1)
            low_block(0)
            for f in range(KD):
                feature_major(f)
            low_block(1)
            for column in (16, 18):
                then(v.tensor_scalar(gains[:, column:column + 1], gains[:, column:column + 1], HD ** -0.5, None, ALU.mult))
            dve.wait_ge(lb_exp, 1)
            then(v.tensor_tensor(lb[:, 4:6], lb[:, 0:2], lb[:, 2:4], ALU.add))
            then(v.reciprocal(lb[:, 6:8], lb[:, 4:6]))
            then(v.tensor_tensor(lb[:, 4:6], lb[:, 0:2], lb[:, 6:8], ALU.mult))
            then(v.tensor_scalar(lb[:, 6:8], lb[:, 4:6], -1.0, 1.0, ALU.mult, ALU.add))
            dve.wait_ge(x_rooted, 2)
            then(v.reciprocal(small[:, 16:18], small[:, 10:12]))
            for t in range(NM):
                v.tensor_scalar(mem[:, t, :], mem[:, t, :], small[:, 16 + t:17 + t], None, ALU.mult).then_inc(mem_normed, 1)
            low_block(2)
            for f in range(KD, 2 * KD):
                feature_major(f)
            low_block(3)
            dve.wait_ge(f_exp, 1)
            then(v.tensor_scalar(expo[0][:, :, :], expo[0][:, :, :], 1.0, None, ALU.add))
            then(v.reciprocal(kT[:, :, :], expo[0][:, :, :]))
            for b in range(2):
                ins = v.tensor_scalar(fT[:, b, :], kT[:, b, :], lb[:, 6 + b:7 + b], lb[:, 4 + b:5 + b], ALU.mult, ALU.add)
                then(ins)
            then(v.tensor_scalar(kT[:, :, :], fT[:, :, :], -1.0, 1.0, ALU.mult, ALU.add))
            v.tensor_copy(small[:, 310:311], small[:, 0:1]).then_inc(f_ready, 1)
            dve.wait_ge(q_tanh, 1)
            then(v.scalar_tensor_tensor(qT[:, :, :], expo[1][:, :, :], 1.0, qT[:, :, :], ALU.add, ALU.mult))
            then(v.tensor_scalar(qT[:, :, :], qT[:, :, :], 0.5 * HD ** -0.5, None, ALU.mult))
            dve.wait_ge(log_ready, 1)
            dve.wait_ge(c_in[0], 16)
            for b in range(2):
                for c in range(NT):
                    last = v.tensor_tensor_scan(bT[:, b, c * P:(c + 1) * P], ones, fT[:, b, c * P:(c + 1) * P],
                                                0.0, ALU.mult, ALU.add)
            then(last)

            def differences(j):
                m = 1 << (LEVELS - 1 - j) if j < LEVELS else P // 2
                ref = m - 1 if j < LEVELS else P - 1
                b_v = bT.rearrange("p b (n m) -> p (b n) m", m=2 * m)
                e_v = expo[j % 2].rearrange("p b (n m) -> p (b n) m", m=2 * m)
                n = 2 * T // (2 * m)
                v.tensor_tensor(e_v, b_v, bcast(b_v[:, :, ref:ref + 1], P, n, 2 * m), ALU.subtract).then_inc(diff_ready, 1)

            def products(j):
                dve.wait_ge(expo_ready, 2 * (j + 1))
                if 2 <= j < LEVELS + 1:
                    dve.wait_ge(level_done, 4 * (j - 1))
                elif j == LEVELS + 1:
                    dve.wait_ge(level_done, 4 * (j - 2))
                if j < LEVELS:
                    m = 1 << (LEVELS - 1 - j)
                    e_v, o_v, k_v, q_v = (a.rearrange("p b (n m) -> p (b n) m", m=2 * m) for a in (expo[j % 2], kq[j % 2], kT, qT))
                    then(v.tensor_tensor(o_v[:, :, 0:m], e_v[:, :, 0:m], k_v[:, :, 0:m], ALU.mult))
                    v.tensor_tensor(o_v[:, :, m:2 * m], e_v[:, :, m:2 * m], q_v[:, :, m:2 * m], ALU.mult).then_inc(kq_ready, 1)
                else:
                    v.tensor_tensor(kq[j % 2][:, :, :], expo[j % 2][:, :, :], (kT if j == LEVELS else qT)[:, :, :],
                                    ALU.mult).then_inc(kq_ready, 1)

            def take_level(j):
                if j > 0:
                    reach = 1 << (LEVELS - j)
                    then(v.tensor_scalar(mask[:, j % 2, :].bitcast(I32), level, float(reach), None, ALU.is_lt))
                for c in range(NT):
                    dve.wait_ge(level_done, 4 * j + c + 1)
                    src = view(ps[4 + c][:, :], 4, P)
                    if j == 0:
                        v.scalar_tensor_tensor(scores[:, 4 * c:4 * c + 4, :], bcast(level[:, None, :], P, 4, P), float(P), src,
                                               ALU.is_lt, ALU.mult).then_inc(level_taken, 1)
                    else:
                        m_v = mask[:, j % 2, :].bitcast(I32)
                        v.copy_predicated(scores[:, 4 * c:4 * c + 4, :], bcast(m_v[:, None, :], P, 4, P), src).then_inc(level_taken, 1)
                dve.wait_ge(level_taken, 4 * (j + 1))

            differences(0)
            differences(1)
            products(0)
            dve.wait_ge(unit_out, number["bias", 5] + 1)
            then(v.memset(state[:, :, :, :], 0.0))
            q_sq, k_sq = view(c_sq[:, 0:1024], NT, CW), view(c_sq[:, 1024:1536], NM, CW)
            for g in range(1, len(groups)):
                low_block(2 * g + 2)
                if g < len(groups) - 1:
                    low_block(2 * g + 3)
                if g <= 2:
                    a, name = ((qa, "qa"), (ka, "ka"))[g - 1]
                    dve.wait_ge(unit_out, number[name, NT - 1] + 1)
                    then(v.tensor_tensor(squares[:, g - 1, :, :], a[:, :, :], a[:, :, :], ALU.mult))
                    v.tensor_reduce(small[:, 24 * g - 4:24 * g + 20], squares[:, g - 1, :, :].rearrange("p t (h e) -> p (t h) e", e=HD),
                                    AX.X, ALU.add).then_inc(qk_summed, 1)
                take_level(g - 1)
                products(g)
                if g + 1 <= LEVELS:
                    differences(g + 1)
                if g == 4:
                    dve.wait_ge(qk_rooted, 1)
                    then(v.reciprocal(small[:, 116:164], small[:, 68:116]))
                if g == 6:
                    dve.wait_ge(og_tanh, 1)
                    then(v.scalar_tensor_tensor(o_gate[:, :, :], o_gate[:, :, :], 1.0, og[:, :, :], ALU.add, ALU.mult))
                    dve.wait_ge(c_in[7], 16)
                    then(v.tensor_tensor(o_gate[:, :, :], o_gate[:, :, :], bcast(out_norm[:, None, :], P, NT, BV), ALU.mult))
                    then(v.tensor_tensor(k_sq, kv[:, :, 0:CW], kv[:, :, 0:CW], ALU.mult))
                    v.tensor_reduce(small[:, 228:236], k_sq.rearrange("p t (h e) -> p (t h) e", e=HD), AX.X, ALU.add).then_inc(c_summed, 1)
            products(LEVELS + 1)
            take_level(LEVELS)
            dve.wait_ge(unit_out, group_done(len(groups) - 1))
            then(v.tensor_tensor(q_sq, qc[:, :, :], qc[:, :, :], ALU.mult))
            v.tensor_reduce(small[:, 212:228], q_sq.rearrange("p t (h e) -> p (t h) e", e=HD), AX.X, ALU.add).then_inc(c_summed, 1)
            for c in range(NT - 1):
                dve.wait_ge(inc_done, c + 1)
                for b in range(2):
                    for hh in range(2):
                        rows = slice(hh * HD, (hh + 1) * HD)
                        col = b * 2 * VD + hh * VD
                        inc = ps[4 + c][rows, col:col + VD]
                        cols = slice(hh * VD, (hh + 1) * VD)
                        if c == 0:
                            ins = v.tensor_copy(state[rows, 0, b, cols], inc)
                        else:
                            ins = v.scalar_tensor_tensor(state[rows, c, b, cols], state[rows, c - 1, b, cols],
                                                         expo[(LEVELS + 1) % 2][rows, b, c * P + P - 1:c * P + P], inc,
                                                         ALU.mult, ALU.add)
                        if hh == 0:
                            then(ins)
                        else:
                            ins.then_inc(state_ready, 1)
                dve.wait_ge(state_ready, 2 * (c + 1))
            low_block(2 * len(groups) + 1)
            for c in range(NT):
                dve.wait_ge(unit_out, number["o", c] + 1)
                then(v.tensor_tensor(o_sq[:, c, :], o_tok[:, c, :], o_tok[:, c, :], ALU.mult))
                v.tensor_reduce(small[:, 164 + 4 * c:168 + 4 * c], o_sq[:, c, :].rearrange("p (h e) -> p h e", e=VD), AX.X,
                                ALU.add).then_inc(o_summed, 1)
            dve.wait_ge(c_rooted, 1)
            then(v.reciprocal(small[:, 260:284], small[:, 236:260]))
            dve.wait_ge(o_rooted, 1)
            then(v.reciprocal(small[:, 196:212], small[:, 180:196]))
            o_v = o_tok.rearrange("p t (h e) -> p (t h) e", e=VD)
            then(v.tensor_tensor(o_v, o_v, bcast(small[:, 196:212, None], P, 16, VD), ALU.mult))
            then(v.scalar_tensor_tensor(ib[:, :, :], o_tok[:, :, :], 0.5, o_gate[:, :, :], ALU.mult, ALU.mult))

            def attention(i, dilated, base):
                pairs = 0 if dilated else A_PAIRS
                n0 = i * UNITS + pairs * UNITS
                k = [0]

                def then(ins):
                    k[0] += 1
                    ins.then_inc(v_step, 1)
                    dve.wait_ge(v_step, base + k[0])

                q_src, k_src = (qa, ka) if dilated else (qc, kv)
                heads = 6 if dilated else 4
                roots = [(small[:, 116:140], small[:, 140:164]), (small[:, 260:276], small[:, 276:284])][not dilated]
                for which, (src, root) in enumerate(zip((q_src, k_src), roots)):
                    tiles = NM if which and not dilated else NT
                    o_v = staging[:, which, 0:tiles, :].rearrange("p t (h e) -> p t h e", e=HD)
                    for t in range(tiles):
                        s_v = src[:, t, bass.ds(i * P, P)].rearrange("p (h e) -> p h e", e=HD)
                        r_v = root[:, bass.ds(i * 2 + t * heads, 2)]
                        v.tensor_tensor(o_v[:, t], s_v, bcast(r_v.unsqueeze(2), P, 2, HD), ALU.mult).then_inc(staged, 1)

                def maximum(j):
                    keys = (j % NT + 1) * P if dilated else M
                    dve.wait_ge(qk_done, n0 + (j + 1))
                    src = ps[2 + j % 2][:, 0:keys]
                    if dilated:
                        start = (NT - 1 - j % NT) * P
                        table_h = bias[:, bass.ds(i * 2 + j // NT, 1), start:T].rearrange("p a b -> p (a b)")
                        then(v.tensor_tensor(logits[:, j % 2, 0:keys], src, table_h, ALU.add))
                        src = logits[:, j % 2, 0:keys]
                    v.tensor_reduce(small[:, 284 + j % 2:285 + j % 2], src, AX.X, ALU.max, negate=True).then_inc(max_ready, 1)

                def gate(j):
                    if dilated:
                        dve.wait_ge(gate_tanh, n0 + (j + 1))
                        v.tensor_scalar(gates[:, bass.ds(i * UNITS + j, 1), :].rearrange("p a b -> p (a b)"),
                                        ps[6 + j % 2][:, :], 0.5, 0.5, ALU.mult, ALU.add).then_inc(gate_out, 1)

                gate(0)
                maximum(0)
                for j in range(UNITS):
                    if j + 1 < UNITS:
                        maximum(j + 1)
                        gate(j + 1)
                    dve.wait_ge(exp_done, n0 + (j + 1))
                    then(v.reciprocal(small[:, 292 + j % 2:293 + j % 2], small[:, 288 + j % 2:289 + j % 2]))
                    dve.wait_ge(pv_done, n0 + (j + 1))
                    dst = q_src[:, j % NT, bass.ds(i * P + (j // NT) * HD, HD)]
                    v.tensor_scalar(dst, ps[j % 2][:, 0:HD], small[:, 292 + j % 2:293 + j % 2], None,
                                    ALU.mult).then_inc(y_done, 1)
                    if dilated and j % 2 == 0:
                        q = j // 2
                        dve.wait_ge(front_high, i * 4 + (G0 + 2 + q + 1))
                        high_part, low_part = split_block(G0 + q)
                        v.tensor_tensor(low_part, raw_block(G0 + q), high_part.bitcast(F32), ALU.subtract).then_inc(front_low, 1)
                return k[0]

            a_turn, c_turn = 2 * UNITS, UNITS
            with dve.Fori(0, A_PAIRS) as i:
                assert attention(i, True, i * a_turn + steps[0]) == a_turn
            steps[0] += A_PAIRS * a_turn
            with dve.Fori(0, C_PAIRS) as i:
                assert attention(i, False, i * c_turn + steps[0]) == c_turn
            steps[0] += C_PAIRS * c_turn

            for k in range(KD):
                dve.wait_ge(yT_high, k + 1)
                v.tensor_tensor(yT[1][:, k, :], ps[k % 4][:, :], yT[0][:, k, :].bitcast(F32), ALU.subtract).then_inc(yT_low, 1)
            dve.wait_ge(router_high, 1)
            v.tensor_tensor(routerT[1], w_router, routerT[0].bitcast(F32), ALU.subtract).then_inc(router_low, 1)

            def low_mixed(m):
                dve.wait_ge(mixT_high, m + 1)
                v.tensor_tensor(mixT[1][m], gates[:, KD + m, :], mixT[0][m].bitcast(F32), ALU.subtract).then_inc(mixT_low, 1)
                if m % 2:
                    low_block(B0 + m // 2 + 2)

            for m in range(KD):
                for br in range(3):
                    n = 3 * m + br
                    dve.wait_ge(mix_done, n + 1)
                    g = gates[:, br * KD + m, :]
                    v.tensor_tensor(g, g, ps[4 + n % 4][:, :], ALU.mult).then_inc(mix_taken, 1)
                dve.wait_ge(mix_taken, 3 * m + 3)
                then(v.tensor_tensor(gates[:, KD + m, :], gates[:, m, :], gates[:, KD + m, :], ALU.add))
                v.tensor_tensor(gates[:, KD + m, :], gates[:, KD + m, :], gates[:, 2 * KD + m, :], ALU.add).then_inc(mixed, 1)
                if m > 0:
                    low_mixed(m - 1)
            low_mixed(KD - 1)

            def residual(half, t):
                dve.wait_ge(x1_done, NT * half + t + 1)
                x_v = x_tok[:, t, half * 512:(half + 1) * 512]
                v.tensor_tensor(x_v, x_v, ps[NT * half + t][:, :], ALU.add).then_inc(x1_ready, 1)

            def second_norm(t):
                dve.wait_ge(x1_rooted, t + 1)
                then(v.reciprocal(small[:, 12 + t:13 + t], small[:, 6 + t:7 + t]))
                v.scalar_tensor_tensor(u_tok[:, t, :], x_tok[:, t, :], small[:, 12 + t:13 + t], ffn_gain, ALU.mult,
                                       ALU.mult).then_inc(u_ready, 1)

            low_block(O0 + 2)
            dve.wait_ge(x_again, 16)
            for t in range(NT):
                residual(0, t)
            low_block(O0 + 3)
            low_block(S0)
            dve.wait_ge(c_in[11], 16)
            for t in range(NT):
                residual(1, t)
                if t > 0:
                    second_norm(t - 1)
            second_norm(NT - 1)
            for t in range(NT):
                for half in range(2):
                    dve.wait_ge(uT_high, 2 * t + half + 1)
                    high_part, low_part = (part[:, 4 * half:4 * half + 4, t * P:(t + 1) * P] for part in uT)
                    v.tensor_tensor(low_part, view(ps[2 * (t % 2) + half][:, :], 4, P), high_part.bitcast(F32),
                                    ALU.subtract).then_inc(uT_low, 1)
            low_block(S0 + 1)

            def shared_hidden(t):
                dve.wait_ge(s_tanhed, t + 1)
                then(v.scalar_tensor_tensor(s_hid[:, t, :], s_hid[:, t, :], 1.0, ps[t][:, 0:FH], ALU.add, ALU.mult))
                v.scalar_tensor_tensor(s_hid[:, t, :], s_hid[:, t, :], 0.5, ps[t][:, FH:2 * FH], ALU.mult,
                                       ALU.mult).then_inc(s_hidden, 1)

            def shared():
                def take_down(t):
                    for half in range(2):
                        dve.wait_ge(s_down, 2 * t + half + 1)
                        x_v = x_tok[:, t, half * 512:(half + 1) * 512]
                        ins = v.tensor_tensor(x_v, x_v, ps[(2 * t + half) % 4][:, :], ALU.add)
                        if half:
                            ins.then_inc(out_ready, 1)
                        else:
                            then(ins)

                for t in range(NT):
                    if t < 2:
                        low(t, t)
                    if t > 0:
                        take_down(t - 1)
                take_down(NT - 1)

            dve.wait_ge(r_turned, 1)
            dve.wait_ge(c_in[9], 32)
            r_ps = view(ps[5][:, 0:NT * E], NT, E)
            then(v.tensor_scalar(score, r_ps, 0.5, 0.5, ALU.mult, ALU.add))
            then(v.tensor_tensor(choice, score, bcast(router_bias[:, None, :], P, NT, E), ALU.add))
            best = view(rs[:, 0:256], NT * GROUPS, 8)
            for n in range(NT * GROUPS):
                t, g = divmod(n, GROUPS)
                last = v.max(best[:, n, :], choice[:, t, g * 8:(g + 1) * 8])
            then(last)
            group_score = view(rs[:, 256:288], NT, GROUPS)
            then(v.tensor_tensor(rs[:, 256:288], best[:, :, 0:1].rearrange("p n a -> p (n a)"),
                                 best[:, :, 1:2].rearrange("p n a -> p (n a)"), ALU.add))
            group_top, group_at = view(rs[:, 288:320], NT, 8), view(rs[:, 320:352], NT, 8)
            for t in range(NT):
                last = v.max(group_top[:, t, :], group_score[:, t, :])
            then(last)
            for t in range(NT):
                last = v.max_index(group_at[:, t, :].bitcast(U32), group_top[:, t, :], group_score[:, t, :])
            then(last)
            group_f = view(rs[:, 352:384], NT, 8)
            then(v.tensor_copy(rs[:, 352:384], rs[:, 320:352].bitcast(U32)))
            group_hit = view(rs[:, 384:512], NT, GROUPS, TOP_GROUPS)
            for t in range(NT):
                last = v.tensor_tensor(group_hit[:, t], bcast(counting[:, 0:GROUPS, None], P, GROUPS, TOP_GROUPS),
                                       bcast(group_f[:, t, None, 0:TOP_GROUPS], P, GROUPS, TOP_GROUPS), ALU.is_equal)
            then(last)
            group_mask = view(rs[:, 512:544], NT, GROUPS)
            then(v.tensor_reduce(rs[:, 512:544], group_hit.rearrange("p t g k -> p (t g) k"), AX.X, ALU.add))
            then(v.tensor_scalar(rs[:, 544:576], rs[:, 512:544], -MASKED, MASKED, ALU.mult, ALU.add))
            m_v, c_v = (a.rearrange("p t (g k) -> p (t g) k", k=8) for a in (masked, choice))
            then(v.tensor_tensor(m_v, c_v, bcast(rs[:, 512:544, None], P, 32, 8), ALU.mult))
            then(v.tensor_tensor(m_v, m_v, bcast(rs[:, 544:576, None], P, 32, 8), ALU.add))
            top8 = view(rs[:, 576:608], NT, 8)
            for t in range(NT):
                last = v.max(top8[:, t, :], masked[:, t, :])
            then(last)
            for t in range(NT):
                last = v.match_replace(masked2[:, t, :], top8[:, t, :], masked[:, t, :], 3 * MASKED)
            then(last)
            v.tensor_scalar(picked, masked2, 2 * MASKED, None, ALU.is_lt).then_inc(picked_ready, 1)
            dve.wait_ge(picked_ready, 1)
            then(v.tensor_tensor(weight, score, picked, ALU.mult))
            then(v.tensor_reduce(rs[:, 608:612], weight, AX.X, ALU.add))
            then(v.reciprocal(rs[:, 612:616], rs[:, 608:612]))
            then(v.tensor_scalar(rs[:, 612:616], rs[:, 612:616], ROUTED_SCALE, None, ALU.mult))
            then(v.memset(route_in.bitcast(F32), 0.0))
            for t in range(NT):
                v.tensor_scalar(route_in[:, t, :, 0], picked[:, t, :], 0.0, rs[:, 616 + t:617 + t], ALU.mult, ALU.add)
                last = v.tensor_scalar(weight[:, t, :], weight[:, t, :], rs[:, 612 + t:613 + t], 0.5, ALU.mult, ALU.mult)
            then(last)
            then(v.tensor_copy(route_in[:, :, :, 1], weight))
            then(v.tensor_tensor(route_in[:, :, :, 2], weight, route_in[:, :, :, 1].bitcast(F32), ALU.subtract))
            dve.wait_ge(place_done, 1)
            p_v = view(ps[4][:, 256:256 + NT * E], NT, E)
            then(v.scalar_tensor_tensor(place, p_v, 1.0, picked, ALU.add, ALU.mult))
            then(v.tensor_scalar(place, place, -1.0, None, ALU.add))
            then(v.tensor_reduce(most, ps[5][:, 256:256 + E], AX.X, ALU.max))
            v.tensor_copy(most_i, most).then_inc(routed, 1)
            def low(q, u):
                dve.wait_ge(high_done, u + 1)
                both = split[q % SPLIT]
                v.tensor_tensor(both[:, 1], raw[q % RAW], both[:, 0].bitcast(F32), ALU.subtract).then_inc(low_done, 1)

            def low_tokens(n, m):
                for half in range(2):
                    dve.wait_ge(gT_high, m * 2 + half + 1)
                    parts = gatheredT[:, n % 2, :, 4 * half:4 * half + 4, :]
                    v.tensor_tensor(parts[:, 1], view(ps[half][:, 0:4 * ROWS], 4, ROWS), parts[:, 0].bitcast(F32),
                                    ALU.subtract).then_inc(gT_low, 1)

            def read_route(n, m):
                dve.wait_ge(route_done, m + 1)
                if not isinstance(m, int) or m >= 4:
                    dve.wait_ge(gT_done, m - 3)
                v.tensor_reduce(slot_w[0:ROWS, n % 4:n % 4 + 1], ps[7][0:ROWS, 1:3], AX.X, ALU.add)
                v.tensor_scalar(index[0:ROWS, n % 4:n % 4 + 1], ps[7][0:ROWS, 0:1], NO_TOKEN, None,
                                ALU.add).then_inc(index_ready, 1)

            def choose(n, m, e):
                if not isinstance(m, int) or m >= 2:
                    dve.wait_ge(route_done, m - 1)
                v.tensor_tensor(select[:, n % 2, :, :], bcast(counting[:, None, 0:ROWS], P, NT, ROWS),
                                bcast(place[:, :, bass.ds(e, 1)], P, NT, ROWS), ALU.is_equal).then_inc(sel_ready, 1)

            def hidden(n, m):
                bank = ps[2 + 3 * (n % 2)]
                dve.wait_ge(tanh_done, m + 1)
                v.scalar_tensor_tensor(e_act[0:ROWS, n % 2, :], e_tanh[0:ROWS, n % 2, :], 1.0, bank[0:ROWS, 0:FH], ALU.add,
                                       ALU.mult).then_inc(act_ready, 1)
                if not isinstance(m, int) or m >= 4:
                    dve.wait_ge(added, m * 16 - 48)
                v.tensor_copy(add_index[0:ROWS, n % 4:n % 4 + 1], index[0:ROWS, n % 4:n % 4 + 1])
                dve.wait_ge(act_ready, m + 1)
                v.scalar_tensor_tensor(hid[0:ROWS, n % 2, :], e_act[0:ROWS, n % 2, :], slot_w[0:ROWS, n % 4:n % 4 + 1],
                                       bank[0:ROWS, FH:2 * FH], ALU.mult, ALU.mult).then_inc(hid_ready, 1)

            def expert(n, m, e, u, last=False):
                q, blocks = BLOCKS * n + LEAD, ahead(n, last)
                dve.wait_ge(hidT_high, m + 1)
                parts = hidT[:, n % 2, :, :]
                v.tensor_tensor(parts[:, 1], ps[3][:, 0:2 * ROWS], parts[:, 0].bitcast(F32), ALU.subtract).then_inc(hidT_low, 1)
                if blocks > 0:
                    low(q, u + LEAD)
                if not last or n + 3 < TURN:
                    read_route(n + 3, m + 3)
                if not last:
                    choose(n + 4, m + 4, e + 4)
                if blocks > 1:
                    low(q + 1, u + (LEAD + 1))
                if not last or n + 1 < TURN:
                    hidden(n + 1, m + 1)
                if not last or n + 2 < TURN:
                    low_tokens(n + 2, m + 2)
                if blocks > 2:
                    low(q + 2, u + (LEAD + 2))

            def expert_pass(m0, u0, between=None):
                choose(0, m0, 0)
                choose(1, m0 + 1, 1)
                if between:
                    shared_hidden(0)
                    shared_hidden(1)
                read_route(0, m0)
                read_route(1, m0 + 1)
                choose(2, m0 + 2, 2)
                if between:
                    shared_hidden(2)
                    shared_hidden(3)
                    between()
                else:
                    low(0, u0)
                    low(1, u0 + 1)
                low_tokens(0, m0)
                read_route(2, m0 + 2)
                choose(3, m0 + 3, 3)
                low(2, u0 + 2)
                low(3, u0 + 3)
                hidden(0, m0)
                low_tokens(1, m0 + 1)
                low(4, u0 + 4)
                for n in range(TURN):
                    expert(n, m0 + n, n, u0 + BLOCKS * n)
                with dve.Fori(1, E // TURN - 1) as g:
                    for n in range(TURN):
                        expert(n, m0 + (g * TURN + n), g * TURN + n, u0 + (g * (BLOCKS * TURN) + BLOCKS * n))
                last = E - TURN
                for n in range(TURN):
                    expert(n, m0 + (last + n), last + n, u0 + BLOCKS * (last + n), True)

            expert_pass(0, 0, shared)
            fullest = dve.value_load(most_i[0:1, 0:1], min_val=0, max_val=T)
            with dve.If(fullest > ROWS):
                with dve.Fori(1, PASSES) as r:
                    with dve.If(fullest > r * ROWS):
                        v.tensor_scalar(place, place, -float(ROWS), None, ALU.add).then_inc(v_step, 1)
                        dve.wait_ge(v_step, r + steps[0])
                        expert_pass(r * E, r * (BLOCKS * E))

        @block.tensor
        def _(pe):
            mm = nc.tensor.matmul
            tr = nc.tensor.transpose

            def products(bank, left, right, first, last):
                for q, (a, b) in enumerate(((0, 0), (1, 0), (0, 1))):
                    ins = mm(bank, left[a], right[b], start=first and q == 0, stop=last and q == 2)
                return ins

            def feature_major(f):
                if f >= 4:
                    pe.wait_ge(f_low, f - 3)
                src, tiles, k = (xn, NT, f) if f < KD else (mem, NM, f - KD)
                for t in range(tiles):
                    last = tr(ps[4 + f % 4][:, t * P:(t + 1) * P], src[:, t, k * P:(k + 1) * P], ident)
                last.then_inc(f_done, 1)

            def group(g, n):
                name, _, width = groups[g]
                tiles = tiles_of.get(name, NT)
                for kh in range(2):
                    pe.wait_ge(front_low, 2 * g + kh + 1)
                    weights = split_block(2 * g + kh)
                    for t in range(tiles):
                        bank = ps[(n + t) % 4]
                        if kh == 0:
                            if n + t >= 4:
                                pe.wait_ge(unit_out, n + t - 3)
                            elif n + t == 3:
                                pe.wait_ge(gains_out, 1)
                        for kk in range(4):
                            k = 4 * kh + kk
                            if g == 0:
                                left, right = [w[:, kk, t * P:(t + 1) * P] for w in weights], [part[:, k, :] for part in hT]
                            else:
                                left = [part[:, k, t * P:(t + 1) * P] for part in (memT if name == "kv" else hT)]
                                right = [w[:, kk, :] for w in weights]
                            last = products(bank[:, 0:width], left, right, k == 0, k == KD - 1)
                        if kh == 1:
                            last.then_inc(unit_done, 1)
                    if kh == 0:
                        last.then_inc(front_used, 1)

            pe.wait_ge(c_in[0], 16)
            pe.wait_ge(c_in[1], 16 * 11)
            tr(ps[3][:, 0:24], gain_rows[0:24, :], ident[0:24, 0:24]).then_inc(gains_done, 1)
            pe.wait_ge(c_in[5], 16)
            pe.wait_ge(c_in[6], 16)
            pe.wait_ge(c_in[8], 2)
            n = 0
            for kind, k in plan:
                if kind == "group":
                    if k == 0:
                        pe.wait_ge(x_normed, NT)
                        for f in range(KD):
                            feature_major(f)
                        pe.wait_ge(f_low, KD)
                    elif groups[k][0] == "kv":
                        pe.wait_ge(f_low, 2 * KD)
                    group(k, n)
                    n += tiles_of.get(groups[k][0], NT)
                    if k == 0:
                        pe.wait_ge(mem_normed, NM)
                        for f in range(KD, 2 * KD):
                            feature_major(f)
                    continue
                if kind == "level":
                    left, right = (kT, qT) if k == LEVELS else (kq[k % 2], kq[k % 2])
                    if k == 0:
                        pe.wait_ge(f_low, 2 * KD)
                    if k < LEVELS:
                        pe.wait_ge(kq_ready, k + 1)
                    for q in range(4):
                        if k > 0:
                            pe.wait_ge(level_taken, 4 * (k - 1) + q + 1)
                        rows = slice(q % 2 * HD, (q % 2 + 1) * HD)
                        for z in range(4):
                            b, c = z % 2, q // 2 * 2 + z // 2
                            last = mm(ps[4 + q][:, z * P:(z + 1) * P], left[rows, b, c * P:(c + 1) * P],
                                      right[rows, b, c * P:(c + 1) * P], start=True, stop=True)
                        last.then_inc(level_done, 1)
                    continue
                if kind == "increments":
                    pe.wait_ge(unit_out, number["kdT", 1] + 1)
                    pe.wait_ge(level_taken, 4 * (LEVELS + 1))
                    for c in range(NT - 1):
                        for b in range(2):
                            last = mm(ps[4 + c][:, b * 2 * VD:(b + 1) * 2 * VD], kdT[:, b, c * P:(c + 1) * P],
                                      ib[:, c, b * 2 * VD:(b + 1) * 2 * VD], start=True, stop=True)
                        last.then_inc(inc_done, 1)
                    continue
                bank = ps[n % 4]
                if n >= 4:
                    pe.wait_ge(unit_out, n - 3)
                if kind == "table":
                    lo, hi = k * T, min(SPAN, (k + 1) * T)
                    last = mm(bank[0:6, 0:hi - lo], rel[0:33, :], bucket[0:33, lo:hi], start=True, stop=True)
                elif kind == "bias":
                    if k == 0:
                        pe.wait_ge(hankel_in, 16 * 6)
                    last = mm(bank[:, :], flip, hankel[:, k, :], start=True, stop=True)
                elif kind == "kdT":
                    if k == 0:
                        pe.wait_ge(kq_ready, LEVELS + 1)
                    for c in range(NT - 1):
                        last = tr(bank[:, c * P:(c + 1) * P], kq[LEVELS % 2][:, k, c * P:(c + 1) * P], ident)
                elif kind == "o":
                    pe.wait_ge(kq_ready, LEVELS + 2)
                    if k > 0:
                        pe.wait_ge(state_ready, 2 * k)
                    for b in range(2):
                        if k > 0:
                            mm(bank[:, b * 2 * VD:(b + 1) * 2 * VD], kq[(LEVELS + 1) % 2][:, b, k * P:(k + 1) * P],
                               state[:, k - 1, b, :], start=True, stop=False)
                        for hh in range(2):
                            h = 2 * b + hh
                            last = mm(bank[:, h * VD:(h + 1) * VD], scores[:, score_at(k, h), :],
                                      ib[:, k, h * VD:(h + 1) * VD], start=k == 0, stop=k == 0 or hh == 1)
                last.then_inc(unit_done, 1)
                n += 1

            def attention(i, dilated):
                pairs = 0 if dilated else A_PAIRS
                n0 = i * UNITS + pairs * UNITS
                k_tiles = NT if dilated else NM
                width = k_tiles * P

                def gate(j, part):
                    if not dilated:
                        return
                    if part == 0:
                        if j % 2 == 0:
                            pe.wait_ge(front_low, i * 4 + (G0 + j // 2 + 1))
                        if j >= 2:
                            pe.wait_ge(gate_out, n0 + (j - 1))
                    weights = split_block(G0 + j // 2)
                    for kk in range(part * KD // 2, (part + 1) * KD // 2):
                        last = products(ps[6 + j % 2][:, :], [w[:, kk, (j % 2) * P:(j % 2 + 1) * P] for w in weights],
                                        [part_[:, kk, :] for part_ in hT], kk == 0, kk == KD - 1)
                    if part == 1:
                        last.then_inc(gate_done, 1)

                gate(0, 0)
                pe.wait_ge(staged, (i * (2 * NT) if dilated else i * (NT + NM)) + (A_PAIRS * 2 * NT * (not dilated) + NT + k_tiles))
                for which, tiles in ((0, NT), (1, k_tiles)):
                    for t in range(tiles):
                        last = tr(ps[which][:, t * P:(t + 1) * P], staging[:, which, t, :], ident)
                last.then_inc(pair_done, 1)

                def scores_of(j):
                    hh, t = divmod(j, NT)
                    keys = (t + 1) * P if dilated else M
                    rows = slice(hh * HD, (hh + 1) * HD)
                    if j >= 2:
                        pe.wait_ge(max_ready if dilated else exp_done, n0 + (j - 1))
                    mm(ps[2 + j % 2][:, 0:keys], qkT[rows, 0, t * P:(t + 1) * P], qkT[rows, 1, 0:keys], start=True,
                       stop=True).then_inc(qk_done, 1)

                gate(0, 1)
                pe.wait_ge(pair_out, i * 2 + (2 * pairs + 2))
                scores_of(0)
                scores_of(1)
                for j in range(UNITS):
                    hh, t = divmod(j, NT)
                    if j + 1 < UNITS:
                        gate(j + 1, 0)
                    tiles = t + 1 if dilated else NM
                    pe.wait_ge(exp_done, n0 + (j + 1))
                    for kt in range(tiles):
                        last = tr(ps[4][:, kt * P:(kt + 1) * P], probs[:, j % 2, kt * P:(kt + 1) * P], ident)
                    last.then_inc(pT_done, 1)
                    if j + 2 < UNITS:
                        scores_of(j + 2)
                    if j + 1 < UNITS:
                        gate(j + 1, 1)
                    pe.wait_ge(pT_out, n0 + (j + 1))
                    if j >= 2:
                        pe.wait_ge(y_done, n0 + (j - 1))
                    for kt in range(tiles):
                        values = (va[:, kt, bass.ds(i * P + hh * HD, HD)] if dilated
                                  else kv[:, kt, bass.ds(i * P + (CW + hh * HD), HD)])
                        last = mm(ps[j % 2][:, 0:HD], probsT[:, j % 2, kt * P:(kt + 1) * P], values,
                                  start=kt == 0, stop=kt == tiles - 1)
                    last.then_inc(pv_done, 1)
                if dilated:
                    pe.wait_ge(gate_out, n0 + UNITS)

            with pe.Fori(0, A_PAIRS) as i:
                attention(i, True)
            with pe.Fori(0, C_PAIRS) as i:
                attention(i, False)

            pe.wait_ge(y_done, (A_PAIRS + C_PAIRS) * UNITS)
            pe.wait_ge(pT_out, (A_PAIRS + C_PAIRS) * UNITS)
            for k in range(KD):
                if k >= 4:
                    pe.wait_ge(yT_low, k - 3)
                src, col = (qa, k) if k < 3 else (ib, k - 3) if k < 6 else (qc, k - 6)
                for t in range(NT):
                    last = tr(ps[k % 4][:, t * P:(t + 1) * P], src[:, t, col * P:(col + 1) * P], ident)
                last.then_inc(yT_done, 1)
            for m in range(KD):
                if m % 2 == 0:
                    pe.wait_ge(front_low, B0 + m // 2 + 1)
                weights = split_block(B0 + m // 2)
                for br, (first, blocks) in enumerate(((0, 3), (3, 3), (6, 2))):
                    n = 3 * m + br
                    if m == 0:
                        pe.wait_ge(yT_low, first + blocks)
                    if n >= 4:
                        pe.wait_ge(mix_taken, n - 3)
                    for kk in range(first, first + blocks):
                        last = products(ps[4 + n % 4][:, :], [w[:, kk, (m % 2) * P:(m % 2 + 1) * P] for w in weights],
                                        [part[:, kk, :] for part in yT], kk == first, kk == first + blocks - 1)
                    last.then_inc(mix_done, 1)
            for half in range(2):
                if half == 1:
                    pe.wait_ge(mix_taken, 3 * KD)
                for kh in range(2):
                    w = O0 + 2 * half + kh
                    pe.wait_ge(front_low, w + 1)
                    if half == 0:
                        pe.wait_ge(mixT_low, 4 * kh + 4)
                    weights = split_block(w)
                    for t in range(NT):
                        for kk in range(4):
                            k = 4 * kh + kk
                            last = products(ps[NT * half + t][:, :], [part[k][:, t * P:(t + 1) * P] for part in mixT],
                                            [w[:, kk, :] for w in weights], k == 0, k == KD - 1)
                        if kh == 1:
                            last.then_inc(x1_done, 1)
                    if kh == 0:
                        last.then_inc(front_used, 1)
            pe.wait_ge(x1_ready, NT)
            for t in range(NT):
                pe.wait_ge(u_ready, t + 1)
                if t >= 2:
                    pe.wait_ge(uT_low, 2 * (t - 1))
                for k in range(KD):
                    last = tr(ps[2 * (t % 2) + k // 4][:, (k % 4) * P:(k % 4 + 1) * P], u_tok[:, t, k * P:(k + 1) * P], ident)
                last.then_inc(uT_done, 1)
            pe.wait_ge(router_low, 1)
            pe.wait_ge(x1_ready, 2 * NT)
            pe.wait_ge(uT_low, 2 * NT)
            for kk in range(KD):
                last = products(ps[4][0:E, :], [w[:, kk, :] for w in routerT], [part[:, kk, :] for part in uT], kk == 0, kk == KD - 1)
            last.then_inc(r_done, 1)
            pe.wait_ge(r_tanh, 1)
            for t in range(NT):
                last = tr(ps[5][:, t * E:(t + 1) * E], r_sig[0:E, t * P:(t + 1) * P], ident[0:E, 0:E])
            last.then_inc(r_turned, 1)

            pe.wait_ge(front_low, S0 + 2)
            def shared_up(t):
                for kk in range(KD):
                    last = products(ps[t][:, :], [part[:, kk, t * P:(t + 1) * P] for part in uT],
                                    [w[:, kk % 4, :] for w in split_block(S0 + kk // 4)], kk == 0, kk == KD - 1)
                last.then_inc(s_up, 1)

            for t in range(NT - 1):
                shared_up(t)
                if t == 1:
                    pe.wait_ge(picked_ready, 1)
                    for tt in range(NT):
                        for other in range(tt + 1):
                            last = mm(ps[4][:, 256 + tt * E:256 + (tt + 1) * E], before if other == tt else ones, picked[:, other, :],
                                      start=other == 0, stop=other == tt)
                    for other in range(NT):
                        last = mm(ps[5][:, 256:256 + E], ones, picked[:, other, :], start=other == 0, stop=other == NT - 1)
                    last.then_inc(place_done, 1)

            def shared():
                def turn_hidden(t):
                    pe.wait_ge(s_hidden, t + 1)
                    if t == 0:
                        pe.wait_ge(routed, 1)
                    elif t >= 2:
                        pe.wait_ge(s_hidT_out, t - 1)
                    for f in range(2):
                        last = tr(ps[6 - t % 2][:, f * P:(f + 1) * P], s_hid[:, t, f * P:(f + 1) * P], ident)
                    last.then_inc(s_hidT_done, 1)

                pe.wait_ge(s_down_in, 16)
                turn_hidden(0)
                pe.wait_ge(s_hidden, NT)
                for t in range(NT):
                    if t + 1 < NT:
                        turn_hidden(t + 1)
                    pe.wait_ge(s_hidT_out, t + 1)
                    if t >= 2:
                        pe.wait_ge(out_ready, t - 1)
                    for half in range(2):
                        for f in range(2):
                            last = mm(ps[(2 * t + half) % 4][:, :], s_hidT[t % 2][:, f * P:(f + 1) * P],
                                      s_down_w[:, f, half * 512:(half + 1) * 512], start=f == 0, stop=f == 1)
                        last.then_inc(s_down, 1)
                pe.wait_ge(out_ready, NT)

            def route(n, m, e):
                pe.wait_ge(sel_ready, m + 1)
                if not isinstance(m, int) or m >= 1:
                    pe.wait_ge(index_ready, m)
                for t in range(NT):
                    last = mm(ps[7][0:ROWS, 0:4], select[:, n % 2, t, :],
                              route_in[:, t, bass.ds(e, 1), :].rearrange("p a b -> p (a b)"), start=t == 0, stop=t == NT - 1)
                last.then_inc(route_done, 1)

            def transpose_tokens(n, m, turn):
                pe.wait_ge(gather_in[n % 2], turn * 16 + 16)
                for k in range(KD):
                    last = tr(ps[k // 4][:, (k % 4) * ROWS:(k % 4 + 1) * ROWS], gathered[0:ROWS, n % 2, k * P:(k + 1) * P],
                              ident[0:ROWS, 0:ROWS])
                last.then_inc(gT_done, 1)

            def up(n, m, u):
                pe.wait_ge(gT_low, m * 2 + 2)
                for j in range(2):
                    pe.wait_ge(low_done, u + (j + 1))
                    both = split[(BLOCKS * n + j) % SPLIT]
                    for kk in range(4):
                        k = 4 * j + kk
                        last = products(ps[2 + 3 * (n % 2)][0:ROWS, :], [gatheredT[:, n % 2, part, k, :] for part in range(2)],
                                        [both[:, part, kk, :] for part in range(2)], k == 0, k == KD - 1)
                    last.then_inc(block_used, 1)

            def expert(n, m, e, u, turn, last_turn=False):
                pe.wait_ge(hid_ready, m + 1)
                for f in range(2):
                    last = tr(ps[3][:, f * ROWS:(f + 1) * ROWS], hid[0:ROWS, n % 2, f * P:(f + 1) * P], ident[0:ROWS, 0:ROWS])
                last.then_inc(hidT_done, 1)
                if not last_turn or n + 3 < TURN:
                    route(n + 3, m + 3, e + 3)
                if not last_turn or n + 1 < TURN:
                    up(n + 1, m + 1, u + BLOCKS)
                if not last_turn or n + 2 < TURN:
                    transpose_tokens(n + 2, m + 2, turn + (n + 2) // 2)
                pe.wait_ge(low_done, u + 3)
                pe.wait_ge(hidT_low, m + 1)
                if not isinstance(m, int) or m >= 1:
                    pe.wait_ge(y_ready, m)
                both = split[(BLOCKS * n + 2) % SPLIT]
                for half in range(2):
                    for f in range(2):
                        last = products(ps[4 + 2 * half][0:ROWS, :], [hidT[:, n % 2, part, f * ROWS:(f + 1) * ROWS] for part in range(2)],
                                        [both[:, part, 2 * f + half, :] for part in range(2)], f == 0, f == 1)
                last.then_inc(block_used, 1)

            def expert_pass(m0, u0, pair0, between=None):
                route(0, m0, 0)
                route(1, m0 + 1, 1)
                if between:
                    shared_up(NT - 1)
                    between()
                transpose_tokens(0, m0, pair0)
                route(2, m0 + 2, 2)
                up(0, m0, u0)
                transpose_tokens(1, m0 + 1, pair0)
                for n in range(TURN):
                    expert(n, m0 + n, n, u0 + BLOCKS * n, pair0)
                with pe.Fori(1, E // TURN - 1) as g:
                    for n in range(TURN):
                        expert(n, m0 + (g * TURN + n), g * TURN + n, u0 + (g * (BLOCKS * TURN) + BLOCKS * n),
                               pair0 + g * (TURN // 2))
                last = E - TURN
                for n in range(TURN):
                    expert(n, m0 + (last + n), last + n, u0 + BLOCKS * (last + n), pair0 + last // 2, True)

            expert_pass(0, 0, 0, shared)
            fullest = pe.value_load(most_i[0:1, 0:1], min_val=0, max_val=T)
            with pe.If(fullest > ROWS):
                with pe.Fori(1, PASSES) as r:
                    with pe.If(fullest > r * ROWS):
                        expert_pass(r * E, r * (BLOCKS * E), r * (E // 2))


_INS = ['x', 'mem', 'attn_norm_g', 'w_in', 'q_norm_a', 'k_norm_a', 'rel_bias', 'lb_logits', 'out_norm_b',
        'mem_norm_g', 'w_mem_kv', 'q_norm_c', 'k_norm_c', 'w_branches', 'w_out',
        'ffn_norm_g', 'w_router', 'router_bias', 'w_exp_up', 'w_exp_down', 'w_shared_up', 'w_shared_down']


def kernel(**inputs):
    import concourse.bacc as _bacc
    from concourse.bass_utils import run_bass_kernel_spmd as _run

    nc = _bacc.Bacc("TRN2", target_bir_lowering=False, num_devices=1)
    arrays, io, const = {}, {}, {}
    inputs["w_branches"] = np.concatenate([np.asarray(inputs[f"w_branch_{n}"])[0] for n in "abc"], 0)
    for name in _INS:
        a = np.ascontiguousarray(inputs[name])
        arrays[f"in_{name}_dram"] = a
        io[name] = nc.dram_tensor(f"in_{name}_dram", a.shape, mybir.dt.from_np(a.dtype), kind="ExternalInput").ap()
    for name, a in shape_constants().items():
        arrays[f"const_{name}_dram"] = a
        const[name] = nc.dram_tensor(f"const_{name}_dram", a.shape, mybir.dt.from_np(a.dtype), kind="ExternalInput").ap()
    out = nc.dram_tensor("out_0_dram", (1, T, D), F32, kind="ExternalOutput").ap()
    u_dram = nc.dram_tensor("u_rows", (T, D), F32).ap()
    table_dram = nc.dram_tensor("distance_table", (6, SPAN), F32).ap()
    build(nc, io, out, const, u_dram, table_dram)
    r = _run(nc, [arrays], core_ids=[0])
    return r.results[0]["out_0_dram"]
```
